# Optimizing a Trainium2 kernel written in Bass

```python
import jax
import jax.numpy as jnp
from jax import lax
import numpy as np
import math

D_MODEL = 1024
BATCH = 1
SEQ = 512
DEPTH = 2

HEAD_DIM = 64
D_MIX = D_MODEL
FOX_HEADS = D_MIX // (4 * HEAD_DIM)
FOX_WIDTH = FOX_HEADS * HEAD_DIM
CONV_CH = D_MIX // 4
CONV_TAPS = 31
NSA_HEADS = D_MIX // (2 * HEAD_DIM)
NSA_WIDTH = NSA_HEADS * HEAD_DIM
NSA_KV_GROUPS = 2
NSA_HPG = NSA_HEADS // NSA_KV_GROUPS
NSA_KV_WIDTH = NSA_KV_GROUPS * HEAD_DIM
N_BRANCH = 3
CMP_LEN = 32
CMP_STRIDE = 16
CMP_HIDDEN = 256
SLC_LEN = 64
SLC_TOPK = 16
WINDOW = 512
Q_BLOCK = 128
ROPE_THETA = 500000.0
ROPE_DIM = HEAD_DIM // 4
EPS = 1e-6
NEG_INF = -1e30
FORCED_SCORE = 1e4
IN_SIZES = (FOX_WIDTH, FOX_WIDTH, FOX_WIDTH, FOX_HEADS, FOX_WIDTH,
            2 * CONV_CH, CONV_CH,
            NSA_WIDTH, NSA_KV_WIDTH, NSA_KV_WIDTH, NSA_KV_WIDTH, NSA_KV_WIDTH,
            NSA_KV_WIDTH, NSA_KV_WIDTH, NSA_HEADS * N_BRANCH, NSA_WIDTH)
D_IN = sum(IN_SIZES)


def rms_norm(x, g):
    xf = x.astype(jnp.float32)
    y = xf * lax.rsqrt(jnp.mean(xf * xf, axis=-1, keepdims=True) + EPS)
    return (y * g.astype(jnp.float32)).astype(x.dtype)

def masked_softmax(s, mask):
    s = jnp.where(mask, s.astype(jnp.float32), NEG_INF)
    return jnp.where(mask, jax.nn.softmax(s, axis=-1), 0.0)

def rope(x, pos):
    half = ROPE_DIM // 2
    inv = ROPE_THETA ** (-jnp.arange(0, ROPE_DIM, 2, dtype=jnp.float32) / ROPE_DIM)
    ang = pos.astype(jnp.float32)[:, None] * inv[None, :]
    cos = jnp.cos(ang)[None, :, None, :].astype(x.dtype)
    sin = jnp.sin(ang)[None, :, None, :].astype(x.dtype)
    x1, x2, rest = x[..., :half], x[..., half:ROPE_DIM], x[..., ROPE_DIM:]
    return jnp.concatenate([x1 * cos - x2 * sin, x1 * sin + x2 * cos, rest], axis=-1)

def fox_attention(q, k, v, f_logit):
    B, T, H, Dh = q.shape
    c = jnp.cumsum(jax.nn.log_sigmoid(f_logit.astype(jnp.float32)), axis=1)
    c = jnp.transpose(c, (0, 2, 1))
    scale = Dh ** -0.5
    kpos = jnp.arange(T)

    def block(i):
        qs = i * Q_BLOCK
        tq = qs + jnp.arange(Q_BLOCK)
        qb = lax.dynamic_slice_in_dim(q, qs, Q_BLOCK, axis=1)
        cb = lax.dynamic_slice_in_dim(c, qs, Q_BLOCK, axis=2)
        s = jnp.einsum('bqhd,bkhd->bhqk', qb, k).astype(jnp.float32) * scale
        s = s + cb[..., :, None] - c[:, :, None, :]
        p = masked_softmax(s, tq[:, None] >= kpos[None, :])
        return jnp.einsum('bhqk,bkhd->bqhd', p.astype(v.dtype), v)

    o = lax.map(block, jnp.arange(T // Q_BLOCK))
    return jnp.moveaxis(o, 0, 1).reshape(B, T, H * Dh)

def conformer_conv(u, conv_w, conv_b, ln_g, ln_b, w_pw):
    a, b = jnp.split(u, 2, axis=-1)
    y = a * jax.nn.sigmoid(b)
    C = y.shape[-1]
    y = lax.conv_general_dilated(
        y, conv_w[:, None, :].astype(y.dtype), window_strides=(1,),
        padding=[(CONV_TAPS - 1, 0)], dimension_numbers=('NWC', 'WIO', 'NWC'),
        feature_group_count=C) + conv_b
    yf = y.astype(jnp.float32)
    mu = jnp.mean(yf, axis=-1, keepdims=True)
    var = jnp.mean(jnp.square(yf - mu), axis=-1, keepdims=True)
    yn = ((yf - mu) * lax.rsqrt(var + EPS) * ln_g + ln_b).astype(y.dtype)
    return jax.nn.silu(yn) @ w_pw

def nsa_attention(q, kc, vc, ks, vs, kw, vw, gate_logit,
                  pe_k, pe_v, k_w1, k_w2, v_w1, v_w2):
    B, T, H, Dh = q.shape
    G = NSA_KV_GROUPS
    dt = q.dtype
    scale = Dh ** -0.5
    pos = jnp.arange(T)
    q = rope(q, pos)
    ks = rope(ks, pos)
    kw = rope(kw, pos)

    n_cmp = (T - CMP_LEN) // CMP_STRIDE + 1
    cmp_start = jnp.arange(n_cmp) * CMP_STRIDE
    cmp_end = cmp_start + CMP_LEN - 1
    cmp_idx = cmp_start[:, None] + jnp.arange(CMP_LEN)[None, :]

    def compress(x, pe, w1, w2):
        blk = x[:, cmp_idx] + pe[None, None, :, None, :]
        blk = jnp.transpose(blk, (0, 1, 3, 2, 4)).reshape(B, n_cmp, G, CMP_LEN * Dh)
        hid = jax.nn.gelu(jnp.einsum('bngi,ih->bngh', blk, w1))
        return jnp.einsum('bngh,ho->bngo', hid, w2)

    k_cmp = rope(compress(kc, pe_k, k_w1, k_w2), cmp_end)
    v_cmp = compress(vc, pe_v, v_w1, v_w2)

    n_slc = T // SLC_LEN
    k_sel = jnp.transpose(ks.reshape(B, n_slc, SLC_LEN, G, Dh), (0, 3, 1, 2, 4))
    v_sel = jnp.transpose(vs.reshape(B, n_slc, SLC_LEN, G, Dh), (0, 3, 1, 2, 4))
    slc_start = jnp.arange(n_slc) * SLC_LEN
    overlap = ((cmp_start[:, None] < slc_start[None, :] + SLC_LEN) &
               (cmp_end[:, None] >= slc_start[None, :])).astype(jnp.float32)
    topk = min(SLC_TOPK, n_slc)
    bi = jnp.arange(B)[:, None, None, None]
    gi = jnp.arange(G)[None, :, None, None]

    kw_p = jnp.pad(kw, ((0, 0), (WINDOW, 0), (0, 0), (0, 0)))
    vw_p = jnp.pad(vw, ((0, 0), (WINDOW, 0), (0, 0), (0, 0)))

    gates = jax.nn.sigmoid(gate_logit.astype(jnp.float32)).reshape(B, T, G, NSA_HPG, N_BRANCH)
    qg = q.reshape(B, T, G, NSA_HPG, Dh)

    def block(i):
        qs = i * Q_BLOCK
        tq = qs + jnp.arange(Q_BLOCK)
        qb = lax.dynamic_slice_in_dim(qg, qs, Q_BLOCK, axis=1)

        s = jnp.einsum('bqghd,bngd->bghqn', qb, k_cmp) * scale
        p_cmp = masked_softmax(s, cmp_end[None, :] <= tq[:, None])
        o_cmp = jnp.einsum('bghqn,bngd->bqghd', p_cmp.astype(dt), v_cmp)

        imp = jnp.einsum('bghqn,nj->bgqj', p_cmp, overlap)
        cur = tq // SLC_LEN
        j = jnp.arange(n_slc)[None, :]
        forced = (j == 0) | (j == cur[:, None]) | (j == cur[:, None] - 1)
        imp = jnp.where(forced, FORCED_SCORE,
                        jnp.where(slc_start[None, :] <= tq[:, None], imp, NEG_INF))
        _, idx = lax.top_k(imp, topk)
        k_g = k_sel[bi, gi, idx]
        v_g = v_sel[bi, gi, idx].reshape(B, G, Q_BLOCK, topk * SLC_LEN, Dh)
        s = jnp.einsum('bqghd,bgqksd->bghqks', qb, k_g) * scale
        s = s.reshape(B, G, NSA_HPG, Q_BLOCK, topk * SLC_LEN)
        key_pos = (idx[..., None] * SLC_LEN + jnp.arange(SLC_LEN)).reshape(
            B, G, 1, Q_BLOCK, topk * SLC_LEN)
        p_slc = masked_softmax(s, key_pos <= tq[:, None])
        o_slc = jnp.einsum('bghqm,bgqmd->bqghd', p_slc.astype(dt), v_g)

        kwb = lax.dynamic_slice_in_dim(kw_p, qs, WINDOW + Q_BLOCK, axis=1)
        vwb = lax.dynamic_slice_in_dim(vw_p, qs, WINDOW + Q_BLOCK, axis=1)
        sp = qs - WINDOW + jnp.arange(WINDOW + Q_BLOCK)
        wmask = ((sp[None, :] >= 0) & (sp[None, :] <= tq[:, None]) &
                 (tq[:, None] - sp[None, :] < WINDOW))
        s = jnp.einsum('bqghd,bkgd->bghqk', qb, kwb) * scale
        o_win = jnp.einsum('bghqk,bkgd->bqghd', masked_softmax(s, wmask).astype(dt), vwb)

        gb = lax.dynamic_slice_in_dim(gates, qs, Q_BLOCK, axis=1)
        o = gb[..., 0:1] * o_cmp + gb[..., 1:2] * o_slc + gb[..., 2:3] * o_win
        return o.astype(dt)

    o = lax.map(block, jnp.arange(T // Q_BLOCK))
    return jnp.moveaxis(o, 0, 1).reshape(B, T, H * Dh)

def hybrid_layer(x, norm_g, w_in, fox_b, conv_w, conv_b, conv_ln_g, conv_ln_b,
                 conv_pw, cmp_pe_k, cmp_pe_v, cmp_k_w1, cmp_k_w2, cmp_v_w1,
                 cmp_v_w2, w_out):
    B, T, _ = x.shape
    h = rms_norm(x, norm_g)
    z = h @ w_in
    split_points = np.cumsum(IN_SIZES)[:-1].tolist()
    (fq, fk, fv, ff, f_gate, glu_in, c_gate,
     nq, nkc, nvc, nks, nvs, nkw, nvw, n_gl, n_gate) = jnp.split(z, split_points, axis=-1)

    def heads(t, n):
        return t.reshape(B, T, n, HEAD_DIM)

    o_a = fox_attention(heads(fq, FOX_HEADS), heads(fk, FOX_HEADS),
                        heads(fv, FOX_HEADS), ff + fox_b) * jax.nn.silu(f_gate)
    o_b = conformer_conv(glu_in, conv_w, conv_b, conv_ln_g, conv_ln_b,
                         conv_pw) * jax.nn.silu(c_gate)
    o_c = nsa_attention(heads(nq, NSA_HEADS), heads(nkc, NSA_KV_GROUPS),
                        heads(nvc, NSA_KV_GROUPS), heads(nks, NSA_KV_GROUPS),
                        heads(nvs, NSA_KV_GROUPS), heads(nkw, NSA_KV_GROUPS),
                        heads(nvw, NSA_KV_GROUPS), n_gl, cmp_pe_k, cmp_pe_v,
                        cmp_k_w1, cmp_k_w2, cmp_v_w1, cmp_v_w2) * jax.nn.silu(n_gate)
    mixed = jnp.concatenate([o_a, o_b, o_c], axis=-1)
    return x + mixed @ w_out

def first_inputs(seed: int = 0) -> dict:
    key = jax.random.key(seed)
    k = jax.random.split(key, 18)
    L = DEPTH

    def nrm(kk, shape, scale):
        return scale * jax.random.normal(kk, shape, jnp.float32)

    return {
        'x': nrm(k[0], (BATCH, SEQ, D_MODEL), 1.0),
        'norm_g': 1.0 + nrm(k[1], (L, D_MODEL), 0.02),
        'w_in': nrm(k[2], (L, D_MODEL, D_IN), D_MODEL ** -0.5),
        'fox_b': 3.0 + nrm(k[3], (L, FOX_HEADS), 0.5),
        'conv_w': nrm(k[4], (L, CONV_TAPS, CONV_CH), CONV_TAPS ** -0.5),
        'conv_b': nrm(k[5], (L, CONV_CH), 0.02),
        'conv_ln_g': 1.0 + nrm(k[6], (L, CONV_CH), 0.02),
        'conv_ln_b': nrm(k[7], (L, CONV_CH), 0.02),
        'conv_pw': nrm(k[8], (L, CONV_CH, CONV_CH), CONV_CH ** -0.5),
        'cmp_pe_k': nrm(k[9], (L, CMP_LEN, HEAD_DIM), 0.1),
        'cmp_pe_v': nrm(k[10], (L, CMP_LEN, HEAD_DIM), 0.1),
        'cmp_k_w1': nrm(k[11], (L, CMP_LEN * HEAD_DIM, CMP_HIDDEN), (CMP_LEN * HEAD_DIM) ** -0.5),
        'cmp_k_w2': nrm(k[12], (L, CMP_HIDDEN, HEAD_DIM), CMP_HIDDEN ** -0.5),
        'cmp_v_w1': nrm(k[13], (L, CMP_LEN * HEAD_DIM, CMP_HIDDEN), (CMP_LEN * HEAD_DIM) ** -0.5),
        'cmp_v_w2': nrm(k[14], (L, CMP_HIDDEN, HEAD_DIM), CMP_HIDDEN ** -0.5),
        'w_out': nrm(k[15], (L, D_MIX, D_MODEL), D_MIX ** -0.5),
        'final_g': 1.0 + nrm(k[16], (D_MODEL,), 0.02),
    }

def first_block(x, norm_g, w_in, fox_b, conv_w, conv_b, conv_ln_g, conv_ln_b,
              conv_pw, cmp_pe_k, cmp_pe_v, cmp_k_w1, cmp_k_w2, cmp_v_w1,
              cmp_v_w2, w_out, final_g):
    for l in range(DEPTH):
        x = hybrid_layer(x, norm_g[l], w_in[l], fox_b[l], conv_w[l], conv_b[l],
                         conv_ln_g[l], conv_ln_b[l], conv_pw[l], cmp_pe_k[l],
                         cmp_pe_v[l], cmp_k_w1[l], cmp_k_w2[l], cmp_v_w1[l],
                         cmp_v_w2[l], w_out[l])
    return rms_norm(x, final_g)


HA = 4
DKA = 128
DVA = 128
CONV_K = 5
CHUNK_A = 64
HB = 4
DHB = 64
QBLK = 128
HC = 8
KVC = 2
GC = HC // KVC
DHC = 64
WINDOW_2 = 128
HD = 4
DKD = 64
DVD = 128
CHUNK_D = 64
N_BRANCH_2 = 4
BRANCH_W = 512
D_FF = 4 * D_MODEL
ROPE_THETA_2 = 10000.0
ROPE_DIM_2 = 64

A_QKV_W = HA * (2 * DKA + DVA)
SPLIT_SIZES = (
    A_QKV_W, HA * DVA, 4 * HA,
    HB * 2 * DHB, HB * 2 * DHB, HB * 2 * DHB,
    HC * DHC, KVC * DHC, KVC * DHC,
    HD * DKD, HD * DKD, HD * DVD, 4 * HD, HD * DVD,
)
IN_W = sum(SPLIT_SIZES)


F32 = jnp.float32

def rmsnorm(x, g):
    xf = x.astype(F32)
    y = xf * lax.rsqrt(jnp.mean(xf * xf, axis=-1, keepdims=True) + EPS)
    return (y * g.astype(F32)).astype(x.dtype)

def l2norm(x):
    xf = x.astype(F32)
    return xf * lax.rsqrt(jnp.sum(xf * xf, axis=-1, keepdims=True) + EPS)

def rope_tables(S, dim):
    inv = 1.0 / (ROPE_THETA_2 ** (jnp.arange(0, dim, 2, dtype=F32) / dim))
    ang = jnp.arange(S, dtype=F32)[:, None] * inv[None, :]
    ang = jnp.concatenate([ang, ang], axis=-1)
    return jnp.cos(ang), jnp.sin(ang)

def apply_rope(x, cos, sin):
    x1, x2 = jnp.split(x, 2, axis=-1)
    rot = jnp.concatenate([-x2, x1], axis=-1)
    return (x * cos[None, :, None, :] + rot * sin[None, :, None, :]).astype(x.dtype)

def centred_dwconv(x, w):
    K, C = w.shape
    return lax.conv_general_dilated(
        x, w.reshape(K, 1, C).astype(x.dtype), window_strides=(1,),
        padding=[(K // 2, K // 2)], dimension_numbers=('NWC', 'WIO', 'NWC'),
        feature_group_count=C)

def gated_delta_chunked(q, k, v, g, beta):
    B, H, S, Dk = k.shape
    Dv = v.shape[-1]
    L = CHUNK_A
    N = S // L
    q = q.reshape(B, H, N, L, Dk)
    k = k.reshape(B, H, N, L, Dk)
    v = v.reshape(B, H, N, L, Dv)
    beta = beta.reshape(B, H, N, L)
    gc = jnp.cumsum(g.reshape(B, H, N, L), axis=-1)
    tri = jnp.tril(jnp.ones((L, L), dtype=bool))
    tri_strict = jnp.tril(jnp.ones((L, L), dtype=bool), -1)
    decay = jnp.where(tri, jnp.exp(jnp.where(tri, gc[..., :, None] - gc[..., None, :], 0.0)), 0.0)
    k_beta = k * beta[..., None]
    v_beta = v * beta[..., None]
    a_strict = jnp.where(tri_strict, jnp.einsum('bhnid,bhnjd->bhnij', k_beta, k) * decay, 0.0)
    t_mat = a_strict + jnp.eye(L, dtype=F32)
    u = lax.linalg.triangular_solve(t_mat, v_beta, left_side=True, lower=True, unit_diagonal=True)
    w = lax.linalg.triangular_solve(t_mat, k_beta * jnp.exp(gc)[..., None], left_side=True,
                                    lower=True, unit_diagonal=True)
    qk_intra = jnp.where(tri, jnp.einsum('bhnid,bhnjd->bhnij', q, k) * decay, 0.0)

    def step(state, inp):
        q_c, k_c, u_c, w_c, g_c, a_c = inp
        v_new = u_c - jnp.einsum('bhld,bhde->bhle', w_c, state)
        o = (jnp.einsum('bhld,bhde->bhle', q_c * jnp.exp(g_c)[..., None], state)
             + jnp.einsum('bhij,bhje->bhie', a_c, v_new))
        g_last = g_c[..., -1]
        k_dec = k_c * jnp.exp(g_last[..., None] - g_c)[..., None]
        state = state * jnp.exp(g_last)[..., None, None] + jnp.einsum('bhld,bhle->bhde', k_dec, v_new)
        return state, o

    xs = tuple(jnp.moveaxis(t, 2, 0) for t in (q, k, u, w, gc, qk_intra))
    _, o = lax.scan(step, jnp.zeros((B, H, Dk, Dv), F32), xs)
    return jnp.moveaxis(o, 0, 2).reshape(B, H, S, Dv)

def gdn_mixer(qkv, z, ab, conv_w, a_log, dt_bias, norm_g):
    B, S, _ = qkv.shape
    qkv = jax.nn.silu(centred_dwconv(qkv, conv_w)).astype(F32)
    q, k, v = jnp.split(qkv, [HA * DKA, 2 * HA * DKA], axis=-1)
    q = l2norm(q.reshape(B, S, HA, DKA)) * (DKA ** -0.5)
    k = l2norm(k.reshape(B, S, HA, DKA))
    v = v.reshape(B, S, HA, DVA)
    ab = ab.astype(F32).reshape(B, S, 2, 2, HA)
    g = -jnp.exp(a_log.astype(F32)) * jax.nn.softplus(ab[:, :, 0] + dt_bias.astype(F32))
    beta = jax.nn.sigmoid(ab[:, :, 1])
    qh, kh, vh = (jnp.moveaxis(t, 1, 2) for t in (q, k, v))
    gh = jnp.transpose(g, (0, 2, 3, 1))
    bh = jnp.transpose(beta, (0, 2, 3, 1))
    flip = lambda t: jnp.flip(t, axis=2)
    o_f = gated_delta_chunked(qh, kh, vh, gh[:, 0], bh[:, 0])
    o_b = flip(gated_delta_chunked(flip(qh), flip(kh), flip(vh), flip(gh[:, 1]), flip(bh[:, 1])))
    o = jnp.moveaxis(o_f + o_b, 1, 2)
    o = rmsnorm(o, norm_g) * jax.nn.silu(z.astype(F32).reshape(B, S, HA, DVA))
    return o.reshape(B, S, HA * DVA)

def diff_mixer(q, k, v, lam_params, norm_g, lam_init, cos, sin):
    B, S, _ = q.shape
    q = apply_rope(q.reshape(B, S, HB * 2, DHB), cos, sin).reshape(B, S, HB, 2, DHB)
    k = apply_rope(k.reshape(B, S, HB * 2, DHB), cos, sin).reshape(B, S, HB, 2, DHB)
    v = v.reshape(B, S, HB, 2 * DHB)
    lp = lam_params.astype(F32)
    lam = jnp.exp(jnp.sum(lp[0] * lp[1])) - jnp.exp(jnp.sum(lp[2] * lp[3])) + lam_init
    scale = DHB ** -0.5
    nq = S // QBLK
    qb = jnp.moveaxis(q.reshape(B, nq, QBLK, HB, 2, DHB), 1, 0)

    def one_block(q_blk):
        s = jnp.einsum('bqhmd,bkhmd->bhmqk', q_blk, k).astype(F32) * scale
        p = jax.nn.softmax(s, axis=-1)
        a = p[:, :, 0] - lam * p[:, :, 1]
        return jnp.einsum('bhqk,bkhe->bqhe', a.astype(v.dtype), v)

    o = lax.map(one_block, qb)
    o = jnp.moveaxis(o, 0, 1).reshape(B, S, HB, 2 * DHB)
    o = rmsnorm(o, norm_g) * (1.0 - lam_init)
    return o.reshape(B, S, HB * 2 * DHB)

def swa_mixer(q, k, v, sink, cos, sin):
    B, S, _ = q.shape
    nb = S // WINDOW_2
    q = apply_rope(q.reshape(B, S, HC, DHC), cos, sin)
    k = apply_rope(k.reshape(B, S, KVC, DHC), cos, sin)
    v = v.reshape(B, S, KVC, DHC)

    def band(t):
        tp = jnp.pad(t, ((0, 0), (WINDOW_2, WINDOW_2), (0, 0), (0, 0))).reshape(B, nb + 2, WINDOW_2, KVC, DHC)
        return jnp.concatenate([tp[:, :-2], tp[:, 1:-1], tp[:, 2:]], axis=2)

    kw, vw = band(k), band(v)
    qb = q.reshape(B, nb, WINDOW_2, KVC, GC, DHC)
    s = jnp.einsum('bnqcgd,bnkcd->bncgqk', qb, kw).astype(F32) * (DHC ** -0.5)
    rel = jnp.arange(3 * WINDOW_2)[None, :] - WINDOW_2 - jnp.arange(WINDOW_2)[:, None]
    kpos = jnp.arange(nb)[:, None] * WINDOW_2 - WINDOW_2 + jnp.arange(3 * WINDOW_2)[None, :]
    valid = (jnp.abs(rel) <= WINDOW_2)[None] & ((kpos >= 0) & (kpos < S))[:, None, :]
    s = jnp.where(valid[None, :, None, None], s, -jnp.inf)
    sk = sink.astype(F32).reshape(1, 1, KVC, GC, 1, 1)
    m = jnp.maximum(jnp.max(s, axis=-1, keepdims=True), sk)
    p = jnp.exp(s - m)
    denom = jnp.sum(p, axis=-1, keepdims=True) + jnp.exp(sk - m)
    o = jnp.einsum('bncgqk,bnkcd->bnqcgd', (p / denom).astype(v.dtype), vw)
    return o.reshape(B, S, HC * DHC)

def mlstm_chunked(q, k, v, log_i, log_f):
    B, H, S, Dk = q.shape
    Dv = v.shape[-1]
    L = CHUNK_D
    N = S // L
    q = q.reshape(B, H, N, L, Dk)
    k = k.reshape(B, H, N, L, Dk)
    v = v.reshape(B, H, N, L, Dv)
    log_i = log_i.reshape(B, H, N, L)
    b = jnp.cumsum(log_f.reshape(B, H, N, L), axis=-1)
    tri = jnp.tril(jnp.ones((L, L), dtype=bool))
    d_log = jnp.where(tri, b[..., :, None] - b[..., None, :] + log_i[..., None, :], -jnp.inf)
    qk = jnp.einsum('bhnid,bhnjd->bhnij', q, k)
    e_log = b[..., -1:] - b + log_i

    def step(carry, inp):
        c, n, m = carry
        q_c, k_c, v_c, b_c, d_c, qk_c, e_c = inp
        inter = b_c + m[..., None]
        m_t = jnp.maximum(inter, jnp.max(d_c, axis=-1))
        w_inter = jnp.exp(inter - m_t)
        w_intra = jnp.exp(d_c - m_t[..., None]) * qk_c
        num = (w_inter[..., None] * jnp.einsum('bhld,bhde->bhle', q_c, c)
               + jnp.einsum('bhij,bhje->bhie', w_intra, v_c))
        den = w_inter * jnp.einsum('bhld,bhd->bhl', q_c, n) + jnp.sum(w_intra, axis=-1)
        h = num / jnp.maximum(jnp.abs(den), jnp.exp(-m_t))[..., None]
        inter_end = b_c[..., -1] + m
        m_new = jnp.maximum(inter_end, jnp.max(e_c, axis=-1))
        k_w = jnp.exp(e_c - m_new[..., None])[..., None] * k_c
        sc = jnp.exp(inter_end - m_new)
        c = sc[..., None, None] * c + jnp.einsum('bhld,bhle->bhde', k_w, v_c)
        n = sc[..., None] * n + jnp.sum(k_w, axis=-2)
        return (c, n, m_new), h

    init = (jnp.zeros((B, H, Dk, Dv), F32), jnp.zeros((B, H, Dk), F32), jnp.zeros((B, H), F32))
    xs = tuple(jnp.moveaxis(t, 2, 0) for t in (q, k, v, b, d_log, qk, e_log))
    _, h = lax.scan(step, init, xs)
    return jnp.moveaxis(h, 0, 2).reshape(B, H, S, Dv)

def mlstm_mixer(q, k, v, gif, o, gate_b, norm_g):
    B, S, _ = q.shape
    q = q.astype(F32).reshape(B, S, HD, DKD)
    k = k.astype(F32).reshape(B, S, HD, DKD) * (DKD ** -0.5)
    v = v.astype(F32).reshape(B, S, HD, DVD)
    pre = gif.astype(F32).reshape(B, S, 2, 2, HD) + gate_b.astype(F32)
    log_i = jnp.transpose(pre[:, :, 0], (0, 2, 3, 1))
    log_f = jnp.transpose(jax.nn.log_sigmoid(pre[:, :, 1]), (0, 2, 3, 1))
    qh, kh, vh = (jnp.moveaxis(t, 1, 2) for t in (q, k, v))
    flip = lambda t: jnp.flip(t, axis=2)
    h_f = mlstm_chunked(qh, kh, vh, log_i[:, 0], log_f[:, 0])
    h_b = flip(mlstm_chunked(flip(qh), flip(kh), flip(vh), flip(log_i[:, 1]), flip(log_f[:, 1])))
    h = jnp.moveaxis(h_f + h_b, 1, 2)
    h = rmsnorm(h, norm_g) * jax.nn.sigmoid(o.astype(F32).reshape(B, S, HD, DVD))
    return h.reshape(B, S, HD * DVD)

def second_inputs(seed: int = 0) -> dict:
    key = jax.random.key(seed)
    ks = jax.random.split(key, 20)
    L, D = DEPTH, D_MODEL
    nrm = lambda kk, shape, sc: jax.random.normal(kk, shape, F32) * sc
    gate_base = jnp.concatenate([jnp.zeros((1, 1, 2, HD), F32), jnp.full((1, 1, 2, HD), 3.0, F32)], axis=1)
    return {
        'x': nrm(ks[0], (BATCH, SEQ, D), 1.0),
        'norm1_g': 1.0 + nrm(ks[1], (L, D), 0.02),
        'w_in': nrm(ks[2], (L, D, IN_W), D ** -0.5),
        'gdn_conv_w': nrm(ks[3], (L, CONV_K, A_QKV_W), CONV_K ** -0.5),
        'gdn_a_log': jnp.log(jax.random.uniform(ks[4], (L, 2, HA), F32, 1.0, 16.0)),
        'gdn_dt_bias': nrm(ks[5], (L, 2, HA), 0.1),
        'gdn_norm_g': 1.0 + nrm(ks[6], (L, DVA), 0.02),
        'diff_lambda': nrm(ks[7], (L, 4, DHB), 0.1),
        'diff_norm_g': 1.0 + nrm(ks[8], (L, 2 * DHB), 0.02),
        'swa_sink': nrm(ks[9], (L, HC), 0.1),
        'mlstm_gate_b': gate_base + nrm(ks[10], (L, 2, 2, HD), 0.1),
        'mlstm_norm_g': 1.0 + nrm(ks[11], (L, DVD), 0.02),
        'w_branch': nrm(ks[12], (L, N_BRANCH_2, BRANCH_W, D), BRANCH_W ** -0.5),
        'w_gate': nrm(ks[13], (L, D, N_BRANCH_2, D), D ** -0.5),
        'w_out': nrm(ks[14], (L, D, D), D ** -0.5),
        'norm2_g': 1.0 + nrm(ks[15], (L, D), 0.02),
        'w_mlp1': nrm(ks[16], (L, D, D_FF), D ** -0.5),
        'w_mlp2': nrm(ks[17], (L, D_FF, D), D_FF ** -0.5),
        'final_norm_g': 1.0 + nrm(ks[18], (D,), 0.02),
    }

def second_block(x, norm1_g, w_in, gdn_conv_w, gdn_a_log, gdn_dt_bias, gdn_norm_g, diff_lambda,
              diff_norm_g, swa_sink, mlstm_gate_b, mlstm_norm_g, w_branch, w_gate, w_out,
              norm2_g, w_mlp1, w_mlp2, final_norm_g):
    S = x.shape[1]
    cos, sin = rope_tables(S, ROPE_DIM_2)
    offsets = np.cumsum(SPLIT_SIZES)[:-1].tolist()
    for l in range(DEPTH):
        xn = rmsnorm(x, norm1_g[l])
        h = xn @ w_in[l]
        (a_qkv, a_z, a_ab, b_q, b_k, b_v, c_q, c_k, c_v,
         d_q, d_k, d_v, d_if, d_o) = jnp.split(h, offsets, axis=-1)
        lam_init = 0.8 - 0.6 * math.exp(-0.3 * l)
        y_a = gdn_mixer(a_qkv, a_z, a_ab, gdn_conv_w[l], gdn_a_log[l], gdn_dt_bias[l], gdn_norm_g[l])
        y_b = diff_mixer(b_q, b_k, b_v, diff_lambda[l], diff_norm_g[l], lam_init, cos, sin)
        y_c = swa_mixer(c_q, c_k, c_v, swa_sink[l], cos, sin)
        y_d = mlstm_mixer(d_q, d_k, d_v, d_if, d_o, mlstm_gate_b[l], mlstm_norm_g[l])
        ys = jnp.stack([y_a.astype(x.dtype), y_b.astype(x.dtype), y_c.astype(x.dtype),
                        y_d.astype(x.dtype)], axis=2)
        branch = jnp.einsum('bsnw,nwd->bsnd', ys, w_branch[l])
        gate = jax.nn.sigmoid(jnp.einsum('bsd,dne->bsne', xn, w_gate[l]))
        x = x + jnp.sum(gate * branch, axis=2) @ w_out[l]
        xn = rmsnorm(x, norm2_g[l])
        x = x + jnp.square(jax.nn.relu(xn @ w_mlp1[l])) @ w_mlp2[l]
    return rmsnorm(x, final_norm_g)


_first_inputs = second_inputs


def second_inputs(seed=0):
    import zlib

    import numpy as np

    out = dict(_first_inputs(seed))
    spreads = {}
    factors = {'gdn_dt_bias': 7.624,
     'gdn_norm_g': 21.832,
     'diff_norm_g': 15.117,
     'swa_sink': 64.0,
     'mlstm_norm_g': 21.91,
     'final_norm_g': 8.419,
     'norm2_g': 4.755}
    for name, (base, spread) in spreads.items():
        noise = np.random.default_rng([zlib.crc32(name.encode()), seed]).standard_normal(out[name].shape)
        drawn = base * np.exp(spread * noise) if base else spread * noise
        out[name] = jnp.asarray(drawn.astype(out[name].dtype))
    for name, factor in factors.items():
        out[name] = (out[name] * factor).astype(out[name].dtype)
    return out


_narrow_inputs = second_inputs


def second_inputs(seed=0):
    out = dict(_narrow_inputs(seed))
    wider = {'gdn_norm_g': 3.58,
     'diff_norm_g': 3.83,
     'swa_sink': 12.0,
     'mlstm_norm_g': 3.6,
     'final_norm_g': 3.27}
    for name, times in wider.items():
        mean = out[name].mean()
        out[name] = (mean + times * (out[name] - mean)).astype(out[name].dtype)
    return out


def setup_inputs(seed=0):
    out = dict(first_inputs(seed))
    for name, value in second_inputs(seed + 1).items():
        if name != "x":
            out[name + "_2"] = value
    return out


def reference(
    x, norm_g, w_in, fox_b, conv_w, conv_b, conv_ln_g, conv_ln_b, conv_pw, cmp_pe_k, cmp_pe_v,
    cmp_k_w1, cmp_k_w2, cmp_v_w1, cmp_v_w2, w_out, final_g, norm1_g_2, w_in_2, gdn_conv_w_2,
    gdn_a_log_2, gdn_dt_bias_2, gdn_norm_g_2, diff_lambda_2, diff_norm_g_2, swa_sink_2,
    mlstm_gate_b_2, mlstm_norm_g_2, w_branch_2, w_gate_2, w_out_2, norm2_g_2, w_mlp1_2,
    w_mlp2_2, final_norm_g_2,
):
    x = first_block(
        x, norm_g, w_in, fox_b, conv_w, conv_b, conv_ln_g, conv_ln_b, conv_pw, cmp_pe_k,
        cmp_pe_v, cmp_k_w1, cmp_k_w2, cmp_v_w1, cmp_v_w2, w_out, final_g,
    )
    return second_block(
        x, norm1_g_2, w_in_2, gdn_conv_w_2, gdn_a_log_2, gdn_dt_bias_2, gdn_norm_g_2,
        diff_lambda_2, diff_norm_g_2, swa_sink_2, mlstm_gate_b_2, mlstm_norm_g_2, w_branch_2,
        w_gate_2, w_out_2, norm2_g_2, w_mlp1_2, w_mlp2_2, final_norm_g_2,
    )


_drawn_inputs = setup_inputs


def setup_inputs(seed=0):
    import zlib

    import numpy as np

    out = dict(_drawn_inputs(seed))
    spreads = {}
    factors = {'conv_ln_b': 2.708, 'cmp_pe_k': 7.19, 'diff_lambda_2': 3.918, 'swa_sink_2': 8.0}
    for name, (base, spread) in spreads.items():
        noise = np.random.default_rng([zlib.crc32(name.encode()), seed]).standard_normal(out[name].shape)
        drawn = base * np.exp(spread * noise) if base else spread * noise
        out[name] = jnp.asarray(drawn.astype(out[name].dtype))
    for name, factor in factors.items():
        out[name] = (out[name] * factor).astype(out[name].dtype)
    return out
```

```python
import numpy as np
from contextlib import ExitStack

import concourse.bass as bass
from concourse import mybir

F32 = mybir.dt.float32
ACT = mybir.ActivationFunctionType
ALU = mybir.AluOpType
AX = mybir.AxisListType
ET = mybir.EngineType

P = 128
T = 512
NT = T // P
D = 1024
KD = D // P
DEPTH = 2
EPS = 1e-6
NEG = -1e30
HD = 64

FOX_W, CONV_CH, TAPS, CMP_LEN, CMP_STRIDE = 256, 256, 31, 32, 16
N_CMP = (T - CMP_LEN) // CMP_STRIDE + 1
C1 = {}
_at = 0
for _name, _size in (("fq", 256), ("fk", 256), ("fv", 256), ("ff", 4), ("fg", 256), ("glu", 512), ("cg", 256),
                     ("nq", 512), ("nkc", 128), ("nvc", 128), ("nks", 128), ("nvs", 128), ("nkw", 128),
                     ("nvw", 128), ("ngl", 24), ("ng", 512)):
    C1[_name] = _at
    _at += _size
C2 = {}
_at = 0
for _name, _size in (("a_qkv", 1536), ("a_z", 512), ("a_ab", 16), ("b_q", 512), ("b_k", 512), ("b_v", 512),
                     ("c_q", 512), ("c_k", 128), ("c_v", 128), ("d_q", 256), ("d_k", 256), ("d_v", 512),
                     ("d_if", 16), ("d_o", 512)):
    C2[_name] = _at
    _at += _size

LEVELS = 7


def constants():
    f = np.float32
    i = np.arange(P)[:, None]
    j = np.arange(P)[None, :]
    out = {}
    out["ident"] = (i == j)
    out["nident"] = -(i == j).astype(f)
    out["later"] = np.where(j > i, NEG, 0.0)
    out["far"] = np.where(j < i, NEG, 0.0)
    out["up"] = (j >= i)
    out["low"] = (j <= i)
    out["sup"] = (j > i)
    out["slow"] = (j < i)
    out["ones"] = np.ones((P, P))
    low = [((i // (2 << s)) == (j // (2 << s))) & (i % (2 << s) >= (1 << s)) & (j % (2 << s) < (1 << s))
           for s in range(LEVELS)]
    out["levlow"] = np.concatenate(low, 1)
    out["levup"] = np.concatenate([m.T for m in low], 1)

    def rope(theta, dim, pos):
        half = dim // 2
        inv = (f(theta) ** (-np.arange(0, dim, 2, dtype=f) / f(dim))).astype(f)
        ang = pos.astype(f)[:, None] * inv[None, :]
        cos = np.ones((P, len(pos)), f)
        sin = np.zeros((P, len(pos)), f)
        rot = np.zeros((P, P), f)
        for p in range(P):
            d = p % HD
            if d < dim:
                cos[p], sin[p] = np.cos(ang[:, d % half]), np.sin(ang[:, d % half])
                if d < half:
                    rot[p + half, p] = -1.0
                else:
                    rot[p - half, p] = 1.0
        return cos, sin, rot

    ends = np.arange(N_CMP) * CMP_STRIDE + CMP_LEN - 1
    out["cos1"], out["sin1"], out["rot1"] = rope(500000.0, 16, np.arange(T))
    out["cosc"], out["sinc"], _ = rope(500000.0, 16, ends)
    out["cos2"], out["sin2"], out["rot2"] = rope(10000.0, 64, np.arange(T))
    tq = np.arange(NT)[None, :, None] * P + np.arange(P)[:, None, None]
    seen = ends[None, None, :] <= tq
    out["cmpneg"] = np.where(seen, 0.0, NEG).reshape(P, -1)
    out["cmpone"] = seen.reshape(P, -1)
    for h in range(4):
        out[f"row{h}"] = np.repeat((np.arange(P) == h)[:, None], P, 1)
    t = np.arange(T)[None, :]
    out["carryf"] = np.repeat(t % P != 0, P, 0)
    out["carryb"] = np.repeat(t % P != P - 1, P, 0)
    out["onesrow"] = np.ones((P, T))
    lam = 0.8 - 0.6 * np.exp(-0.3 * np.arange(DEPTH))
    out["lam"] = np.repeat(np.concatenate([lam, 1 - lam])[None, :], P, 0)
    cols, at, parts = {}, 0, []
    for name, a in out.items():
        a = np.ascontiguousarray(a, f)
        cols[name] = (at, at + a.shape[1])
        at += a.shape[1]
        parts.append(a)
    return cols, np.concatenate(parts, 1)


class Queue:

    def __init__(self, eng, sem):
        self.eng, self.sem = eng, sem
        self.fresh()

    def fresh(self):
        self.n, self.seen = 0, {}

    def wait(self, *marks):
        for m in marks:
            if m is None:
                continue
            if isinstance(m, list):
                self.wait(*m)
            elif self.seen.get(m[0], 0) < m[1]:
                self.eng.wait_ge(m[0], m[1])
                self.seen[m[0]] = m[1]

    def __call__(self, instr, *args, after=(), **kw):
        self.wait(*after)
        instr(*args, **kw).then_inc(self.sem, 1)
        self.n += 1
        return (self.sem, self.n)

    def mark(self):
        return (self.sem, self.n)


class Core:

    N_DMA = 24

    def __init__(self, nc):
        self.nc = nc
        names = ["pe", "dve", "act", "pool"] + [f"dma{i}" for i in range(self.N_DMA)]
        self.sems = [nc.alloc_semaphore(n) for n in names]
        self.pe = Queue(nc.tensor, self.sems[0])
        self.dve = Queue(nc.vector, self.sems[1])
        self.act = Queue(nc.scalar, self.sems[2])
        self.pool = Queue(nc.gpsimd, self.sems[3])
        self.sp = Queue(nc.sync, None)
        self.used = 0
        self.ld, self.mm, self.mid, self.ev = [[nc.alloc_semaphore(f"{n}{i}") for i in range(4)]
                                               for n in ("ld", "mm", "mid", "ev")]
        self.own = nc.alloc_semaphore("own")
        self.zeroed = range(self.sems[0].num, self.own.num + 1)
        self.barrier()

    def barrier(self):
        for i in range(self.used):
            self.sp.wait((self.sems[4 + i], self.total[i]))
        self.nc.multi_engine_barrier([ET.SP, ET.PE, ET.DVE, ET.Activation, ET.Pool], sems_to_clear=self.zeroed)
        for q in (self.pe, self.dve, self.act, self.pool, self.sp):
            q.fresh()
        self.used, self.total = 0, []

    def dma(self, *pairs, after=(), slow=False, on=None):
        q = on or self.sp
        q.wait(*after)
        sem = self.sems[4 + self.used]
        for out, in_ in pairs:
            q.eng.dma_start(out, in_, allow_slow_non_contiguous=slow).then_inc(sem, 16)
        self.used += 1
        self.total.append(16 * len(pairs))
        return (sem, 16 * len(pairs))

    def products(self, out, terms, after=()):
        self.pe.wait(*after)
        for n, (l, r) in enumerate(terms):
            m = self.nc.tensor.matmul(out, l, r, start=n == 0, stop=n == len(terms) - 1)
        m.then_inc(self.pe.sem, 1)
        self.pe.n += 1
        return self.pe.mark()

    def transposes(self, pairs, ident, after=()):
        self.pe.wait(*after)
        for out, in_ in pairs:
            m = self.nc.tensor.transpose(out, in_, ident[0:in_.shape[0], 0:in_.shape[0]])
        m.then_inc(self.pe.sem, 1)
        self.pe.n += 1
        return self.pe.mark()


def cols_of(w, l, c, n):
    return w[l, :, bass.ds(c, n)].rearrange("(k p) n -> p k n", p=P)


class Program:
    def __init__(self, nc, A, out, C, cols):
        self.nc, self.A, self.out, self.cols = nc, A, out, cols
        self.stage = 0
        self.c = Core(nc)
        sb = nc.alloc_sbuf_tensor
        self.const = sb("const", [P, C.shape[1]], F32)
        self.xT = sb("xT", [P, KD, T], F32)
        self.hT = sb("hT", [P, KD, T], F32)
        self.yT = sb("yT", [P, 16, T], F32)
        self.rstd = sb("rstd", [P, T], F32)
        self.bank = [nc.alloc_psum_tensor(f"bank{i}", [P, T], F32) for i in range(8)]
        self.const_dram = C

    def allocator(self, stack):
        self.stage += 1
        n = self.stage
        return lambda name, shape: stack.enter_context(self.nc.sbuf_tensor(f"{name}_{n}", shape, F32))

    def k(self, name, rows=P):
        a, b = self.cols[name]
        return self.const[0:rows, a:b]

    def proj_T(self, out, w, h, after=()):
        return self.c.products(out, [(w[:, k, :], h[:, k, :]) for k in range(KD)], after)

    def proj_tok(self, outs, w, h, after=(), tiles=NT):
        for i, o in enumerate(outs):
            m = self.c.products(o, [(h[:, k, i * P:(i + 1) * P], w[:, k, :]) for k in range(KD)],
                                after if i == 0 else ())
        return m

    def norm(self, dst, g_dram):
        nc, c = self.nc, self.c
        with ExitStack() as es:
            sq = self.allocator(es)("sq", [P, KD, T])
            g = self.allocator(es)("norm_gain", [P, KD])
            eps = self.allocator(es)("norm_eps", [P, 1])
            lg = c.dma((g[:, :], g_dram.rearrange("(k p) -> p k", p=P)), slow=True)
            me = c.dve(nc.vector.memset, eps[:, :], EPS)
            terms = []
            for k in range(KD):
                m = c.act(nc.scalar.activation, sq[:, k, :], self.xT[:, k, :], ACT.Square)
                terms.append((self.k("ones"), sq[:, k, :]))
            m = c.products(self.bank[0][:, :], terms, after=[m])
            m = c.act(nc.scalar.activation, self.rstd[:, :], self.bank[0][:, :], ACT.Ln,
                      bias=eps[:, 0:1], scale=1.0 / D, after=[m, me])
            m = c.act(nc.scalar.activation, self.rstd[:, :], self.rstd[:, :], ACT.Exp, scale=-0.5, after=[m])
            for k in range(KD):
                c.dve(nc.vector.scalar_tensor_tensor, dst[:, k, :], self.xT[:, k, :], g[:, k:k + 1],
                      self.rstd[:, :], ALU.mult, ALU.mult, after=[m, lg])
            c.barrier()

    def to_rows(self, dst, src, bank, after):
        n = dst.shape[0]
        m = self.c.transposes([(bank[0:n, t * P:(t + 1) * P], src[:, t, :]) for t in range(NT)],
                              self.k("ident"), after)
        return self.c.dve(self.nc.vector.tensor_copy, dst, bank[0:n, 0:T], after=[m])

    def spread(self, bank, h, rows, after=()):
        return self.c.products(bank[:, :], [(self.k(f"row{h}", 4), rows)], after)

    def log_sigmoid(self, x, tmp, after, negate=False):
        nc, c = self.nc, self.c
        m = c.act(nc.scalar.activation, tmp, x, ACT.Abs, after=after)
        m = c.act(nc.scalar.activation, tmp, tmp, ACT.Exp, scale=-1.0, after=[m])
        m = c.act(nc.scalar.activation, tmp, tmp, ACT.Ln, bias=1.0, after=[m])
        return c.dve(nc.vector.scalar_tensor_tensor, x, x, 0.0, tmp, ALU.min, ALU.subtract, after=[m])

    def silu(self, out, x, tmp, after, half=0.5):
        nc, c = self.nc, self.c
        m = c.act(nc.scalar.activation, tmp, x, ACT.Tanh, scale=0.5, after=after)
        m = c.dve(nc.vector.scalar_tensor_tensor, out, tmp, 1.0, x, ALU.add, ALU.mult, after=[m])
        return c.dve(nc.vector.tensor_scalar, out, out, half, None, ALU.mult, after=[m])

    def sigmoid(self, out, x, after):
        nc, c = self.nc, self.c
        m = c.act(nc.scalar.activation, out, x, ACT.Tanh, scale=0.5, after=after)
        return c.dve(nc.vector.tensor_scalar, out, out, 0.5, 0.5, ALU.mult, ALU.add, after=[m])

    def rope(self, x, tmp, bank, rot, cos, sin, after):
        nc, c = self.nc, self.c
        n = x.shape[-1]
        mr = c.products(bank[:, 0:n], [(rot, x)], after)
        ms = c.dve(nc.vector.tensor_tensor, tmp, bank[:, 0:n], sin, ALU.mult, after=[mr])
        mc = c.dve(nc.vector.tensor_tensor, x, x, cos, ALU.mult, after=[mr])
        return c.dve(nc.vector.tensor_tensor, x, x, tmp, ALU.add, after=[ms, mc])

    def attention_buffers(self, es, maps):
        nc = self.nc
        self.scores = [self.bank[0], self.bank[1]]
        self.ptp = [self.bank[2], self.bank[3]]
        self.obanks = [self.bank[4], self.bank[5]]
        self.prob = [[self.allocator(es)(f"prob{i}_{m}", [P, T]) for m in range(maps)] for i in range(2)]
        self.pt = [self.allocator(es)(f"pt{i}", [P, T]) for i in range(2)]
        self.stat = self.allocator(es)("stat", [P, 32, 2 * maps, 4])
        self.shifted = [self.allocator(es)(f"shifted{i}", [P, T]) for i in range(2)]

    def attention(self, units, ready):
        nc, c = self.nc, self.c
        N = len(units)
        c.dve.wait(ready)
        freeS, freeP, freePT, freeO, shift_free = [None, None], [None, None], [None, None], [None, None], [None, None]
        mid, ncall = {}, 0
        assert N <= 32
        for step in range(N + 2):
            if step < N:
                u, s = units[step], step % 2
                W = u["width"]
                done, stats = [], []
                for m, (q, kk) in enumerate(u["maps"]):
                    b = ncall % 2
                    ncall += 1
                    S = self.scores[b]
                    c.pe.wait(ready, freeS[b])
                    for n, (l, r, o, w) in enumerate([(q, kk, 0, W)] + u["extra"]):
                        mm = nc.tensor.matmul(S[:, o:o + w], l, r, start=n == 0, stop=n == len(u["extra"]),
                                              skip_group_check=True)
                    mm.then_inc(c.pe.sem, 1)
                    c.pe.n += 1
                    ms = c.pe.mark()
                    nmax = self.stat[:, step, 2 * m, 0:1]
                    rsum = self.stat[:, step, 2 * m, 1:2]
                    rinv = self.stat[:, step, 2 * m, 2:3]
                    Pm = self.prob[s][m][:, 0:W]
                    if u["decay"] is not None:
                        sh = self.shifted[b]
                        mx = c.dve(nc.vector.tensor_tensor_reduce, out=sh[:, 0:W], in0=S[:, 0:W],
                                   in1=u["decay"][:, 0:W], scale=1.0, scalar=3e38, op0=ALU.add, op1=ALU.min,
                                   accum_out=nmax, after=[ms, shift_free[b]])
                        freeS[b] = mx
                        me = c.act(nc.scalar.activation, Pm, sh[:, 0:W], ACT.Exp, bias=nmax, scale=-1.0,
                                   accum_out=rsum, after=[mx, freeP[s]])
                        shift_free[b] = me
                    else:
                        mx = c.dve(nc.vector.tensor_reduce, nmax, S[:, 0:W], AX.X, ALU.max, negate=True, after=[ms])
                        if u["sink"] is not None:
                            mx = c.dve(nc.vector.tensor_scalar, nmax, nmax, u["nsink"], None, ALU.min, after=[mx])
                        me = c.act(nc.scalar.activation, Pm, S[:, 0:W], ACT.Exp, bias=nmax, scale=1.0,
                                   accum_out=rsum, after=[mx, freeP[s]])
                        freeS[b] = me
                        if u["sink"] is not None:
                            esink = self.stat[:, step, 2 * m, 3:4]
                            mk = c.act(nc.scalar.activation, esink, u["sink"], ACT.Exp, bias=nmax, scale=1.0)
                            me = c.dve(nc.vector.tensor_tensor, rsum, rsum, esink, ALU.add, after=[me, mk])
                    mi = c.dve(nc.vector.reciprocal, rinv, rsum, after=[me])
                    done.append(mi)
                    stats.append(rinv)
                if u["mix"] is not None:
                    mix = u["mix"](self.prob[s][0][:, 0:W], self.prob[s][1][:, 0:W], stats, done)
                    done = [mix]
                mid[step] = (done, me, stats)
            if 1 <= step <= N:
                n = step - 1
                u, s = units[n], n % 2
                W = u["width"]
                done, me, stats = mid[n]
                mt = c.transposes([(self.ptp[s][:, i * P:(i + 1) * P], self.prob[s][0][:, i * P:(i + 1) * P])
                                   for i in range(W // P)], self.k("ident"),
                                  after=[done if u["mix"] is not None else me, freePT[s]])
                freeP[s] = mt
                if n % 2:
                    me2 = c.act(nc.scalar.copy, self.pt[s][:, 0:W], self.ptp[s][:, 0:W], after=[mt, mid.get(("pv", n - 2))])
                else:
                    me2 = c.dve(nc.vector.tensor_copy, self.pt[s][:, 0:W], self.ptp[s][:, 0:W], after=[mt, mid.get(("pv", n - 2))])
                freePT[s] = me2
                mid[("pt", n)] = me2
            if step >= 2:
                n = step - 2
                u, s = units[n], n % 2
                dv = u["values"][0].shape[-1]
                o = self.obanks[s][:, 0:dv]
                mp = c.products(o, [(self.pt[s][:, i * P:(i + 1) * P], v) for i, v in enumerate(u["values"])],
                                after=[mid[("pt", n)], freeO[s]])
                mid[("pv", n)] = mp
                freeO[s] = u["out"](o, mid[n][2][0], [mp, mid[n][0]])
        return freeO

    def store_T(self, y, n, banks, first, after):
        nc, c = self.nc, self.c
        free = [None] * len(banks)
        for j in range(n):
            b = j % len(banks)
            m = c.transposes([(banks[b][:, t * P:(t + 1) * P], y[:, t, j * P:(j + 1) * P]) for t in range(NT)],
                             self.k("ident"), after=[after, free[b]])
            free[b] = c.dve(nc.vector.tensor_copy, self.yT[:, bass.ds(first + j, 1), :].rearrange("p a t -> p (a t)"),
                            banks[b][:, :], after=[m])

    def fox(self, l):
        nc, c, A = self.nc, self.c, self.A
        with ExitStack() as es:
            sb = self.allocator(es)
            wf = sb("w_ff", [P, KD, 4])
            fb = sb("fox_bias", [P, 4])
            lf = sb("log_f", [P, NT, 4])
            tmp = sb("log_f_tmp", [P, NT, 4])
            rows = sb("log_f_rows", [4, T])
            crow = sb("c_rows", [4, T])
            cwide = sb("c_wide", [P, 4, T])
            wq, wk, wv, wg = [sb(n, [P, KD, P]) for n in ("wq", "wk", "wv", "wg")]
            qT, kT, v, g, gt, y = [sb(n, [P, T]) for n in ("qT", "kT", "v_tok", "gate", "gate_tmp", "y_tok")]
            cpair = sb("c_pair", [P, 2, T])
            self.attention_buffers(es, 1)
            ld = c.dma((wf[:, :, :], cols_of(A["w_in"], l, C1["ff"], 4)),
                       (fb[:, :], A["fox_b"][l].partition_broadcast(P)), slow=True)
            b = self.bank[0]
            m = self.proj_tok([b[:, 4 * i:4 * i + 4] for i in range(NT)], wf, self.hT, [ld])
            m = c.dve(nc.vector.tensor_tensor, lf[:, :, :], b[:, 0:16].rearrange("p (t h) -> p t h", h=4),
                      fb[:, :].unsqueeze(1).to_broadcast([P, NT, 4]), ALU.add, after=[m])
            m = self.log_sigmoid(lf[:, :, :], tmp[:, :, :], [m])
            m = self.to_rows(rows[:, :], lf, self.bank[1], [m])
            mc = c.dve(nc.vector.tensor_tensor_scan, crow[:, :], self.k("onesrow", 4), rows[:, :], 0.0,
                       ALU.mult, ALU.add, after=[m])
            for h in range(4):
                m = self.spread(self.bank[2 + h], h, crow[:, :], after=[mc])
                c.act(nc.scalar.copy, cwide[:, h, :], self.bank[2 + h][:, :], after=[m])
            c.barrier()
            b5, b6, b7 = self.bank[5], self.bank[6], self.bank[7]
            with nc.Fori(0, 2) as pair:
                lq, lk, lv, lg = [c.dma((w[:, :, :], cols_of(A["w_in"], l, pair * P + C1[n], P)))
                                  for w, n in ((wq, "fq"), (wk, "fk"), (wv, "fv"), (wg, "fg"))]
                mc = c.dve(nc.vector.tensor_copy, cpair[:, :, :], cwide[:, bass.ds(pair * 2, 2), :])
                mq = self.proj_T(b5[:, :], wq, self.hT, [lq])
                mq = c.act(nc.scalar.activation, qT[:, :], b5[:, :], ACT.Copy, scale=-HD ** -0.5, after=[mq])
                mk = self.proj_T(b6[:, :], wk, self.hT, [lk])
                mk = c.act(nc.scalar.copy, kT[:, :], b6[:, :], after=[mk])
                mv = self.proj_tok([b7[:, i * P:(i + 1) * P] for i in range(NT)], wv, self.hT, [lv])
                mv = c.act(nc.scalar.copy, v[:, :], b7[:, :], after=[mv])
                mg = self.proj_tok([b5[:, i * P:(i + 1) * P] for i in range(NT)], wg, self.hT, [lg, mq])
                mg = self.silu(g[:, :], b5[:, :], gt[:, :], [mg])
                units = []
                for h in range(2):
                    r = slice(HD * h, HD * h + HD)
                    for t in range(NT):
                        def out(o, rinv, marks, cs=slice(t * P + h * HD, t * P + h * HD + HD)):
                            return c.dve(nc.vector.scalar_tensor_tensor, y[:, cs], o, rinv, g[:, cs],
                                         ALU.mult, ALU.mult, after=[*marks, mg])
                        units.append(dict(
                            maps=[(qT[r, t * P:(t + 1) * P], kT[r, 0:(t + 1) * P])], width=(t + 1) * P,
                            extra=[(self.k("nident"), self.k("later"), t * P, P)], decay=cpair[:, h, :],
                            sink=None, mix=None,
                            values=[v[:, i * P + h * HD:i * P + h * HD + HD] for i in range(t + 1)], out=out))
                self.attention(units, [mq, mk, mv, mg, mc])
                self.store_T(y[:, :].rearrange("p (t n) -> p t n", n=P), 1, [b6], pair, [c.dve.mark()])
                c.barrier()

    def conv(self, l):
        nc, c, A = self.nc, self.c, self.A
        CT = CONV_CH // P
        PAD = TAPS - 1
        with ExitStack() as es:
            sb = self.allocator(es)
            wa, wb = sb("w_glu_a", [P, KD, CONV_CH]), sb("w_glu_b", [P, KD, CONV_CH])
            wg = sb("w_conv_gate", [P, KD, CONV_CH])
            wp = sb("w_pointwise", [P, CT, CONV_CH])
            taps = sb("taps", [P, TAPS, CT])
            small = sb("conv_params", [P, 3, CT])
            eps = sb("conv_eps", [P, 1])
            gl = sb("glu_padded", [P, CT, PAD + T])
            acc = sb("conv_acc", [P, CT, T])
            sq = sb("conv_sq", [P, CT, T])
            mean, rstd = sb("conv_mean", [P, T]), sb("conv_rstd", [P, T])
            gate, gtmp, y = [sb(n, [P, NT, CONV_CH]) for n in ("conv_gate", "conv_gate_tmp", "conv_y")]
            lw = [c.dma((w[:, :, :], cols_of(A["w_in"], l, C1[n] + o, CONV_CH)))
                  for w, n, o in ((wa, "glu", 0), (wb, "glu", CONV_CH), (wg, "cg", 0))]
            lp = c.dma((wp[:, :, :], A["conv_pw"][l].rearrange("(k p) n -> p k n", p=P)))
            lt = c.dma(*[(taps[:, :, j], A["conv_w"][l, :, j * P:(j + 1) * P].rearrange("w p -> p w")) for j in range(CT)],
                       *[(small[:, n, :], A[name][l].rearrange("(j p) -> p j", p=P))
                         for n, name in enumerate(("conv_b", "conv_ln_g", "conv_ln_b"))], slow=True)
            mz = [c.dve(nc.vector.memset, gl[:, :, 0:PAD], 0.0), c.dve(nc.vector.memset, eps[:, :], EPS)]
            ready = []
            for j in range(CT):
                ba, bb = self.bank[2 * j], self.bank[2 * j + 1]
                ma = self.proj_T(ba[:, :], wa[:, :, j * P:(j + 1) * P], self.hT, [lw[0]])
                mb = self.proj_T(bb[:, :], wb[:, :, j * P:(j + 1) * P], self.hT, [lw[1]])
                m = c.act(nc.scalar.activation, sq[:, j, :], bb[:, :], ACT.Tanh, scale=0.5, after=[mb])
                m = c.dve(nc.vector.tensor_scalar, sq[:, j, :], sq[:, j, :], 0.5, 0.5, ALU.mult, ALU.add, after=[m])
                ready.append(c.dve(nc.vector.tensor_tensor, gl[:, j, PAD:], sq[:, j, :], ba[:, :], ALU.mult, after=[m, ma]))
            for i in range(NT):
                bg = self.bank[4 + i // 2]
                m = c.products(bg[:, (i % 2) * 256:(i % 2) * 256 + 256],
                               [(self.hT[:, k, i * P:(i + 1) * P], wg[:, k, :]) for k in range(KD)], [lw[2]])
            mt = [c.act(nc.scalar.activation, gtmp[:, 2 * i:2 * i + 2, :].rearrange("p a n -> p (a n)"),
                        self.bank[4 + i][:, :], ACT.Tanh, scale=0.5, after=[m]) for i in range(2)]
            marks = [[ready[j], mz, lt] for j in range(CT)]
            for w in range(TAPS):
                for j in range(CT):
                    src = gl[:, j, w:w + T]
                    if w == 0:
                        marks[j] = [c.dve(nc.vector.tensor_scalar, acc[:, j, :], src, taps[:, w, j:j + 1],
                                          small[:, 0, j:j + 1], ALU.mult, ALU.add, after=marks[j])]
                    else:
                        marks[j] = [c.dve(nc.vector.scalar_tensor_tensor, acc[:, j, :], src, taps[:, w, j:j + 1],
                                          acc[:, j, :], ALU.mult, ALU.add, after=marks[j])]
            for i in range(2):
                mg = c.dve(nc.vector.scalar_tensor_tensor, gate[:, 2 * i:2 * i + 2, :].rearrange("p a n -> p (a n)"),
                           gtmp[:, 2 * i:2 * i + 2, :].rearrange("p a n -> p (a n)"), 1.0, self.bank[4 + i][:, :],
                           ALU.add, ALU.mult, after=mt)
            m = c.products(self.bank[0][:, :], [(self.k("ones"), acc[:, j, :]) for j in range(CT)], marks)
            mm = c.act(nc.scalar.activation, mean[:, :], self.bank[0][:, :], ACT.Copy, scale=1.0 / CONV_CH, after=[m])
            md = [c.dve(nc.vector.tensor_tensor, acc[:, j, :], acc[:, j, :], mean[:, :], ALU.subtract, after=[mm])
                  for j in range(CT)]
            m = [c.act(nc.scalar.activation, sq[:, j, :], acc[:, j, :], ACT.Square, after=[md[j]]) for j in range(CT)]
            m = c.products(self.bank[1][:, :], [(self.k("ones"), sq[:, j, :]) for j in range(CT)], m)
            m = c.act(nc.scalar.activation, rstd[:, :], self.bank[1][:, :], ACT.Ln, bias=eps[:, 0:1],
                      scale=1.0 / CONV_CH, after=[m])
            m = c.act(nc.scalar.activation, rstd[:, :], rstd[:, :], ACT.Exp, scale=-0.5, after=[m])
            ms = []
            for j in range(CT):
                a = c.dve(nc.vector.scalar_tensor_tensor, acc[:, j, :], acc[:, j, :], small[:, 1, j:j + 1], rstd[:, :],
                          ALU.mult, ALU.mult, after=[m])
                a = c.dve(nc.vector.tensor_scalar, acc[:, j, :], acc[:, j, :], small[:, 2, j:j + 1], None, ALU.add, after=[a])
                a = self.silu(acc[:, j, :], acc[:, j, :], sq[:, j, :], [a])
                ms.append(a)
            for i in range(NT):
                m = c.products(self.bank[2 + i // 2][:, (i % 2) * 256:(i % 2) * 256 + 256],
                               [(acc[:, j, i * P:(i + 1) * P], wp[:, j, :]) for j in range(CT)], [ms, lp])
            for i in range(NT):
                md = c.dve(nc.vector.scalar_tensor_tensor, y[:, i, :], self.bank[2 + i // 2][:, (i % 2) * 256:(i % 2) * 256 + 256],
                          0.5, gate[:, i, :], ALU.mult, ALU.mult, after=[m, mg])
            for j in range(CT):
                b = self.bank[6 + j]
                mt = c.transposes([(b[:, t * P:(t + 1) * P], y[:, t, j * P:(j + 1) * P]) for t in range(NT)],
                                  self.k("ident"), after=[md])
                c.dve(nc.vector.tensor_copy, self.yT[:, FOX_W // P + j, :], b[:, :], after=[mt])
            c.barrier()

    def compress(self, l, kcmpT, vcmp):
        nc, c, A = self.nc, self.c, self.A
        M = CMP_LEN // 2
        N = N_CMP
        with ExitStack() as es:
            sb = self.allocator(es)
            wx = [sb(f"w_cmp_in{i}", [P, KD, 2, 2, HD]) for i in range(2)]
            w1 = [sb(f"cmp_w1_{i}", [P, M, 256]) for i in range(2)]
            w2 = [sb(f"cmp_w2_{i}", [P, 2, 2, HD]) for i in range(2)]
            pe = [sb(f"cmp_pe{i}", [P, M]) for i in range(2)]
            two = sb("two_tokens", [P, T])
            blk = sb("cmp_blocks", [P, M, 2, N])
            hid, cube, hidT = sb("hid", [P, 2, 2 * N]), sb("cube", [P, 2, 2 * N]), sb("hid_gelu", [P, 2, 2 * N])
            rtmp = sb("cmp_rope_tmp", [P, 2, N])
            loads = []
            for i, (col, kv) in enumerate((("nkc", "k"), ("nvc", "v"))):
                src = cols_of(A["w_in"], l, C1[col], P).rearrange("p k (g d) -> p k g d", g=2)
                la = c.dma(*[(wx[i][:, :, g, r, :], src[:, :, g, :]) for g in range(2) for r in range(2)])
                lb = c.dma((w1[i][:, :, :], A[f"cmp_{kv}_w1"][l].rearrange("(m p) h -> p m h", p=P)))
                w2d = A[f"cmp_{kv}_w2"][l].rearrange("(j p) o -> p j o", p=P)
                lc = c.dma((w2[i][:, :, 0, :], w2d), (w2[i][:, :, 1, :], w2d),
                           (pe[i][0:HD, :], A[f"cmp_pe_{kv}"][l].rearrange("(m r) d -> r d m", r=2)[0]),
                           (pe[i][HD:P, :], A[f"cmp_pe_{kv}"][l].rearrange("(m r) d -> r d m", r=2)[1]), slow=True)
                loads.append((la, lb, lc))
            used, usedh = None, None
            for i in range(2):
                la, lb, lc = loads[i]
                mb = []
                for g in range(2):
                    b = self.bank[g]
                    m = self.proj_T(b[:, :], wx[i][:, :, g, :, :].rearrange("p k r d -> p k (r d)"), self.hT,
                                    [la, mb, used])
                    ma = c.act(nc.scalar.copy, two[0:HD, :], b[0:HD, :], after=[m, mb])
                    mz = c.act(nc.scalar.copy, two[HD:P, 0:T - 1], b[HD:P, 1:T], after=[mb])
                    for q in range(CMP_LEN // CMP_STRIDE):
                        h = M // 2
                        src = two[:, CMP_STRIDE * q:CMP_STRIDE * q + CMP_STRIDE * N].rearrange(
                            "p (n m r) -> p m n r", m=h, r=2)[:, :, :, 0]
                        m2 = c.dve(nc.vector.tensor_tensor, blk[:, q * h:(q + 1) * h, g, :], src,
                                   pe[i][:, q * h:(q + 1) * h].unsqueeze(2).to_broadcast([P, h, N]), ALU.add,
                                   after=[ma, mz, lc, used])
                    mb = [m2]
                bh = self.bank[2 + i]
                for j in range(2):
                    m = c.products(bh[:, j * 2 * N:(j + 1) * 2 * N],
                                   [(w1[i][:, q, j * P:(j + 1) * P], blk[:, q, :, :].rearrange("p g n -> p (g n)"))
                                    for q in range(M)], [lb, mb])
                used = m
                x = bh[:, 0:4 * N].rearrange("p (j n) -> p j n", j=2)
                m = c.act(nc.scalar.activation, cube[:, :, :], x, ACT.Square, after=[m, usedh])
                m = c.dve(nc.vector.tensor_scalar, cube[:, :, :], cube[:, :, :], 0.044715, 1.0, ALU.mult, ALU.add, after=[m])
                m = c.dve(nc.vector.tensor_tensor, cube[:, :, :], cube[:, :, :], x, ALU.mult, after=[m])
                m = c.act(nc.scalar.activation, hid[:, :, :], cube[:, :, :], ACT.Tanh,
                          scale=float(np.sqrt(2 / np.pi)), after=[m])
                m = c.dve(nc.vector.scalar_tensor_tensor, hidT[:, :, :], hid[:, :, :], 1.0, x, ALU.add, ALU.mult,
                          after=[m, usedh])
                m = c.dve(nc.vector.tensor_scalar, hidT[:, :, :], hidT[:, :, :], 0.5, None, ALU.mult, after=[m])
                if i == 0:
                    m = c.products(self.bank[4][:, 0:2 * N],
                                   [(w2[i][:, j, :, :].rearrange("p r d -> p (r d)"), hidT[:, j, :]) for j in range(2)], [m, lc])
                    usedh = m
                    mk = c.act(nc.scalar.copy, kcmpT[:, :, :].rearrange("p g n -> p (g n)"), self.bank[4][:, 0:2 * N], after=[m])
                    for g in range(2):
                        self.rope(kcmpT[:, g, :], rtmp[:, g, :], self.bank[5 + g], self.k("rot1"), self.k("cosc"),
                                  self.k("sinc"), [mk])
                else:
                    for g in range(2):
                        m2 = c.products(self.bank[7][0:N, g * HD:(g + 1) * HD],
                                        [(hidT[:, j, g * N:(g + 1) * N], w2[i][:, j, 0, :]) for j in range(2)], [m, lc])
                    c.act(nc.scalar.copy, vcmp[:, :, :].rearrange("p g d -> p (g d)"), self.bank[7][0:N, 0:2 * HD], after=[m2])
            c.barrier()

    def nsa(self, l):
        nc, c, A = self.nc, self.c, self.A
        N = N_CMP
        H = 4
        with ExitStack() as es:
            sb = self.allocator(es)
            kcmpT = sb("k_cmp", [P, 2, N])
            vcmp = sb("v_cmp", [N, 2, HD])
            self.compress(l, kcmpT, vcmp)
            gl = sb("branch_gates", [P, NT, 24])
            wgl = sb("w_branch_gates", [P, KD, 24])
            wk = [sb(f"w_{n}", [P, KD, 2, HD]) for n in ("ks", "kw")]
            wv = sb("w_vs_vw", [P, KD, 2, HD])
            wq, wg = sb("w_q", [P, KD, 2 * P]), sb("w_gate", [P, KD, 2 * P])
            qT = [sb(f"qT{i}", [P, T]) for i in range(2)]
            kT = [sb(f"kT{i}", [P, T]) for i in range(2)]
            rt = sb("rope_tmp", [P, T])
            v = sb("v_tok", [P, NT, 2 * HD])
            gate, y = sb("gate", [P, NT, 2 * P]), sb("y_tok", [P, NT, 2 * P])
            kc, vc, gg = sb("k_cmp_group", [P, N]), sb("v_cmp_group", [N, HD]), sb("gates_group", [P, NT, 12])
            pc, pcT = sb("p_cmp", [P, H, NT * N]), sb("p_cmpT", [N, NT, P])
            cst = sb("cmp_stat", [P, 3, H, NT])
            coef = sb("coef", [P, 32])
            self.attention_buffers(es, 1)
            ld = c.dma((wgl[:, :, :], cols_of(A["w_in"], l, C1["ngl"], 24)), slow=True)
            m = self.proj_tok([self.bank[0][:, 24 * i:24 * i + 24] for i in range(NT)], wgl, self.hT, [ld])
            self.sigmoid(gl[:, :, :], self.bank[0][:, 0:96].rearrange("p (t n) -> p t n", n=24), [m])
            c.barrier()
            with nc.Fori(0, 2) as grp:
                def dup(name):
                    return cols_of(A["w_in"], l, grp * HD + C1[name], HD)
                lq = c.dma((wq[:, :, :], cols_of(A["w_in"], l, grp * 256 + C1["nq"], 2 * P)))
                lk = [c.dma((wk[i][:, :, 0, :], dup(n)), (wk[i][:, :, 1, :], dup(n))) for i, n in enumerate(("nks", "nkw"))]
                lv = c.dma((wv[:, :, 0, :], dup("nvs")), (wv[:, :, 1, :], dup("nvw")))
                lg = c.dma((wg[:, :, :], cols_of(A["w_in"], l, grp * 256 + C1["ng"], 2 * P)))
                mg1 = [c.dve(nc.vector.tensor_copy, kc[:, :], kcmpT[:, bass.ds(grp, 1), :].rearrange("p a n -> p (a n)")),
                       c.dve(nc.vector.tensor_copy, vc[:, :], vcmp[:, bass.ds(grp, 1), :].rearrange("p a n -> p (a n)")),
                       c.dve(nc.vector.tensor_copy, gg[:, :, :], gl[:, :, bass.ds(grp * 12, 12)])]
                ready = []
                for i in range(2):
                    m = self.proj_T(self.bank[i][:, :], wq[:, :, i * P:(i + 1) * P], self.hT, [lq])
                    m = c.act(nc.scalar.activation, qT[i][:, :], self.bank[i][:, :], ACT.Copy, scale=HD ** -0.5, after=[m])
                    ready.append(self.rope(qT[i][:, :], rt[:, :], self.bank[4 + i], self.k("rot1"), self.k("cos1"),
                                           self.k("sin1"), [m, ready[:]]))
                for i in range(2):
                    m = self.proj_T(self.bank[2 + i][:, :], wk[i][:, :, :, :].rearrange("p k r d -> p k (r d)"), self.hT, [lk[i]])
                    m = c.act(nc.scalar.copy, kT[i][:, :], self.bank[2 + i][:, :], after=[m])
                    ready.append(self.rope(kT[i][:, :], rt[:, :], self.bank[6 + i], self.k("rot1"), self.k("cos1"),
                                           self.k("sin1"), [m, ready[:]]))
                b5 = self.bank[5]
                m = self.proj_tok([b5[:, i * P:(i + 1) * P] for i in range(NT)],
                                  wv[:, :, :, :].rearrange("p k r d -> p k (r d)"), self.hT, [lv, ready])
                mv = c.act(nc.scalar.copy, v[:, :, :].rearrange("p t n -> p (t n)"), b5[:, :], after=[m])
                for i in range(2):
                    b = self.bank[6 + i]
                    m = self.proj_tok([b[:, j * 256:(j + 1) * 256] for j in range(2)], wg[:, :, :],
                                      self.hT[:, :, i * 256:(i + 1) * 256], [lg, ready], tiles=2)
                    mg = self.silu(gate[:, 2 * i:2 * i + 2, :].rearrange("p a n -> p (a n)"), b[:, :],
                                   y[:, 2 * i:2 * i + 2, :].rearrange("p a n -> p (a n)"), [m])
                for h in (0, 2, 1, 3):
                    r = slice(HD * (h % 2), HD * (h % 2) + HD)
                    for t in range(NT):
                        at = (h // 2 * NT + t) * N
                        m = c.products(self.bank[h % 2][:, at:at + N], [(qT[h // 2][r, t * P:(t + 1) * P], kc[r, :])], [ready, mg1])
                neg, one = self.k("cmpneg").unsqueeze(1), self.k("cmpone").unsqueeze(1)
                wide = [P, H, NT * N]
                for par in range(2):
                    ma = c.dve(nc.vector.tensor_tensor, pc[:, par::2, :],
                               self.bank[par][:, 0:2 * NT * N].rearrange("p (h n) -> p h n", h=2),
                               neg.to_broadcast([P, 2, NT * N]), ALU.add, after=[m])
                m = ma
                p4 = pc[:, :, :].rearrange("p h (t n) -> p (h t) n", n=N)
                st = [cst[:, i, :, :].rearrange("p h t -> p (h t)") for i in range(3)]
                m = c.dve(nc.vector.tensor_reduce, st[0], p4, AX.X, ALU.max, after=[m])
                m = c.dve(nc.vector.tensor_tensor, p4, p4, st[0].unsqueeze(2).to_broadcast([P, H * NT, N]), ALU.subtract, after=[m])
                m = c.act(nc.scalar.activation, p4, p4, ACT.Exp, after=[m])
                m = c.dve(nc.vector.tensor_reduce, st[1], p4, AX.X, ALU.add, after=[m])
                mi = c.dve(nc.vector.reciprocal, st[2], st[1], after=[m])
                mp = c.dve(nc.vector.tensor_tensor, pc[:, :, :], pc[:, :, :], one.to_broadcast(wide), ALU.mult, after=[m])
                b1, b4 = self.bank[1], self.bank[4]
                mc = None
                for h in range(H):
                    m = c.transposes([(b1[0:N, t * P:(t + 1) * P], pc[:, h, t * N:(t + 1) * N]) for t in range(NT)],
                                     self.k("ident"), after=[mp, mc])
                    m = c.act(nc.scalar.copy, pcT[:, :, :].rearrange("p t n -> p (t n)"), b1[0:N, :], after=[m, mc])
                    for t in range(NT):
                        mc = c.products(b4[:, t * HD:(t + 1) * HD], [(pcT[:, t, :], vc[:, :])], [m, mg1, mv, mg])
                    for t in range(NT):
                        j = h * NT + t
                        m2 = c.dve(nc.vector.tensor_tensor, coef[:, j:j + 1], gg[:, t, 3 * h:3 * h + 1], st[2][:, j:j + 1],
                                   ALU.mult, after=[mi, mg1, mg])
                        mc = c.dve(nc.vector.tensor_scalar, y[:, t, h * HD:(h + 1) * HD], b4[:, t * HD:(t + 1) * HD],
                                   coef[:, j:j + 1], None, ALU.mult, after=[m2, mc])
                cmp_done = mc
                units = []
                n = 0
                for br in range(2):
                    for h in range(H):
                        r = slice(HD * (h % 2), HD * (h % 2) + HD)
                        for t in range(NT):
                            def out(o, rinv, marks, br=br, h=h, t=t):
                                w = y[:, t, h * HD:(h + 1) * HD]
                                cf = rinv
                                m = c.dve(nc.vector.tensor_tensor, cf, rinv, gg[:, t, 3 * h + 1 + br:3 * h + 2 + br],
                                          ALU.mult, after=marks)
                                m = c.dve(nc.vector.scalar_tensor_tensor, w, o, cf, w, ALU.mult, ALU.add, after=[m])
                                if br:
                                    c.dve(nc.vector.tensor_tensor, w, w, gate[:, t, h * HD:(h + 1) * HD], ALU.mult, after=[m])
                                return m
                            units.append(dict(
                                maps=[(qT[h // 2][r, t * P:(t + 1) * P], kT[br][r, 0:(t + 1) * P])], width=(t + 1) * P,
                                extra=[(self.k("ident"), self.k("later"), t * P, P)], decay=None, sink=None, mix=None,
                                values=[v[:, i, br * HD:(br + 1) * HD] for i in range(t + 1)], out=out))
                self.attention(units, [ready, mv, mg, cmp_done])
                self.store_T(y, 2, [self.bank[5], self.bank[6]], grp * 2 + 4, [c.dve.mark()])
                c.barrier()

    def prime(self, slots):
        for s in range(slots):
            self.nc.tensor.sem_inc(self.c.mm[s], 1)
            self.nc.vector.sem_inc(self.c.ev[s], 1)

    def stream_add(self, load, src, kt, trips=4, slots=2):
        nc, c = self.nc, self.c
        with ExitStack() as es:
            w = [self.allocator(es)(f"w_slot{s}", [P, kt, P]) for s in range(slots)]
            self.prime(slots)
            with nc.Fori(0, trips) as i:
                for s in range(slots):
                    tile = i * slots + s
                    nc.sync.wait_ge(c.mm[s], i + 1)
                    nc.sync.dma_start(w[s][:, :, :], load(tile)).then_inc(c.ld[s], 16)
                    nc.tensor.wait_ge(c.ld[s], i * 16 + 16)
                    nc.tensor.wait_ge(c.ev[s], i + 1)
                    for k in range(kt):
                        m = nc.tensor.matmul(self.bank[s][:, :], w[s][:, k, :], src[:, k, :], start=k == 0, stop=k == kt - 1)
                    m.then_inc(c.mm[s], 1)
                    nc.vector.wait_ge(c.mm[s], i + 2)
                    x = self.xT[:, bass.ds(tile, 1), :].rearrange("p a t -> p (a t)")
                    nc.vector.tensor_tensor(x, x, self.bank[s][:, :], ALU.add).then_inc(c.ev[s], 1)
            c.barrier()

    def load_x(self, x):
        nc, c = self.nc, self.c
        with ExitStack() as es:
            xt = self.allocator(es)("x_tok", [P, NT, D])
            lc = c.dma((self.const[:, :], self.const_dram))
            lx = c.dma((xt[:, :, :], x.rearrange("(t p) d -> p t d", p=P)))
            for k in range(KD):
                m = c.transposes([(self.bank[k][:, t * P:(t + 1) * P], xt[:, t, k * P:(k + 1) * P]) for t in range(NT)],
                                 self.k("ident"), after=[lc, lx])
                c.dve(nc.vector.tensor_copy, self.xT[:, k, :], self.bank[k][:, :], after=[m])
            c.barrier()

    def store(self, out, src):
        nc, c = self.nc, self.c
        with ExitStack() as es:
            xt = self.allocator(es)("x_tok", [P, NT, D])
            for k in range(KD):
                m = c.transposes([(self.bank[k][:, t * P:(t + 1) * P], src[:, k, t * P:(t + 1) * P]) for t in range(NT)],
                                 self.k("ident"))
                for t in range(NT):
                    m2 = c.dve(nc.vector.tensor_copy, xt[:, t, k * P:(k + 1) * P], self.bank[k][:, t * P:(t + 1) * P], after=[m])
            c.dma((out.rearrange("(t p) d -> p t d", p=P), xt[:, :, :]), after=[m2])
            c.barrier()

    def first_block(self):
        nc, A = self.nc, self.A
        with nc.Fori(0, DEPTH) as l:
            self.norm(self.hT, A["norm_g"][l])
            self.fox(l)
            self.conv(l)
            self.nsa(l)
            self.stream_add(lambda e: cols_of(A["w_out"], l, e * P, P), self.yT, KD)
        self.norm(self.xT, A["final_g"])

    def scan_rows(self, out, rows, keep, op, backward, after):
        nc, c = self.nc, self.c
        if backward:
            out, rows, keep = out[:, ::-1], rows[:, ::-1], keep[:, ::-1]
        return c.dve(nc.vector.tensor_tensor_scan, out, keep, rows, 0.0, ALU.mult, op, after=after)

    def to_cols(self, dst, rows, bank, after):
        n = rows.shape[0]
        m = self.c.transposes([(bank[:, t * n:(t + 1) * n], rows[:, t * P:(t + 1) * P]) for t in range(NT)],
                              self.k("ident"), after)
        return self.c.dve(self.nc.vector.tensor_copy, dst, bank[:, 0:NT * n].rearrange("p (t n) -> p t n", n=n), after=[m])

    def norm_blocks(self, y, n, gain, sq, ss, eps, after):
        nc, c = self.nc, self.c
        for i in range(n):
            m = c.act(nc.scalar.activation, sq[:, i, :], y[:, i, :], ACT.Square, accum_out=ss[:, i:i + 1], after=after)
        m = c.act(nc.scalar.activation, ss[:, 0:n], ss[:, 0:n], ACT.Ln, bias=eps, scale=1.0 / P, after=[m])
        m = c.act(nc.scalar.activation, ss[:, 0:n], ss[:, 0:n], ACT.Exp, scale=-0.5, after=[m])
        for i in range(n):
            m2 = c.dve(nc.vector.scalar_tensor_tensor, y[:, i, :], y[:, i, :], ss[:, i:i + 1], gain(i), ALU.mult, ALU.mult,
                       after=[m, *after])
        return m2

    def gdn(self, l):
        nc, c, A = self.nc, self.c, self.A
        H = 4
        W4 = [P, NT, P]
        with ExitStack() as es:
            sb = self.allocator(es)
            wab = sb("w_ab", [P, KD, 16])
            par = sb("gdn_params", [P, 2, 8])
            q5 = sb("chunk_scalars", [P, 6, NT, 2, H])
            g = sb("log_decay", [P, NT, 8])
            tmp = sb("log_decay_tmp", [P, NT, 8])
            tot = sb("chunk_total", [P, NT, 8])
            rows = [sb(f"g_rows{d}", [H, T]) for d in range(2)]
            gcr = [sb(f"gc_rows{d}", [H, T]) for d in range(2)]
            wide = sb("gc_wide", [P, 8, T])
            gain = sb("gdn_gain", [P, P])
            eps = sb("gdn_eps", [P, 1])
            pad = sb("qkv_padded", [P, 3, T + 4])
            ld = c.dma((wab[:, :, :], cols_of(A["w_in_2"], l, C2["a_ab"], 16)),
                       (par[:, 0, :], A["gdn_a_log_2"][l].rearrange("d h -> (d h)").partition_broadcast(P)),
                       (par[:, 1, :], A["gdn_dt_bias_2"][l].rearrange("d h -> (d h)").partition_broadcast(P)),
                       (gain[:, :], A["gdn_norm_g_2"][l].partition_broadcast(P)), slow=True)
            c.dve(nc.vector.memset, eps[:, :], EPS)
            c.dve(nc.vector.memset, pad[:, :, :], 0.0)
            b = self.bank[0]
            m = self.proj_tok([b[:, 16 * i:16 * i + 16] for i in range(NT)], wab, self.hT, [ld])
            z = b[:, 0:64].rearrange("p (t n) -> p t n", n=16)
            mb = c.act(nc.scalar.activation, q5[:, 0, :, :, :].rearrange("p t d h -> p t (d h)"), z[:, :, 8:16], ACT.Tanh,
                       scale=0.5, after=[m])
            m = c.dve(nc.vector.tensor_tensor, g[:, :, :], z[:, :, 0:8], par[:, 1:2, :].to_broadcast([P, NT, 8]),
                      ALU.add, after=[mb])
            beta = q5[:, 0, :, :, :].rearrange("p t d h -> p t (d h)")
            mb = c.dve(nc.vector.tensor_scalar, beta, beta, 0.5, 0.5, ALU.mult, ALU.add, after=[mb])
            m = c.act(nc.scalar.activation, tmp[:, :, :], g[:, :, :], ACT.Abs, after=[m])
            m = c.act(nc.scalar.activation, tmp[:, :, :], tmp[:, :, :], ACT.Exp, scale=-1.0, after=[m])
            m = c.act(nc.scalar.activation, tmp[:, :, :], tmp[:, :, :], ACT.Ln, bias=1.0, after=[m])
            ma = c.act(nc.scalar.activation, par[:, 0, :], par[:, 0, :], ACT.Exp, after=[ld])
            m = c.dve(nc.vector.scalar_tensor_tensor, g[:, :, :], g[:, :, :], 0.0, tmp[:, :, :], ALU.max, ALU.add, after=[m])
            m = c.dve(nc.vector.tensor_tensor, g[:, :, :], g[:, :, :], par[:, 0:1, :].to_broadcast([P, NT, 8]), ALU.mult, after=[m, ma])
            mg = c.dve(nc.vector.tensor_scalar, g[:, :, :], g[:, :, :], -1.0, None, ALU.mult, after=[m])
            m = c.products(self.bank[1][:, 0:32], [(self.k("ones"), g[:, :, :].rearrange("p t n -> p (t n)"))], [mg])
            mt = c.dve(nc.vector.tensor_copy, tot[:, :, :].rearrange("p t n -> p (t n)"), self.bank[1][:, 0:32], after=[m])
            for d in range(2):
                m = self.to_rows(rows[d][:, :], g[:, :, d * H:(d + 1) * H], self.bank[2 + d], [mg])
                m = self.scan_rows(gcr[d][:, :], rows[d][:, :], self.k("carryb" if d else "carryf", H), ALU.add, d, [m])
                mc = self.to_cols(q5[:, 5, :, d, :], gcr[d][:, :], self.bank[4 + d], [m])
                for h in range(H):
                    bb = self.bank[6 + h % 2]
                    mw = self.spread(bb, h, gcr[d][:, :], after=[m, c.act.mark()])
                    c.act(nc.scalar.copy, wide[:, d * H + h, :], bb[:, :], after=[mw])
            q = [q5[:, i, :, :, :].rearrange("p t d h -> p t (d h)") for i in range(6)]
            c.act(nc.scalar.activation, q[4], tot[:, :, :], ACT.Exp, after=[mt])
            me = c.act(nc.scalar.activation, q[2], q[5], ACT.Exp, after=[mc])
            m = c.dve(nc.vector.tensor_tensor, q[3], tot[:, :, :], q[5], ALU.subtract, after=[mc, mt])
            c.act(nc.scalar.activation, q[3], q[3], ACT.Exp, after=[m])
            c.dve(nc.vector.tensor_tensor, q[1], q[2], q[0], ALU.mult, after=[me, mb])
            c.barrier()

            ws = [sb(f"w_{n}", [P, KD, P]) for n in "qkvz"]
            taps = sb("qkv_taps", [P, 3, 5])
            acc = sb("qkv", [P, 3, T])
            sqt = sb("qkv_tmp", [P, 3, T])
            zt = sb("z_gate", W4)
            ktok, vtok = sb("k_tok", W4), sb("v_tok", W4)
            osum = sb("o_sum", W4)
            ss = sb("sum_sq", [P, 8])
            hq = sb("head_scalars", [P, 6, NT, 2])
            buf = {n: [sb(f"{n}{d}", W4) for d in range(2)] for n in
                   ("A", "AT", "aT", "M", "MT", "LT", "X", "vb", "kbe", "kdec")}
            S = [sb(f"state{d}", [P, P]) for d in range(2)]
            vn = [sb(f"v_new{d}", [P, P]) for d in range(2)]
            with nc.Fori(0, H) as h:
                lw = [c.dma((w[:, :, :], cols_of(A["w_in_2"], l, h * P + C2[n] + o, P)))
                      for w, n, o in zip(ws, ("a_qkv", "a_qkv", "a_qkv", "a_z"), (0, 512, 1024, 0))]
                lt = c.dma(*[(taps[:, i, :], A["gdn_conv_w_2"][l, :, bass.ds(h * P + 512 * i, P)].rearrange("w p -> p w"))
                             for i in range(3)], slow=True)
                mh = c.dve(nc.vector.tensor_copy, hq[:, :, :, :].rearrange("p i t d -> p (i t d)"),
                           q5[:, :, :, :, bass.ds(h, 1)].rearrange("p i t d o -> p (i t d o)"))
                conv = []
                for i in range(3):
                    m = self.proj_T(self.bank[i][:, :], ws[i], self.hT, [lw[i]])
                    m = c.act(nc.scalar.copy, pad[:, i, 2:2 + T], self.bank[i][:, :], after=[m])
                    m = c.dve(nc.vector.tensor_scalar, acc[:, i, :], pad[:, i, 0:T], taps[:, i, 0:1], None, ALU.mult, after=[m, lt])
                    for w in range(1, 5):
                        m = c.dve(nc.vector.scalar_tensor_tensor, acc[:, i, :], pad[:, i, w:w + T], taps[:, i, w:w + 1],
                                  acc[:, i, :], ALU.mult, ALU.add, after=[m])
                    conv.append(self.silu(acc[:, i, :], acc[:, i, :], sqt[:, i, :], [m]))
                m = self.proj_tok([self.bank[3][:, i * P:(i + 1) * P] for i in range(NT)], ws[3], self.hT, [lw[3]])
                m = self.silu(zt[:, :, :].rearrange("p t n -> p (t n)"), self.bank[3][:, :],
                              osum[:, :, :].rearrange("p t n -> p (t n)"), [m])
                mz = c.pool(nc.gpsimd.tensor_tensor, zt[:, :, :], zt[:, :, :], gain[:, :].unsqueeze(1).to_broadcast(W4),
                            ALU.mult, after=[m])
                unit = []
                for i in range(2):
                    bb = self.bank[4 + i]
                    m = c.act(nc.scalar.activation, sqt[:, i, :], acc[:, i, :], ACT.Square, after=[conv[i]])
                    m = c.products(bb[:, :], [(self.k("ones"), sqt[:, i, :])], [m])
                    m = c.act(nc.scalar.activation, sqt[:, i, :], bb[:, :], ACT.Ln, bias=eps[:, 0:1], after=[m])
                    m = c.act(nc.scalar.activation, sqt[:, i, :], sqt[:, i, :], ACT.Exp, scale=-0.5, after=[m])
                    unit.append(c.dve(nc.vector.scalar_tensor_tensor, acc[:, i, :], acc[:, i, :],
                                      P ** -0.5 if i == 0 else 1.0, sqt[:, i, :], ALU.mult, ALU.mult, after=[m]))
                qT, kT, vT = acc[:, 0, :], acc[:, 1, :], acc[:, 2, :]
                tok = []
                for bb, dst, src, mk in ((self.bank[6], ktok, kT, unit[1]), (self.bank[7], vtok, vT, conv[2])):
                    m = c.transposes([(bb[:, t * P:(t + 1) * P], src[:, t * P:(t + 1) * P]) for t in range(NT)],
                                     self.k("ident"), [mk])
                    tok.append(c.act(nc.scalar.copy, dst[:, :, :].rearrange("p t n -> p (t n)"), bb[:, :], after=[m]))
                ch = [slice(t * P, (t + 1) * P) for t in range(NT)]
                for t in range(NT):
                    mkk = c.products(self.bank[0][:, ch[t]], [(kT[:, ch[t]], kT[:, ch[t]])], [unit])
                for t in range(NT):
                    mkq = c.products(self.bank[1][:, ch[t]], [(kT[:, ch[t]], qT[:, ch[t]])], [conv])
                flat = lambda x: x[:, :, :].rearrange("p t n -> p (t n)")
                mAT, mM, mMT, maT, mA, used = [None] * 2, [None] * 2, [None] * 2, [None] * 2, [None] * 2, [None] * 2
                mvb = [None] * 2
                wide3 = lambda name: self.k(name).unsqueeze(1).to_broadcast(W4)
                lev = lambda name, s: self.k(name)[:, s * P:(s + 1) * P].unsqueeze(1).to_broadcast(W4)
                for d in range(2):
                    A_, AT, aT = buf["A"][d], buf["AT"][d], buf["aT"][d]
                    for t in range(NT):
                        gc = hq[:, 5, t, d:d + 1]
                        row = wide[:, bass.ds(h + d * H, 1), ch[t]].rearrange("p a t -> p (a t)")
                        m1 = c.dve(nc.vector.tensor_scalar, A_[:, t, :], row, gc, 0.0, ALU.subtract, ALU.max, after=[mh])
                        m2 = c.dve(nc.vector.tensor_scalar, aT[:, t, :], row, gc, 0.0, ALU.subtract, ALU.min, after=[mh])
                    m1 = c.act(nc.scalar.activation, flat(A_), flat(A_), ACT.Exp, scale=-1.0, after=[m1])
                    m2 = c.act(nc.scalar.activation, flat(aT), flat(aT), ACT.Exp, after=[m2])
                    m1 = c.dve(nc.vector.tensor_tensor, A_[:, :, :], A_[:, :, :], wide3("sup" if d else "slow"), ALU.mult, after=[m1])
                    m2 = c.pool(nc.gpsimd.tensor_tensor, aT[:, :, :], aT[:, :, :], wide3("low" if d else "up"), ALU.mult, after=[m2])
                    maT[d] = c.dve(nc.vector.tensor_tensor, flat(aT), flat(aT), self.bank[1][:, :], ALU.mult, after=[m2, mkq])
                    for t in range(NT):
                        mA[d] = c.dve(nc.vector.scalar_tensor_tensor, A_[:, t, :], self.bank[0][:, ch[t]], hq[:, 0, t, d:d + 1],
                                      A_[:, t, :], ALU.mult, ALU.mult, after=[m1, mkk])
                    bb = self.bank[2 + d]
                    m = c.transposes([(bb[:, ch[t]], A_[:, t, :]) for t in range(NT)], self.k("ident"), [mA[d]])
                    mAT[d] = c.act(nc.scalar.copy, flat(AT), bb[:, :], after=[m])
                    for n, src, i in (("vb", vtok, 0), ("kbe", ktok, 1), ("kdec", ktok, 3)):
                        mvb[d] = c.pool(nc.gpsimd.tensor_tensor, buf[n][d][:, :, :], src[:, :, :],
                                        hq[:, i, :, d:d + 1].to_broadcast(W4), ALU.mult, after=[tok, mh])
                for d in range(2):
                    A_, AT, M, MT = buf["A"][d], buf["AT"][d], buf["M"][d], buf["MT"][d]
                    lo, up = ("levup", "levlow") if d else ("levlow", "levup")
                    m1 = c.dve(nc.vector.tensor_tensor, M[:, :, :], A_[:, :, :], lev(lo, 0), ALU.mult, after=[mA[d]])
                    m2 = c.dve(nc.vector.tensor_tensor, MT[:, :, :], AT[:, :, :], lev(up, 0), ALU.mult, after=[mAT[d]])
                    mM[d] = c.dve(nc.vector.tensor_tensor, M[:, :, :], wide3("ident"), M[:, :, :], ALU.subtract, after=[m1])
                    mMT[d] = c.dve(nc.vector.tensor_tensor, MT[:, :, :], wide3("ident"), MT[:, :, :], ALU.subtract, after=[m2])
                for s in range(1, LEVELS):
                    for d in range(2):
                        A_, AT, M, MT = buf["A"][d], buf["AT"][d], buf["M"][d], buf["MT"][d]
                        LT, X = buf["LT"][d], buf["X"][d]
                        bx, by, bz = self.bank[2 + 3 * d], self.bank[3 + 3 * d], self.bank[4 + 3 * d]
                        up = "levlow" if d else "levup"
                        ml = c.pool(nc.gpsimd.tensor_tensor, LT[:, :, :], AT[:, :, :], lev(up, s), ALU.mult, after=[mAT[d], used[d]])
                        for t in range(NT):
                            m = c.products(bx[:, ch[t]], [(LT[:, t, :], M[:, t, :])], [ml, mM[d], mMT[d], mAT])
                        used[d] = m
                        mx = c.act(nc.scalar.copy, flat(X), bx[:, :], after=[m])
                        if s < LEVELS - 1:
                            for t in range(NT):
                                m = c.products(by[:, ch[t]], [(MT[:, t, :], X[:, t, :])], [mx])
                            my = m
                        for t in range(NT):
                            m = c.products(bz[:, ch[t]], [(X[:, t, :], MT[:, t, :])], [mx])
                        if s < LEVELS - 1:
                            mM[d] = c.dve(nc.vector.tensor_tensor, flat(M), flat(M), by[:, :], ALU.subtract, after=[my])
                        mMT[d] = c.dve(nc.vector.tensor_tensor, flat(MT), flat(MT), bz[:, :], ALU.subtract, after=[m])
                U, WT = buf["A"], buf["LT"]
                mu, mw = [None] * 2, [None] * 2
                for d in range(2):
                    bu, bw = self.bank[2 + 3 * d], self.bank[3 + 3 * d]
                    for t in range(NT):
                        m = c.products(bu[:, ch[t]], [(buf["MT"][d][:, t, :], buf["vb"][d][:, t, :])], [mMT[d], mvb[d]])
                    mu[d] = c.act(nc.scalar.copy, flat(U[d]), bu[:, :], after=[m])
                    for t in range(NT):
                        m = c.products(bw[:, ch[t]], [(buf["kbe"][d][:, t, :], buf["MT"][d][:, t, :])], [mMT[d], mvb[d]])
                    mw[d] = c.dve(nc.vector.tensor_copy, flat(WT[d]), bw[:, :], after=[m])
                mS, mo = [None] * 2, [None] * NT
                for n in range(NT):
                    for d in range(2):
                        t = NT - 1 - n if d else n
                        o = osum[:, t, :]
                        b1, b2, b3 = self.bank[4 * d], self.bank[1 + 4 * d], self.bank[2 + 4 * d]
                        if n == 0:
                            V, mv = U[d][:, t, :], mu[d]
                        else:
                            m = c.products(b1[:, 0:P], [(WT[d][:, t, :], S[d][:, :])], [mw, mS[d], mu, c.dve.mark()])
                            mv = c.dve(nc.vector.tensor_tensor, vn[d][:, :], U[d][:, t, :], b1[:, 0:P], ALU.subtract, after=[m, mS[d]])
                            V = vn[d][:, :]
                            mq = c.products(b2[:, 0:P], [(qT[:, ch[t]], S[d][:, :])], [mS[d]])
                        mi = c.products(b3[:, 0:P], [(buf["aT"][d][:, t, :], V)], [mv, maT[d], mw, mu, c.dve.mark()])
                        if mo[t] is None:
                            mo[t] = c.dve(nc.vector.tensor_copy, o, b3[:, 0:P], after=[mi, mz])
                        else:
                            mo[t] = c.dve(nc.vector.tensor_tensor, o, o, b3[:, 0:P], ALU.add, after=[mi, mo[t]])
                        if n > 0:
                            mo[t] = c.dve(nc.vector.scalar_tensor_tensor, o, b2[:, 0:P], hq[:, 2, t, d:d + 1], o,
                                          ALU.mult, ALU.add, after=[mq, mo[t]])
                        if n < NT - 1:
                            ms = c.products(b3[:, P:2 * P], [(buf["kdec"][d][:, t, :], V)], [mo[t]])
                            if n == 0:
                                mS[d] = c.dve(nc.vector.tensor_copy, S[d][:, :], b3[:, P:2 * P], after=[ms])
                            else:
                                mS[d] = c.dve(nc.vector.scalar_tensor_tensor, S[d][:, :], S[d][:, :], hq[:, 4, t, d:d + 1],
                                              b3[:, P:2 * P], ALU.mult, ALU.add, after=[ms])
                m = self.norm_blocks(osum, NT, lambda i: zt[:, i, :], sqt[:, 0, :].rearrange("p (t n) -> p t n", n=P), ss,
                                     eps[:, 0:1], [mo, mz])
                self.store_T(osum, 1, [self.bank[7]], h, [m])
                c.barrier()

    def diff(self, l):
        nc, c, A = self.nc, self.c, self.A
        with ExitStack() as es:
            sb = self.allocator(es)
            lp = sb("lambda_params", [P, 4, HD])
            lam = sb("lambda", [P, 4])
            gain = sb("diff_gain", [P, P])
            eps = sb("diff_eps", [P, 1])
            ld = c.dma((lp[:, :, :].rearrange("p a d -> p (a d)"), A["diff_lambda_2"][l].rearrange("a d -> (a d)").partition_broadcast(P)),
                       (gain[:, :], A["diff_norm_g_2"][l].partition_broadcast(P)), slow=True)
            c.dve(nc.vector.memset, eps[:, :], EPS)
            for i in range(2):
                m = c.dve(nc.vector.tensor_tensor, lp[:, 2 * i, :], lp[:, 2 * i, :], lp[:, 2 * i + 1, :], ALU.mult, after=[ld])
                m = c.dve(nc.vector.tensor_reduce, lam[:, i:i + 1], lp[:, 2 * i, :], AX.X, ALU.add, after=[m])
            m = c.act(nc.scalar.activation, lam[:, 0:2], lam[:, 0:2], ACT.Exp, after=[m])
            m = c.dve(nc.vector.tensor_tensor, lam[:, 2:3], lam[:, 0:1], lam[:, 1:2], ALU.subtract, after=[m])
            m = c.dve(nc.vector.tensor_tensor, lam[:, 2:3], lam[:, 2:3], self.k("lam")[:, bass.ds(l, 1)], ALU.add, after=[m])
            m = c.dve(nc.vector.tensor_copy, lam[:, 3:4], self.k("lam")[:, bass.ds(l + DEPTH, 1)])
            c.dve(nc.vector.tensor_scalar, gain[:, :], gain[:, :], lam[:, 3:4], None, ALU.mult, after=[m, ld])
            c.barrier()
            wq, wk, wv = [sb(n, [P, KD, P]) for n in ("wq", "wk", "wv")]
            qT, kT, rt = sb("qT", [P, T]), sb("kT", [P, T]), sb("rope_tmp", [P, T])
            v, y = sb("v_tok", [P, NT, P]), sb("y_tok", [P, NT, P])
            ss = sb("sum_sq", [P, 8])
            self.attention_buffers(es, 2)
            with nc.Fori(0, 4) as h:
                lq, lk, lv = [c.dma((w[:, :, :], cols_of(A["w_in_2"], l, h * P + C2[n], P)))
                              for w, n in ((wq, "b_q"), (wk, "b_k"), (wv, "b_v"))]
                m = self.proj_T(self.bank[0][:, :], wq, self.hT, [lq])
                m = c.act(nc.scalar.activation, qT[:, :], self.bank[0][:, :], ACT.Copy, scale=HD ** -0.5, after=[m])
                mq = self.rope(qT[:, :], rt[:, :], self.bank[2], self.k("rot2"), self.k("cos2"), self.k("sin2"), [m])
                m = self.proj_T(self.bank[1][:, :], wk, self.hT, [lk])
                m = c.act(nc.scalar.copy, kT[:, :], self.bank[1][:, :], after=[m])
                mk = self.rope(kT[:, :], rt[:, :], self.bank[3], self.k("rot2"), self.k("cos2"), self.k("sin2"), [m, mq])
                m = self.proj_tok([self.bank[6][:, i * P:(i + 1) * P] for i in range(NT)], wv, self.hT, [lv])
                mv = c.act(nc.scalar.copy, v[:, :, :].rearrange("p t n -> p (t n)"), self.bank[6][:, :], after=[m])

                def mix(p0, p1, rinv, marks):
                    m = c.dve(nc.vector.tensor_tensor, rinv[1], rinv[1], lam[:, 2:3], ALU.mult, after=marks)
                    m = c.dve(nc.vector.tensor_scalar, p1, p1, rinv[1], None, ALU.mult, after=[m])
                    return c.dve(nc.vector.scalar_tensor_tensor, p0, p0, rinv[0], p1, ALU.mult, ALU.subtract, after=[m])
                units = []
                for t in range(NT):
                    def out(o, rinv, marks, t=t):
                        return c.dve(nc.vector.tensor_copy, y[:, t, :], o, after=marks)
                    units.append(dict(maps=[(qT[HD * i:HD * i + HD, t * P:(t + 1) * P], kT[HD * i:HD * i + HD, :]) for i in range(2)],
                                      width=T, extra=[], decay=None, sink=None, mix=mix,
                                      values=[v[:, i, :] for i in range(NT)], out=out))
                self.attention(units, [mq, mk, mv])
                m = self.norm_blocks(y, NT, lambda i: gain[:, :], v, ss, eps[:, 0:1], [c.dve.mark(), c.pe.mark()])
                self.store_T(y, 1, [self.bank[7]], h + 4, [m])
                c.barrier()

    def swa(self, l):
        nc, c, A = self.nc, self.c, self.A
        with ExitStack() as es:
            sb = self.allocator(es)
            sinks = sb("sinks", [P, 8])
            wq, wk, wv = sb("wq", [P, KD, 2 * P]), sb("wk", [P, KD, 2, HD]), sb("wv", [P, KD, HD])
            qT = [sb(f"qT{i}", [P, T]) for i in range(2)]
            kT, rt = sb("kT", [P, T]), sb("rope_tmp", [P, T])
            v, y = sb("v_tok", [P, NT, HD]), sb("y_tok", [P, NT, 2 * P])
            sk, nsk = sb("group_sinks", [P, 4]), sb("group_sinks_neg", [P, 4])
            self.attention_buffers(es, 1)
            c.dma((sinks[:, :], A["swa_sink_2"][l].partition_broadcast(P)), slow=True)
            c.barrier()
            with nc.Fori(0, 2) as grp:
                lq = c.dma((wq[:, :, :], cols_of(A["w_in_2"], l, grp * 256 + C2["c_q"], 2 * P)))
                kd = cols_of(A["w_in_2"], l, grp * HD + C2["c_k"], HD)
                lk = c.dma((wk[:, :, 0, :], kd), (wk[:, :, 1, :], kd))
                lv = c.dma((wv[:, :, :], cols_of(A["w_in_2"], l, grp * HD + C2["c_v"], HD)))
                m = c.dve(nc.vector.tensor_copy, sk[:, :], sinks[:, bass.ds(grp * 4, 4)])
                ms = c.dve(nc.vector.tensor_scalar, nsk[:, :], sk[:, :], -1.0, None, ALU.mult, after=[m])
                ready = [ms]
                for i in range(2):
                    m = self.proj_T(self.bank[i][:, :], wq[:, :, i * P:(i + 1) * P], self.hT, [lq])
                    m = c.act(nc.scalar.activation, qT[i][:, :], self.bank[i][:, :], ACT.Copy, scale=HD ** -0.5, after=[m])
                    ready.append(self.rope(qT[i][:, :], rt[:, :], self.bank[4 + i], self.k("rot2"), self.k("cos2"),
                                           self.k("sin2"), [m, ready[:]]))
                m = self.proj_T(self.bank[2][:, :], wk[:, :, :, :].rearrange("p k r d -> p k (r d)"), self.hT, [lk])
                m = c.act(nc.scalar.copy, kT[:, :], self.bank[2][:, :], after=[m])
                ready.append(self.rope(kT[:, :], rt[:, :], self.bank[6], self.k("rot2"), self.k("cos2"),
                                       self.k("sin2"), [m, ready[:]]))
                m = self.proj_tok([self.bank[3][:, i * HD:(i + 1) * HD] for i in range(NT)], wv, self.hT, [lv])
                mv = c.act(nc.scalar.copy, v[:, :, :].rearrange("p t n -> p (t n)"), self.bank[3][:, 0:NT * HD], after=[m])
                units = []
                for h in range(4):
                    r = slice(HD * (h % 2), HD * (h % 2) + HD)
                    for t in range(NT):
                        lo, hi = max(t - 1, 0), min(t + 2, NT)
                        extra = [(self.k("ident"), self.k("far"), 0, P)] if t > 0 else []
                        extra += [(self.k("ident"), self.k("later"), (hi - lo - 1) * P, P)] if t < NT - 1 else []

                        def out(o, rinv, marks, h=h, t=t):
                            return c.dve(nc.vector.tensor_scalar, y[:, t, h * HD:(h + 1) * HD], o, rinv, None, ALU.mult, after=marks)
                        units.append(dict(maps=[(qT[h // 2][r, t * P:(t + 1) * P], kT[r, lo * P:hi * P])], width=(hi - lo) * P,
                                          extra=extra, decay=None, sink=sk[:, h:h + 1], nsink=nsk[:, h:h + 1], mix=None,
                                          values=[v[:, i, :] for i in range(lo, hi)], out=out))
                self.attention(units, [ready, mv])
                self.store_T(y, 2, [self.bank[6], self.bank[7]], grp * 2 + 8, [c.dve.mark()])
                c.barrier()

    def mlstm(self, l):
        nc, c, A = self.nc, self.c, self.A
        with ExitStack() as es:
            sb = self.allocator(es)
            wif = sb("w_if", [P, KD, 16])
            bias = sb("gate_bias", [P, 16])
            gi, gf, tmp = [sb(n, [P, NT, 8]) for n in ("log_i", "log_f", "log_f_tmp")]
            gain = sb("mlstm_gain", [P, P])
            eps = sb("mlstm_eps", [P, 1])
            R = sb("R_wide", [P, 8, T])
            cols = sb("r_and_exp_m", [P, 2, NT, 8])
            ir, fr, Br, rr, Rr = [[sb(f"{n}{d}", [4, T]) for d in range(2)] for n in ("i_rows", "f_rows", "B_rows", "r_rows", "R_rows")]
            ld = c.dma((wif[:, :, :], cols_of(A["w_in_2"], l, C2["d_if"], 16)),
                       (bias[:, :], A["mlstm_gate_b_2"][l].rearrange("a d h -> (a d h)").partition_broadcast(P)),
                       (gain[:, :], A["mlstm_norm_g_2"][l].partition_broadcast(P)), slow=True)
            c.dve(nc.vector.memset, eps[:, :], EPS)
            b = self.bank[0]
            m = self.proj_tok([b[:, 16 * i:16 * i + 16] for i in range(NT)], wif, self.hT, [ld])
            z = b[:, 0:64].rearrange("p (t n) -> p t n", n=16)
            mi = c.dve(nc.vector.tensor_tensor, gi[:, :, :], z[:, :, 0:8], bias[:, 0:8].unsqueeze(1).to_broadcast([P, NT, 8]), ALU.add, after=[m])
            m = c.dve(nc.vector.tensor_tensor, gf[:, :, :], z[:, :, 8:16], bias[:, 8:16].unsqueeze(1).to_broadcast([P, NT, 8]), ALU.add, after=[m])
            mf = self.log_sigmoid(gf[:, :, :], tmp[:, :, :], [m])
            for d in range(2):
                hs = slice(4 * d, 4 * d + 4)
                m1 = self.to_rows(ir[d][:, :], gi[:, :, hs], self.bank[1], [mi, c.dve.mark()])
                m2 = self.to_rows(fr[d][:, :], gf[:, :, hs], self.bank[2], [mf, c.dve.mark()])
                m2 = self.scan_rows(Br[d][:, :], fr[d][:, :], self.k("onesrow", 4), ALU.add, d, [m2])
                m1 = c.dve(nc.vector.tensor_tensor, rr[d][:, :], ir[d][:, :], Br[d][:, :], ALU.subtract, after=[m1, m2])
                mR = self.scan_rows(Rr[d][:, :], rr[d][:, :], self.k("onesrow", 4), ALU.max, d, [m1])
                m2 = c.dve(nc.vector.tensor_tensor, Br[d][:, :], Br[d][:, :], Rr[d][:, :], ALU.add, after=[mR])
                self.to_cols(cols[:, 0, :, hs], rr[d][:, :], self.bank[3], [m1, c.dve.mark()])
                m2 = self.to_cols(cols[:, 1, :, hs], Br[d][:, :], self.bank[4], [m2, c.dve.mark()])
                for h in range(4):
                    bb = self.bank[5 + h % 2]
                    m = self.spread(bb, h, Rr[d][:, :], after=[mR, c.act.mark()])
                    c.act(nc.scalar.copy, R[:, 4 * d + h, :], bb[:, :], after=[m])
            c.act(nc.scalar.activation, cols[:, 1, :, :], cols[:, 1, :, :], ACT.Exp, scale=-1.0, after=[m2])
            c.barrier()
            wq, wk = [sb(n, [P, KD, P]) for n in ("wq", "wk")]
            wv, wo = [sb(n, [P, KD, 2 * P]) for n in ("wv", "wo")]
            qT, kT = sb("qT", [P, T]), sb("kT", [P, T])
            V = P + 1
            va = sb("v_and_one", [P, NT, 2, V])
            og, y = sb("o_gate", [P, NT, 2, P]), sb("y_tok", [P, NT, 2, P])
            pc = sb("pair_cols", [P, 2, NT, 2, 2])
            pR = sb("pair_R", [P, 2, 2, T])
            WT = [[sb(f"weights{i}_{d}", [P, NT, T]) for d in range(2)] for i in range(1)]
            den = sb("den", [P, 2, 2, NT])
            ss = sb("sum_sq", [P, 8])
            with nc.Fori(0, 2) as pair:
                lq, lk = [c.dma((w[:, :, :], cols_of(A["w_in_2"], l, pair * P + C2[n], P))) for w, n in ((wq, "d_q"), (wk, "d_k"))]
                lv, lo = [c.dma((w[:, :, :], cols_of(A["w_in_2"], l, pair * 256 + C2[n], 2 * P))) for w, n in ((wv, "d_v"), (wo, "d_o"))]
                mc = []
                for i in range(2):
                    for d in range(2):
                        mc.append(c.dve(nc.vector.tensor_copy, pc[:, i, :, d, :], cols[:, i, :, bass.ds(pair * 2 + 4 * d, 2)]))
                for d in range(2):
                    mc.append(c.pool(nc.gpsimd.tensor_copy, pR[:, d, :, :], R[:, bass.ds(pair * 2 + 4 * d, 2), :]))
                m1 = c.dve(nc.vector.memset, va[:, :, :, P:V], 1.0)
                m = self.proj_T(self.bank[0][:, :], wq, self.hT, [lq])
                mq = c.act(nc.scalar.copy, qT[:, :], self.bank[0][:, :], after=[m])
                m = self.proj_T(self.bank[1][:, :], wk, self.hT, [lk])
                mk = c.act(nc.scalar.activation, kT[:, :], self.bank[1][:, :], ACT.Copy, scale=HD ** -0.5, after=[m])
                mv = [m1]
                for i in range(2):
                    bv, bo = self.bank[2 + i], self.bank[4 + i]
                    m = self.proj_tok([bv[:, j * 256:(j + 1) * 256] for j in range(2)], wv, self.hT[:, :, i * 256:(i + 1) * 256], [lv])
                    mv.append(c.act(nc.scalar.copy, va[:, 2 * i:2 * i + 2, :, 0:P], bv[:, :].rearrange("p (t h n) -> p t h n", t=2, h=2), after=[m]))
                    m = self.proj_tok([bo[:, j * 256:(j + 1) * 256] for j in range(2)], wo, self.hT[:, :, i * 256:(i + 1) * 256], [lo])
                    g = og[:, 2 * i:2 * i + 2, :, :].rearrange("p t h n -> p (t h n)")
                    mo = self.sigmoid(g, bo[:, :], [m])
                mo = c.pool(nc.gpsimd.tensor_tensor, og[:, :, :, :].rearrange("p t h n -> p (t h) n"),
                            og[:, :, :, :].rearrange("p t h n -> p (t h) n"),
                            gain[:, :].unsqueeze(1).to_broadcast([P, 2 * NT, P]), ALU.mult, after=[mo])
                used, my = [None, None], None
                free = [[mv, mo]] * 4
                fs = [[mq], [mk]]
                for h in range(2):
                    r = slice(HD * h, HD * h + HD)
                    mw = [[None] * NT for _ in range(2)]
                    for j in range(NT):
                        bs = self.bank[j % 2]
                        m = c.products(bs[:, :], [(kT[r, j * P:(j + 1) * P], qT[r, :])], [mq, mk, fs[j % 2]])
                        for d in range(2):
                            rng = slice(0, (j + 1) * P) if d else slice(j * P, T)
                            w = WT[0][d][:, j, rng]
                            diag = WT[0][d][:, j, j * P:(j + 1) * P]
                            a = c.dve(nc.vector.tensor_scalar, w, pR[:, d, h, rng], pc[:, 0, j, d, h:h + 1], 0.0,
                                      ALU.subtract, ALU.max, after=[mc, used[d]])
                            a = c.act(nc.scalar.activation, w, w, ACT.Exp, scale=-1.0, after=[a])
                            a = c.pool(nc.gpsimd.tensor_tensor, diag, diag, self.k("low" if d else "up"), ALU.mult, after=[a])
                            mw[d][j] = c.dve(nc.vector.tensor_tensor, w, w, bs[:, rng], ALU.mult, after=[a, m])
                        fs[j % 2] = [mw[0][j], mw[1][j]]
                    for d in range(2):
                        mo2 = []
                        for t in range(NT):
                            bo = self.bank[2 + 2 * d + t // 2]
                            js = range(t, NT) if d else range(0, t + 1)
                            m = c.products(bo[:, (t % 2) * V:(t % 2) * V + V],
                                           [(WT[0][d][:, j, t * P:(t + 1) * P], va[:, j, h, :]) for j in js],
                                           [mw[d], mv, free[2 * d + t // 2], free[2 * d + t // 2]])
                            mo2.append(m)
                        used[d] = m
                        dn = den[:, d, h, :]
                        for i in range(2):
                            bo = self.bank[2 + 2 * d + i]
                            mm = c.act(nc.scalar.activation, dn[:, 2 * i:2 * i + 2],
                                       bo[:, 0:2 * V].rearrange("p (t v) -> p t v", v=V)[:, :, P], ACT.Abs, after=[m])
                        mm = c.dve(nc.vector.tensor_tensor, dn, dn, pc[:, 1, :, d, h], ALU.max, after=[mm, mc])
                        mm = c.dve(nc.vector.reciprocal, dn, dn, after=[mm])
                        for t in range(NT):
                            bo = self.bank[2 + 2 * d + t // 2]
                            num = bo[:, (t % 2) * V:(t % 2) * V + P]
                            if d == 0:
                                my = c.dve(nc.vector.tensor_scalar, y[:, t, h, :], num, dn[:, t:t + 1], None, ALU.mult, after=[mm])
                            else:
                                my = c.dve(nc.vector.scalar_tensor_tensor, y[:, t, h, :], num, dn[:, t:t + 1], y[:, t, h, :],
                                           ALU.mult, ALU.add, after=[mm, my])
                            free[2 * d + t // 2] = my
                fold = lambda x: x[:, :, :, :].rearrange("p t h n -> p (t h) n")
                m = self.norm_blocks(fold(y), 2 * NT, lambda i: fold(og)[:, i, :], pR[:, :, :, :].rearrange("p d h (a n) -> p (d h a) n", n=P),
                                     ss, eps[:, 0:1], [my, mo])
                self.store_T(y[:, :, :, :].rearrange("p t h n -> p t (h n)"), 2, [self.bank[6], self.bank[7]], pair * 2 + 12, [m])
                c.barrier()

    def gate_branches(self, l, mT):
        nc, c, A = self.nc, self.c, self.A
        B = 4
        with ExitStack() as es:
            wg = [self.allocator(es)(f"w_gate{s}", [P, KD, P]) for s in range(B)]
            wb = [self.allocator(es)(f"w_branch{s}", [P, 4, P]) for s in range(B)]
            sg = [self.allocator(es)(f"gate{s}", [P, T]) for s in range(B)]
            self.prime(B)
            with nc.Fori(0, KD) as e:
                acc = mT[:, bass.ds(e, 1), :].rearrange("p a t -> p (a t)")
                for s in range(B):
                    nc.sync.wait_ge(c.mm[s], e + 1)
                    nc.sync.dma_start(wg[s][:, :, :], A["w_gate_2"][l, :, s, bass.ds(e * P, P)].rearrange("(k p) n -> p k n", p=P)).then_inc(c.ld[s], 16)
                    nc.sync.dma_start(wb[s][:, :, :], A["w_branch_2"][l, s, :, bass.ds(e * P, P)].rearrange("(k p) n -> p k n", p=P)).then_inc(c.ld[s], 16)
                    nc.tensor.wait_ge(c.ld[s], e * 32 + 32)
                    nc.tensor.wait_ge(c.ev[s], e + 1)
                    gb, bb = self.bank[s], self.bank[4 + s]
                    for k in range(KD):
                        nc.tensor.matmul(gb[:, :], wg[s][:, k, :], self.hT[:, k, :], start=k == 0, stop=k == KD - 1)
                    for k in range(4):
                        m = nc.tensor.matmul(bb[:, :], wb[s][:, k, :], self.yT[:, 4 * s + k, :], start=k == 0, stop=k == 3)
                    m.then_inc(c.mm[s], 1)
                    nc.scalar.wait_ge(c.mm[s], e + 2)
                    nc.scalar.wait_ge(c.ev[s], e + 1)
                    nc.scalar.activation(sg[s][:, :], gb[:, :], ACT.Tanh, scale=0.5).then_inc(c.mid[s], 1)
                    nc.vector.wait_ge(c.mid[s], e + 1)
                    nc.vector.scalar_tensor_tensor(sg[s][:, :], sg[s][:, :], 1.0, bb[:, :], ALU.add, ALU.mult).then_inc(c.own, 1)
                    nc.vector.wait_ge(c.own, e * B + s + 1)
                    if s == 0:
                        m = nc.vector.tensor_scalar(acc, sg[s][:, :], 0.5, None, ALU.mult)
                    else:
                        nc.vector.wait_ge(c.ev[s - 1], e + 2)
                        m = nc.vector.scalar_tensor_tensor(acc, sg[s][:, :], 0.5, acc, ALU.mult, ALU.add)
                    m.then_inc(c.ev[s], 1)
            c.barrier()

    def mlp(self, l):
        nc, c, A = self.nc, self.c, self.A
        F = 4 * KD
        S = 4
        with ExitStack() as es:
            up = self.allocator(es)("mlp_hidden", [P, F, T])
            with ExitStack() as ws:
                w = [self.allocator(ws)(f"w_up{s}", [P, KD, P]) for s in range(S)]
                tmp = [self.allocator(ws)(f"relu{s}", [P, T]) for s in range(S)]
                self.prime(S)
                with nc.Fori(0, F // S) as i:
                    for s in range(S):
                        f = i * S + s
                        nc.sync.wait_ge(c.mm[s], i + 1)
                        nc.sync.dma_start(w[s][:, :, :], cols_of(A["w_mlp1_2"], l, f * P, P)).then_inc(c.ld[s], 16)
                        nc.tensor.wait_ge(c.ld[s], i * 16 + 16)
                        nc.tensor.wait_ge(c.ev[s], i + 1)
                        for k in range(KD):
                            m = nc.tensor.matmul(self.bank[s][:, :], w[s][:, k, :], self.hT[:, k, :], start=k == 0, stop=k == KD - 1)
                        m.then_inc(c.mm[s], 1)
                        nc.scalar.wait_ge(c.mm[s], i + 2)
                        nc.scalar.wait_ge(c.ev[s], i + 1)
                        nc.scalar.activation(tmp[s][:, :], self.bank[s][:, :], ACT.Relu).then_inc(c.mid[s], 1)
                        nc.vector.wait_ge(c.mid[s], i + 1)
                        nc.vector.tensor_tensor(up[:, bass.ds(f, 1), :].rearrange("p a t -> p (a t)"), tmp[s][:, :],
                                                self.bank[s][:, :], ALU.mult).then_inc(c.ev[s], 1)
                c.barrier()
            self.stream_add(lambda e: cols_of(A["w_mlp2_2"], l, e * P, P), up, F)

    def second_block(self):
        nc, A = self.nc, self.A
        with nc.Fori(0, DEPTH) as l:
            self.norm(self.hT, A["norm1_g_2"][l])
            self.gdn(l)
            self.diff(l)
            self.swa(l)
            self.mlstm(l)
            with ExitStack() as es:
                mT = self.allocator(es)("mixed", [P, KD, T])
                self.gate_branches(l, mT)
                self.stream_add(lambda e: cols_of(A["w_out_2"], l, e * P, P), mT, KD)
            self.norm(self.hT, A["norm2_g_2"][l])
            self.mlp(l)
        self.norm(self.xT, A["final_norm_g_2"])


def build(nc, A, table, out):
    cols, _ = constants()
    p = Program(nc, A, out, table, cols)
    p.load_x(A["x"][0])
    p.first_block()
    p.second_block()
    p.store(out[0], p.xT)


NAMES = ["x", "norm_g", "w_in", "fox_b", "conv_w", "conv_b", "conv_ln_g", "conv_ln_b", "conv_pw", "cmp_pe_k",
         "cmp_pe_v", "cmp_k_w1", "cmp_k_w2", "cmp_v_w1", "cmp_v_w2", "w_out", "final_g", "norm1_g_2", "w_in_2",
         "gdn_conv_w_2", "gdn_a_log_2", "gdn_dt_bias_2", "gdn_norm_g_2", "diff_lambda_2", "diff_norm_g_2",
         "swa_sink_2", "mlstm_gate_b_2", "mlstm_norm_g_2", "w_branch_2", "w_gate_2", "w_out_2", "norm2_g_2",
         "w_mlp1_2", "w_mlp2_2", "final_norm_g_2"]


def kernel(**inputs):
    import concourse.bacc as bacc
    from concourse.bass_utils import run_bass_kernel_spmd

    nc = bacc.Bacc("TRN2", target_bir_lowering=False, num_devices=1)
    arrays, A = {}, {}
    for name in NAMES:
        arrays["in_" + name] = np.ascontiguousarray(inputs[name])
        A[name] = nc.dram_tensor("in_" + name, arrays["in_" + name].shape, F32, kind="ExternalInput").ap()
    arrays["table"] = constants()[1]
    table = nc.dram_tensor("table", arrays["table"].shape, F32, kind="ExternalInput").ap()
    out = nc.dram_tensor("out", (1, T, D), F32, kind="ExternalOutput").ap()
    build(nc, A, table, out)
    r = run_bass_kernel_spmd(nc, [arrays], core_ids=[0])
    return r.results[0]["out"]
```

```python
import numpy as np
from contextlib import ExitStack

import concourse.bass as bass
from concourse import mybir

F32 = mybir.dt.float32
F32R = mybir.dt.float32r
ACT = mybir.ActivationFunctionType
ALU = mybir.AluOpType
AX = mybir.AxisListType
ET = mybir.EngineType

P = 128
T = 512
NT = T // P
D = 1024
KD = D // P
DEPTH = 2
EPS = 1e-6
NEG = -1e30
HD = 64

FOX_W, CONV_CH, TAPS, CMP_LEN, CMP_STRIDE = 256, 256, 31, 32, 16
N_CMP = (T - CMP_LEN) // CMP_STRIDE + 1
C1 = {}
_at = 0
for _name, _size in (("fq", 256), ("fk", 256), ("fv", 256), ("ff", 4), ("fg", 256), ("glu", 512), ("cg", 256),
                     ("nq", 512), ("nkc", 128), ("nvc", 128), ("nks", 128), ("nvs", 128), ("nkw", 128),
                     ("nvw", 128), ("ngl", 24), ("ng", 512)):
    C1[_name] = _at
    _at += _size
C1_WIDTH = _at
C2 = {}
_at = 0
for _name, _size in (("a_qkv", 1536), ("a_z", 512), ("a_ab", 16), ("b_q", 512), ("b_k", 512), ("b_v", 512),
                     ("c_q", 512), ("c_k", 128), ("c_v", 128), ("d_q", 256), ("d_k", 256), ("d_v", 512),
                     ("d_if", 16), ("d_o", 512)):
    C2[_name] = _at
    _at += _size

C2_WIDTH = _at

LEVELS = 7


GROUPS = {"all": ("ident", "nident", "later", "far", "up", "low", "ones", "onesrow"),
          "nsa": ("cos1", "sin1", "rot1", "cosc", "sinc", "cmpneg", "cmpone"),
          "rope": ("cos2", "sin2", "rot2", "lam"),
          "gdn": ("levlow", "levup", "sup", "slow", "carryf", "carryb")}


def constants():
    f = np.float32
    i = np.arange(P)[:, None]
    j = np.arange(P)[None, :]
    out = {}
    out["ident"] = (i == j)
    out["nident"] = -(i == j).astype(f)
    out["later"] = np.where(j > i, NEG, 0.0)
    out["far"] = np.where(j < i, NEG, 0.0)
    out["up"] = (j >= i)
    out["low"] = (j <= i)
    out["sup"] = (j > i)
    out["slow"] = (j < i)
    out["ones"] = np.ones((P, P))
    low = [((i // (2 << s)) == (j // (2 << s))) & (i % (2 << s) >= (1 << s)) & (j % (2 << s) < (1 << s))
           for s in range(LEVELS)]
    out["levlow"] = np.concatenate(low, 1)
    out["levup"] = np.concatenate([m.T for m in low], 1)

    def rope(theta, dim, pos):
        half = dim // 2
        inv = (f(theta) ** (-np.arange(0, dim, 2, dtype=f) / f(dim))).astype(f)
        ang = pos.astype(f)[:, None] * inv[None, :]
        cos = np.ones((P, len(pos)), f)
        sin = np.zeros((P, len(pos)), f)
        rot = np.zeros((P, P), f)
        for p in range(P):
            d = p % HD
            if d < dim:
                cos[p], sin[p] = np.cos(ang[:, d % half]), np.sin(ang[:, d % half])
                if d < half:
                    rot[p + half, p] = -1.0
                else:
                    rot[p - half, p] = 1.0
        return cos, sin, rot

    ends = np.arange(N_CMP) * CMP_STRIDE + CMP_LEN - 1
    out["cos1"], out["sin1"], out["rot1"] = rope(500000.0, 16, np.arange(T))
    out["cosc"], out["sinc"], _ = rope(500000.0, 16, ends)
    out["cos2"], out["sin2"], out["rot2"] = rope(10000.0, 64, np.arange(T))
    tq = np.arange(NT)[None, :, None] * P + np.arange(P)[:, None, None]
    seen = ends[None, None, :] <= tq
    out["cmpneg"] = np.where(seen, 0.0, NEG).reshape(P, -1)
    out["cmpone"] = seen.reshape(P, -1)
    t = np.arange(T)[None, :]
    out["carryf"] = np.repeat(t % P != 0, P, 0)
    out["carryb"] = np.repeat(t % P != P - 1, P, 0)
    out["onesrow"] = np.ones((P, T))
    lam = 0.8 - 0.6 * np.exp(-0.3 * np.arange(DEPTH))
    out["lam"] = np.repeat(np.concatenate([lam, 1 - lam])[None, :], P, 0)
    cols, at, parts = {}, 0, []
    for group, names in GROUPS.items():
        first, cols[group] = at, {}
        for name in names:
            a = np.ascontiguousarray(out[name], f)
            cols[group][name] = (at - first, at - first + a.shape[1])
            at += a.shape[1]
            parts.append(a)
        cols[group][""] = (first, at)
    return cols, np.concatenate(parts, 1)


class Queue:

    def __init__(self, eng, sem):
        self.eng, self.sem = eng, sem
        self.fresh()

    def fresh(self):
        self.n, self.seen = 0, {}

    def wait(self, *marks):
        for m in marks:
            if m is None:
                continue
            if isinstance(m, list):
                self.wait(*m)
            elif self.seen.get(m[0], 0) < m[1]:
                self.eng.wait_ge(m[0], m[1])
                self.seen[m[0]] = m[1]

    def __call__(self, instr, *args, after=(), **kw):
        self.wait(*after)
        instr(*args, **kw).then_inc(self.sem, 1)
        self.n += 1
        return (self.sem, self.n)

    def mark(self):
        return (self.sem, self.n)


class Core:

    N_DMA = 40

    def __init__(self, nc):
        self.nc = nc
        names = ["pe", "dve", "act", "pool"] + [f"dma{i}" for i in range(self.N_DMA)]
        self.sems = [nc.alloc_semaphore(n) for n in names]
        self.pe = Queue(nc.tensor, self.sems[0])
        self.dve = Queue(nc.vector, self.sems[1])
        self.act = Queue(nc.scalar, self.sems[2])
        self.pool = Queue(nc.gpsimd, self.sems[3])
        self.sp = Queue(nc.sync, None)
        self.used = 0
        self.ld, self.hi, self.lo, self.mm, self.mid, self.fin, self.ev, self.st = [
            [nc.alloc_semaphore(f"{n}{i}") for i in range(4)] for n in ("ld", "hi", "lo", "mm", "mid", "fin", "ev", "st")]
        self.own = nc.alloc_semaphore("own")
        self.zeroed = range(self.sems[0].num, self.own.num + 1)
        self.barrier()

    def barrier(self):
        for i in range(self.used):
            self.sp.wait((self.sems[4 + i], self.total[i]))
        self.nc.multi_engine_barrier([ET.SP, ET.PE, ET.DVE, ET.Activation, ET.Pool], sems_to_clear=self.zeroed)
        for q in (self.pe, self.dve, self.act, self.pool, self.sp):
            q.fresh()
        self.used, self.total = 0, []

    def dma(self, *pairs, after=(), slow=False, on=None):
        q = on or self.sp
        q.wait(*after)
        sem = self.sems[4 + self.used]
        for out, in_ in pairs:
            q.eng.dma_start(out, in_, allow_slow_non_contiguous=slow).then_inc(sem, 16)
        self.used += 1
        self.total.append(16 * len(pairs))
        return (sem, 16 * len(pairs))

    def products(self, out, terms, after=()):
        self.pe.wait(*after)
        for n, (l, r) in enumerate(terms):
            m = self.nc.tensor.matmul(out, l, r, start=n == 0, stop=n == len(terms) - 1)
        m.then_inc(self.pe.sem, 1)
        self.pe.n += 1
        return self.pe.mark()

    def transposes(self, pairs, ident, after=()):
        self.pe.wait(*after)
        for out, in_ in pairs:
            m = self.nc.tensor.transpose(out, in_, ident[0:in_.shape[0], 0:in_.shape[0]])
        m.then_inc(self.pe.sem, 1)
        self.pe.n += 1
        return self.pe.mark()


def cols_of(w, l, c, n):
    return w[l, :, bass.ds(c, n)].rearrange("(k p) n -> p k n", p=P)


class Program:
    def __init__(self, nc, A, out, C, cols):
        self.nc, self.A, self.out, self.cols = nc, A, out, cols
        self.stage = 0
        self.c = Core(nc)
        sb = nc.alloc_sbuf_tensor
        self.tables, self.place, self.lows = {}, {}, {}
        self.xT = sb("xT", [P, KD, T], F32)
        self.hH = sb("hH", [P, KD, T], F32R)
        self.hL = sb("hL", [P, KD, T], F32R)
        self.yT = self.note(sb("yT", [P, 16, T], F32))
        self.rstd = sb("rstd", [P, T], F32)
        self.one_pass = sb("one_pass_tables", [P, 4, P], F32R)
        self.z1 = nc.dram_tensor("z1", [C1_WIDTH, T], F32, kind="Internal").ap()
        self.z2 = nc.dram_tensor("z2", [C2_WIDTH, T], F32, kind="Internal").ap()
        self.rows = nc.dram_tensor("rows", [8, T], F32, kind="Internal").ap()
        self.bank = [nc.alloc_psum_tensor(f"bank{i}", [P, T], F32) for i in range(8)]
        self.tables_dram = C
        self.resident = sb("tables", [P, cols["all"][""][1]], F32)

    def allocator(self, stack):
        self.stage += 1
        n = self.stage

        def sb(name, shape, dt=F32):
            return self.note(stack.enter_context(self.nc.sbuf_tensor(f"{name}_{n}", shape, dt)))
        return sb

    def note(self, t):
        self.place[t.name] = self.nc.sbuf_base - 4 * int(np.prod(t.shape[1:]))
        return t

    def low(self, t):
        if t.name not in self.lows:
            self.lows[t.name] = self.nc.alloc_sbuf_tensor_at(f"{t.name}_low", list(t.shape), F32R, offset=self.place[t.name])
        return self.lows[t.name]

    def row(self, h):
        return self.rows[bass.ds(h, 1), :].rearrange("a t -> (a t)").partition_broadcast(P)

    def r(self, name):
        return self.one_pass[:, ("ident", "nident", "later", "far").index(name), :]

    def k(self, name, rows=P):
        return self.tables[name][0:rows, :]

    def load_tables(self, group, dst):
        first, end = self.cols[group][""]
        for name, (a, b) in self.cols[group].items():
            if name:
                self.tables[name] = dst[:, a:b]
        return self.c.dma((dst[:, 0:end - first], self.tables_dram[:, first:end]))

    def group_width(self, group):
        first, end = self.cols[group][""]
        return end - first

    def split(self, hi, lo, x, after=(), high=None, low=None):
        nc, c = self.nc, self.c
        m = c.act(nc.scalar.copy, hi, x, after=after)
        return [m, (low or c.dve)((nc.gpsimd if low is c.pool else nc.vector).tensor_tensor, lo, x, hi.bitcast(F32),
                                  ALU.subtract, after=[m, *after])]

    def norm(self, dst, g_dram):
        nc, c = self.nc, self.c
        with ExitStack() as es:
            sq = self.allocator(es)("sq", [P, KD, T])
            g = self.allocator(es)("norm_gain", [P, KD])
            eps = self.allocator(es)("norm_eps", [P, 1])
            lg = c.dma((g[:, :], g_dram.rearrange("(k p) -> p k", p=P)), slow=True)
            me = c.dve(nc.vector.memset, eps[:, :], EPS)
            terms = []
            for k in range(KD):
                m = c.act(nc.scalar.activation, sq[:, k, :], self.xT[:, k, :], ACT.Square)
                terms.append((self.k("ones"), sq[:, k, :]))
            m = c.products(self.bank[0][:, :], terms, after=[m])
            m = c.act(nc.scalar.activation, self.rstd[:, :], self.bank[0][:, :], ACT.Ln,
                      bias=eps[:, 0:1], scale=1.0 / D, after=[m, me])
            m = c.act(nc.scalar.activation, self.rstd[:, :], self.rstd[:, :], ACT.Exp, scale=-0.5, after=[m])
            for k in range(KD):
                if dst is not None:
                    c.dve(nc.vector.scalar_tensor_tensor, dst[:, k, :], self.xT[:, k, :], g[:, k:k + 1],
                          self.rstd[:, :], ALU.mult, ALU.mult, after=[m, lg])
                else:
                    mk = c.dve(nc.vector.scalar_tensor_tensor, sq[:, k, :], self.xT[:, k, :], g[:, k:k + 1],
                               self.rstd[:, :], ALU.mult, ALU.mult, after=[m, lg])
                    self.split(self.hH[:, k, :], self.hL[:, k, :], sq[:, k, :], [mk])
            c.barrier()

    def twice(self, dst, src):
        return (dst[0:HD, :], src), (dst[HD:P, :], src)

    def stack(self, x, hi, scale, after):
        nc, c = self.nc, self.c
        m = c.act(nc.scalar.activation, hi[:, :], x[:, :], ACT.Copy, scale=scale, after=after)
        return c.dve(nc.vector.scalar_tensor_tensor, hi[HD:P, :], x[HD:P, :], scale, hi[HD:P, :].bitcast(F32),
                     ALU.mult, ALU.subtract, after=[m])

    def to_tokens(self, dst, src, bank, after, n=P):
        m = self.c.transposes([(bank[:, t * n:(t + 1) * n], src[:, t * P:(t + 1) * P]) for t in range(NT)],
                              self.k("ident"), after)
        return self.c.act(self.nc.scalar.copy, dst, bank[:, 0:NT * n].rearrange("p (t n) -> p t n", n=n), after=[m])

    def log_sigmoid(self, x, tmp, after, negate=False):
        nc, c = self.nc, self.c
        m = c.act(nc.scalar.activation, tmp, x, ACT.Abs, after=after)
        m = c.act(nc.scalar.activation, tmp, tmp, ACT.Exp, scale=-1.0, after=[m])
        m = c.act(nc.scalar.activation, tmp, tmp, ACT.Ln, bias=1.0, after=[m])
        return c.dve(nc.vector.scalar_tensor_tensor, x, x, 0.0, tmp, ALU.min, ALU.subtract, after=[m])

    def silu(self, out, x, tmp, after, half=0.5):
        nc, c = self.nc, self.c
        m = c.act(nc.scalar.activation, tmp, x, ACT.Tanh, scale=0.5, after=after)
        m = c.dve(nc.vector.scalar_tensor_tensor, out, tmp, 1.0, x, ALU.add, ALU.mult, after=[m])
        return c.dve(nc.vector.tensor_scalar, out, out, half, None, ALU.mult, after=[m])

    def sigmoid(self, out, x, after):
        nc, c = self.nc, self.c
        m = c.act(nc.scalar.activation, out, x, ACT.Tanh, scale=0.5, after=after)
        return c.dve(nc.vector.tensor_scalar, out, out, 0.5, 0.5, ALU.mult, ALU.add, after=[m])

    def rope(self, x, tmp, bank, rot, cos, sin, after):
        nc, c = self.nc, self.c
        n = x.shape[-1]
        mr = c.products(bank[:, 0:n], [(rot, x)], after)
        ms = c.dve(nc.vector.tensor_tensor, tmp, bank[:, 0:n], sin, ALU.mult, after=[mr])
        mc = c.pool(nc.gpsimd.tensor_tensor, x, x, cos, ALU.mult, after=[mr])
        return c.dve(nc.vector.tensor_tensor, x, x, tmp, ALU.add, after=[ms, mc])

    def attention_buffers(self, es, maps):
        sb = self.allocator(es)
        self.scores = [self.bank[0], self.bank[1], self.bank[2]]
        self.ptp = [self.bank[3], self.bank[6]]
        self.obanks = [self.bank[4], self.bank[5]]
        self.prob = [[sb(f"prob{i}_{m}", [P, T]) for m in range(maps)] for i in range(3)]
        self.pt = [sb(f"prob_T{i}", [P, T]) for i in range(2)]
        self.stat = sb("softmax_stat", [P, 32, maps, 4])
        self.shifted = [sb(f"shifted{i}", [P, T]) for i in range(2)]

    def attention(self, units, ready):
        nc, c = self.nc, self.c
        N = len(units)
        assert N <= 32
        c.dve.wait(ready)
        S_free, P_free, PT_free, O_free, shift_free = [None] * 3, [None] * 3, [None] * 2, [None] * 2, [None] * 2
        expd, scaled, transposed, PT_ready, valued = {}, {}, {}, {}, {}
        calls = 0
        for step in range(N + 3):
            if step < N:
                u, ring = units[step], step % 3
                W = u["width"]
                expd[step] = []
                for m, (q, kk) in enumerate(u["maps"]):
                    b = calls % 3
                    sh = calls % 2
                    calls += 1
                    S = self.scores[b]
                    c.pe.wait(ready, S_free[b])
                    terms = [(q, kk[0], 0, W), (q, kk[1], 0, W)] + u["extra"]
                    for n, (l, r, o, w) in enumerate(terms):
                        mm = nc.tensor.matmul(S[:, o:o + w], l, r, start=n == 0, stop=n == len(terms) - 1,
                                              skip_group_check=True)
                    mm.then_inc(c.pe.sem, 1)
                    c.pe.n += 1
                    ms = c.pe.mark()
                    nmax, rsum = self.stat[:, step, m, 0:1], self.stat[:, step, m, 1:2]
                    Pm = self.prob[ring][m][:, 0:W]
                    if u["decay"] is not None:
                        x = self.shifted[sh][:, 0:W]
                        mx = c.dve(nc.vector.tensor_tensor_reduce, out=x, in0=S[:, 0:W],
                                   in1=u["decay"][:, 0:W], scale=1.0, scalar=3e38, op0=ALU.add, op1=ALU.min,
                                   accum_out=nmax, after=[ms, shift_free[sh]])
                        S_free[b] = mx
                        me = c.act(nc.scalar.activation, Pm, x, ACT.Exp, bias=nmax, scale=-1.0,
                                   accum_out=rsum, after=[mx, P_free[ring]])
                        shift_free[sh] = me
                    else:
                        mx = c.dve(nc.vector.tensor_reduce, nmax, S[:, 0:W], AX.X, ALU.max, negate=True, after=[ms])
                        if u["sink"] is not None:
                            mx = c.dve(nc.vector.tensor_scalar, nmax, nmax, u["sink"][1], None, ALU.min, after=[mx])
                        me = c.act(nc.scalar.activation, Pm, S[:, 0:W], ACT.Exp, bias=nmax, scale=1.0,
                                   accum_out=rsum, after=[mx, P_free[ring]])
                        S_free[b] = me
                        if u["sink"] is not None:
                            me = [me, c.act(nc.scalar.activation, self.stat[:, step, m, 3:4], u["sink"][0], ACT.Exp,
                                            bias=nmax, scale=1.0)]
                    expd[step].append(me)
            if 2 <= step < N + 2:
                n = step - 2
                u, ring, s = units[n], n % 3, n % 2
                W = u["width"]
                done = []
                for m in range(len(u["maps"])):
                    rsum, scale = self.stat[:, n, m, 1:2], self.stat[:, n, m, 2:3]
                    mr = expd[n][m]
                    if u["sink"] is not None:
                        mr = c.dve(nc.vector.tensor_tensor, rsum, rsum, self.stat[:, n, m, 3:4], ALU.add, after=[mr])
                    mr = c.dve(nc.vector.reciprocal, scale, rsum, after=[mr])
                    if u["coef"] is not None:
                        mr = c.dve(nc.vector.tensor_tensor, scale, scale, u["coef"], ALU.mult, after=[mr])
                    done.append(mr)
                before = expd[n]
                if u["mix"] is not None:
                    before = [u["mix"](self.prob[ring][0][:, 0:W], self.prob[ring][1][:, 0:W],
                                       [self.stat[:, n, m, 2:3] for m in range(2)], done)]
                scaled[n] = done
                mt = c.transposes([(self.ptp[s][:, i * P:(i + 1) * P], self.prob[ring][0][:, i * P:(i + 1) * P])
                                   for i in range(W // P)], self.k("ident"), after=[before, PT_free[s]])
                P_free[ring] = mt
                if n % 2:
                    PT_ready[n] = c.act(nc.scalar.copy, self.pt[s][:, 0:W], self.ptp[s][:, 0:W], after=[mt, valued.get(n - 2)])
                else:
                    PT_ready[n] = c.dve(nc.vector.tensor_copy, self.pt[s][:, 0:W], self.ptp[s][:, 0:W], after=[mt, valued.get(n - 2)])
                PT_free[s] = PT_ready[n]
            if step >= 3:
                n = step - 3
                u, s = units[n], n % 2
                o = self.obanks[s][:, 0:u["values"][0].shape[-1]]
                valued[n] = c.products(o, [(self.pt[s][:, i * P:(i + 1) * P], v) for i, v in enumerate(u["values"])],
                                       after=[PT_ready[n], O_free[s]])
                O_free[s] = u["out"](o, self.stat[:, n, 0, 2:3], [valued[n], scaled[n]])

    def store_T(self, y, n, banks, first, after):
        nc, c = self.nc, self.c
        free = [None] * len(banks)
        for j in range(n):
            b = j % len(banks)
            m = c.transposes([(banks[b][:, t * P:(t + 1) * P], y[:, t, j * P:(j + 1) * P]) for t in range(NT)],
                             self.k("ident"), after=[after, free[b]])
            free[b] = c.dve(nc.vector.tensor_copy, self.yT[:, bass.ds(first + j, 1), :].rearrange("p a t -> p (a t)"),
                            banks[b][:, :], after=[m])

    def fox(self, l):
        nc, c, A = self.nc, self.c, self.A
        with ExitStack() as es:
            sb = self.allocator(es)
            fb = sb("fox_bias", [4, 1])
            f, tmp, crow = sb("f_rows", [4, T]), sb("f_tmp", [4, T]), sb("c_rows", [4, T])
            q2, k2 = [[sb(f"{n}_twice{h}", [P, T]) for h in range(2)] for n in "qk"]
            qs, kh = [[sb(f"{n}{h}", [P, T], F32R) for h in range(2)] for n in ("q_stacked", "k_hi")]
            vf, gf = sb("v_rows", [P, T]), sb("gate_rows", [P, T])
            v, g, gt, y = [sb(n, [P, NT, P]) for n in ("v_tok", "gate", "gate_tmp", "y_tok")]
            cpair = sb("c_pair", [P, 2, T])
            self.attention_buffers(es, 1)
            ld = c.dma((f[:, :], self.z1[C1["ff"]:C1["ff"] + 4, :]), (fb[:, :], A["fox_b"][l].unsqueeze(1)), slow=True)
            m = c.dve(nc.vector.tensor_scalar, f[:, :], f[:, :], fb[:, 0:1], None, ALU.add, after=[ld])
            m = self.log_sigmoid(f[:, :], tmp[:, :], [m])
            m = c.dve(nc.vector.tensor_tensor_scan, crow[:, :], self.k("onesrow", 4), f[:, :], 0.0, ALU.mult, ALU.add, after=[m])
            c.dma((self.rows[0:4, :], crow[:, :]), after=[m])
            c.barrier()
            z = self.z1
            with nc.Fori(0, 2) as pair:
                lq, lk = [[c.dma(*self.twice(x[h], z[bass.ds(pair * P + C1[n] + h * HD, HD), :])) for h in range(2)]
                          for x, n in ((q2, "fq"), (k2, "fk"))]
                lc = [c.dma((cpair[:, h, :], self.row(pair * 2 + h))) for h in range(2)]
                lv, lg = [c.dma((x[:, :], z[bass.ds(pair * P + C1[n], P), :])) for x, n in ((vf, "fv"), (gf, "fg"))]
                ready = []
                for h in range(2):
                    ready.append(self.split(kh[h][:, :], self.low(k2[h])[:, :], k2[h][:, :], [lk[h]]))
                    ready.append(self.stack(q2[h], qs[h], -HD ** -0.5, [lq[h]]))
                mv = self.to_tokens(v[:, :, :], vf, self.bank[6], [lv])
                m = c.transposes([(self.bank[7][:, t * P:(t + 1) * P], gf[:, t * P:(t + 1) * P]) for t in range(NT)],
                                 self.k("ident"), [lg])
                fl = lambda x: x[:, :, :].rearrange("p t n -> p (t n)")
                mg = self.silu(fl(g), self.bank[7][:, :], fl(gt), [m])
                units = []
                for h in range(2):
                    for t in range(NT):
                        def out(o, rinv, marks, t=t, cs=slice(h * HD, h * HD + HD)):
                            return c.dve(nc.vector.scalar_tensor_tensor, y[:, t, cs], o, rinv, g[:, t, cs],
                                         ALU.mult, ALU.mult, after=[*marks, mg])
                        W = (t + 1) * P
                        units.append(dict(
                            maps=[(qs[h][:, t * P:(t + 1) * P], (kh[h][:, 0:W], self.low(k2[h])[:, 0:W]))], width=W,
                            extra=[(self.r("nident"), self.r("later"), t * P, P)], decay=cpair[:, h, :],
                            sink=None, coef=None, mix=None,
                            values=[v[:, i, h * HD:h * HD + HD] for i in range(t + 1)], out=out))
                self.attention(units, [ready, mv, mg, lc])
                self.store_T(y, 1, [self.bank[6]], pair, [c.dve.mark()])
                c.barrier()

    def conv(self, l):
        nc, c, A = self.nc, self.c, self.A
        CT = CONV_CH // P
        PAD = TAPS - 1
        with ExitStack() as es:
            sb = self.allocator(es)
            za, zb, zg = [sb(n, [P, CT, T]) for n in ("glu_a", "glu_b", "conv_gate_rows")]
            wp = sb("w_pointwise", [P, CT, CONV_CH])
            taps = sb("taps", [P, TAPS, CT])
            small = sb("conv_params", [P, 3, CT])
            eps = sb("conv_eps", [P, 1])
            gl = sb("glu_padded", [P, CT, PAD + T])
            acc = sb("conv_acc", [P, CT, T])
            sq = sb("conv_sq", [P, CT, T])
            mean, rstd = sb("conv_mean", [P, T]), sb("conv_rstd", [P, T])
            gate, gtmp, y = [sb(n, [P, NT, CONV_CH]) for n in ("conv_gate", "conv_gate_tmp", "conv_y")]
            lw = [c.dma((x[:, :, :], self.z1[C1[n] + o:C1[n] + o + CONV_CH, :].rearrange("(j p) t -> p j t", p=P)))
                  for x, n, o in ((za, "glu", 0), (zb, "glu", CONV_CH), (zg, "cg", 0))]
            lp = c.dma((wp[:, :, :], A["conv_pw"][l].rearrange("(k p) n -> p k n", p=P)))
            lt = c.dma(*[(taps[:, :, j], A["conv_w"][l, :, j * P:(j + 1) * P].rearrange("w p -> p w")) for j in range(CT)],
                       *[(small[:, n, :], A[name][l].rearrange("(j p) -> p j", p=P))
                         for n, name in enumerate(("conv_b", "conv_ln_g", "conv_ln_b"))], slow=True)
            mz = [c.dve(nc.vector.memset, gl[:, :, 0:PAD], 0.0), c.dve(nc.vector.memset, eps[:, :], EPS)]
            ready = []
            for j in range(CT):
                m = c.act(nc.scalar.activation, sq[:, j, :], zb[:, j, :], ACT.Tanh, scale=0.5, after=[lw[1]])
                m = c.dve(nc.vector.tensor_scalar, sq[:, j, :], sq[:, j, :], 0.5, 0.5, ALU.mult, ALU.add, after=[m])
                ready.append(c.dve(nc.vector.tensor_tensor, gl[:, j, PAD:], sq[:, j, :], za[:, j, :], ALU.mult, after=[m, lw[0]]))
            for i in range(NT):
                bg = self.bank[4 + i // 2]
                m = c.transposes([(bg[:, (i % 2) * 256 + j * P:(i % 2) * 256 + (j + 1) * P], zg[:, j, i * P:(i + 1) * P])
                                  for j in range(CT)], self.k("ident"), [lw[2]])
            mt = [c.act(nc.scalar.activation, gtmp[:, 2 * i:2 * i + 2, :].rearrange("p a n -> p (a n)"),
                        self.bank[4 + i][:, :], ACT.Tanh, scale=0.5, after=[m]) for i in range(2)]
            marks = [[ready[j], mz, lt] for j in range(CT)]
            for w in range(TAPS):
                for j in range(CT):
                    src = gl[:, j, w:w + T]
                    if w == 0:
                        marks[j] = [c.dve(nc.vector.tensor_scalar, acc[:, j, :], src, taps[:, w, j:j + 1],
                                          small[:, 0, j:j + 1], ALU.mult, ALU.add, after=marks[j])]
                    else:
                        marks[j] = [c.dve(nc.vector.scalar_tensor_tensor, acc[:, j, :], src, taps[:, w, j:j + 1],
                                          acc[:, j, :], ALU.mult, ALU.add, after=marks[j])]
            for i in range(2):
                mg = c.dve(nc.vector.scalar_tensor_tensor, gate[:, 2 * i:2 * i + 2, :].rearrange("p a n -> p (a n)"),
                           gtmp[:, 2 * i:2 * i + 2, :].rearrange("p a n -> p (a n)"), 1.0, self.bank[4 + i][:, :],
                           ALU.add, ALU.mult, after=mt)
            m = c.products(self.bank[0][:, :], [(self.k("ones"), acc[:, j, :]) for j in range(CT)], marks)
            mm = c.act(nc.scalar.activation, mean[:, :], self.bank[0][:, :], ACT.Copy, scale=1.0 / CONV_CH, after=[m])
            md = [c.dve(nc.vector.tensor_tensor, acc[:, j, :], acc[:, j, :], mean[:, :], ALU.subtract, after=[mm])
                  for j in range(CT)]
            m = [c.act(nc.scalar.activation, sq[:, j, :], acc[:, j, :], ACT.Square, after=[md[j]]) for j in range(CT)]
            m = c.products(self.bank[1][:, :], [(self.k("ones"), sq[:, j, :]) for j in range(CT)], m)
            m = c.act(nc.scalar.activation, rstd[:, :], self.bank[1][:, :], ACT.Ln, bias=eps[:, 0:1],
                      scale=1.0 / CONV_CH, after=[m])
            m = c.act(nc.scalar.activation, rstd[:, :], rstd[:, :], ACT.Exp, scale=-0.5, after=[m])
            ms = []
            for j in range(CT):
                a = c.dve(nc.vector.scalar_tensor_tensor, acc[:, j, :], acc[:, j, :], small[:, 1, j:j + 1], rstd[:, :],
                          ALU.mult, ALU.mult, after=[m])
                a = c.dve(nc.vector.tensor_scalar, acc[:, j, :], acc[:, j, :], small[:, 2, j:j + 1], None, ALU.add, after=[a])
                a = self.silu(acc[:, j, :], acc[:, j, :], sq[:, j, :], [a])
                ms.append(a)
            for i in range(NT):
                m = c.products(self.bank[2 + i // 2][:, (i % 2) * 256:(i % 2) * 256 + 256],
                               [(acc[:, j, i * P:(i + 1) * P], wp[:, j, :]) for j in range(CT)], [ms, lp])
            for i in range(NT):
                md = c.dve(nc.vector.scalar_tensor_tensor, y[:, i, :], self.bank[2 + i // 2][:, (i % 2) * 256:(i % 2) * 256 + 256],
                          0.5, gate[:, i, :], ALU.mult, ALU.mult, after=[m, mg])
            for j in range(CT):
                b = self.bank[6 + j]
                mt = c.transposes([(b[:, t * P:(t + 1) * P], y[:, t, j * P:(j + 1) * P]) for t in range(NT)],
                                  self.k("ident"), after=[md])
                c.dve(nc.vector.tensor_copy, self.yT[:, FOX_W // P + j, :], b[:, :], after=[mt])
            c.barrier()

    def compress(self, l, kcmp, vcmp, table):
        nc, c, A = self.nc, self.c, self.A
        M = CMP_LEN // 2
        N = N_CMP
        with ExitStack() as es:
            sb = self.allocator(es)
            w1 = [sb(f"cmp_w1_{i}", [P, M, 256]) for i in range(2)]
            w2 = [sb(f"cmp_w2_{i}", [P, 2, 2, HD]) for i in range(2)]
            pe = [sb(f"cmp_pe{i}", [P, M]) for i in range(2)]
            two = sb("two_tokens", [P, 4, T])
            kc = sb("k_cmp_full", [P, 2, N + 1])
            blk = sb("cmp_blocks", [P, M, 2, N])
            hid, cube, hidT = sb("hid", [P, 2, 2 * N]), sb("cube", [P, 2, 2 * N]), sb("hid_gelu", [P, 2, 2 * N])
            rtmp = sb("cmp_rope_tmp", [P, 2, N])
            loads = []
            for i, (col, kv) in enumerate((("nkc", "k"), ("nvc", "v"))):
                la = c.dma(*[(two[r * HD:(r + 1) * HD, 2 * i + g, 0:T - r], self.z1[C1[col] + g * HD:C1[col] + (g + 1) * HD, r:T])
                             for g in range(2) for r in range(2)])
                lb = c.dma((w1[i][:, :, :], A[f"cmp_{kv}_w1"][l].rearrange("(m p) h -> p m h", p=P)))
                w2d = A[f"cmp_{kv}_w2"][l].rearrange("(j p) o -> p j o", p=P)
                lc = c.dma((w2[i][:, :, 0, :], w2d), (w2[i][:, :, 1, :], w2d),
                           (pe[i][0:HD, :], A[f"cmp_pe_{kv}"][l].rearrange("(m r) d -> r d m", r=2)[0]),
                           (pe[i][HD:P, :], A[f"cmp_pe_{kv}"][l].rearrange("(m r) d -> r d m", r=2)[1]), slow=True)
                loads.append((la, lb, lc))
            used, usedh = None, None
            for i in range(2):
                la, lb, lc = loads[i]
                mb = []
                for g in range(2):
                    for q in range(CMP_LEN // CMP_STRIDE):
                        h = M // 2
                        src = two[:, 2 * i + g, CMP_STRIDE * q:CMP_STRIDE * q + CMP_STRIDE * N].rearrange(
                            "p (n m r) -> p m n r", m=h, r=2)[:, :, :, 0]
                        m2 = c.dve(nc.vector.tensor_tensor, blk[:, q * h:(q + 1) * h, g, :], src,
                                   pe[i][:, q * h:(q + 1) * h].unsqueeze(2).to_broadcast([P, h, N]), ALU.add,
                                   after=[la, lc, used])
                    mb.append(m2)
                bh = self.bank[2 + i]
                for j in range(2):
                    m = c.products(bh[:, j * 2 * N:(j + 1) * 2 * N],
                                   [(w1[i][:, q, j * P:(j + 1) * P], blk[:, q, :, :].rearrange("p g n -> p (g n)"))
                                    for q in range(M)], [lb, mb])
                used = m
                x = bh[:, 0:4 * N].rearrange("p (j n) -> p j n", j=2)
                m = c.act(nc.scalar.activation, cube[:, :, :], x, ACT.Square, after=[m, usedh])
                m = c.dve(nc.vector.tensor_scalar, cube[:, :, :], cube[:, :, :], 0.044715, 1.0, ALU.mult, ALU.add, after=[m])
                m = c.dve(nc.vector.tensor_tensor, cube[:, :, :], cube[:, :, :], x, ALU.mult, after=[m])
                m = c.act(nc.scalar.activation, hid[:, :, :], cube[:, :, :], ACT.Tanh,
                          scale=float(np.sqrt(2 / np.pi)), after=[m])
                m = c.dve(nc.vector.scalar_tensor_tensor, hidT[:, :, :], hid[:, :, :], 1.0, x, ALU.add, ALU.mult,
                          after=[m, usedh])
                m = c.dve(nc.vector.tensor_scalar, hidT[:, :, :], hidT[:, :, :], 0.5, None, ALU.mult, after=[m])
                if i == 0:
                    m = c.products(self.bank[4][:, 0:2 * N],
                                   [(w2[i][:, j, :, :].rearrange("p r d -> p (r d)"), hidT[:, j, :]) for j in range(2)], [m, lc])
                    usedh = m
                    mz = c.dve(nc.vector.memset, kc[:, :, N:N + 1], 0.0)
                    mk = c.act(nc.scalar.copy, kc[:, :, 0:N], self.bank[4][:, 0:2 * N].rearrange("p (g n) -> p g n", g=2), after=[m])
                    for g in range(2):
                        mr = self.rope(kc[:, g, 0:N], rtmp[:, g, :], self.bank[5 + g], self.k("rot1"), self.k("cosc"),
                                       self.k("sinc"), [mk, table])
                        self.split(kcmp[0][:, g, :], kcmp[1][:, g, :], kc[:, g, :], [mr, mz])
                else:
                    for g in range(2):
                        m2 = c.products(self.bank[7][0:N, g * HD:(g + 1) * HD],
                                        [(hidT[:, j, g * N:(g + 1) * N], w2[i][:, j, 0, :]) for j in range(2)], [m, lc])
                    c.act(nc.scalar.copy, vcmp[:, :, :].rearrange("p g d -> p (g d)"), self.bank[7][0:N, 0:2 * HD], after=[m2])
            c.barrier()

    def nsa(self, l):
        nc, c, A = self.nc, self.c, self.A
        N = N_CMP
        H = 4
        with ExitStack() as es:
            sb = self.allocator(es)
            table = self.load_tables("nsa", sb("nsa_tables", [P, self.group_width("nsa")]))
            kcmp = [sb(f"k_cmp_{n}", [P, 2, N + 1], F32R) for n in ("hi", "lo")]
            vcmp = sb("v_cmp", [N, 2, HD])
            self.compress(l, kcmp, vcmp, table)
            gl = sb("branch_gates", [P, NT, 24])
            glr = sb("branch_gate_rows", [24, T])
            q2 = [sb(f"q_twice{h}", [P, T]) for h in range(H)]
            k2 = [sb(f"k_twice{b}", [P, T]) for b in range(2)]
            qs = [sb(f"q_stacked{h}", [P, T], F32R) for h in range(H)]
            kh = [sb(f"k_hi{b}", [P, T], F32R) for b in range(2)]
            rt = [sb(f"rope_tmp{i}", [P, T]) for i in range(2)]
            vf, gf = sb("v_rows", [P, T]), [sb(f"gate_rows{i}", [P, T]) for i in range(2)]
            v = sb("v_tok", [P, NT, 2 * HD])
            gate, y = sb("gate", [P, NT, 2, P]), sb("y_tok", [P, NT, 2 * P])
            gtmp = sb("gate_tmp", [P, NT, P])
            kc = [sb(f"k_cmp_group{i}", [P, N + 1], F32R) for i in range(2)]
            vc, gg = sb("v_cmp_group", [N, HD]), sb("gates_group", [P, NT, 12])
            pc, pcT = sb("p_cmp", [P, H, NT * N]), [sb(f"p_cmpT{i}", [N, NT, P]) for i in range(2)]
            cst = sb("cmp_stat", [P, 3, H, NT])
            coef = sb("coef", [P, H, NT])
            self.attention_buffers(es, 1)
            z = self.z1
            ld = c.dma((glr[:, :], z[C1["ngl"]:C1["ngl"] + 24, :]))
            m = self.to_tokens(gl[:, :, :], glr, self.bank[0], [ld], 24)
            self.sigmoid(gl[:, :, :], gl[:, :, :], [m])
            c.barrier()
            with nc.Fori(0, 2) as grp:
                lk = [c.dma(*self.twice(k2[i], z[bass.ds(grp * HD + C1[n], HD), :])) for i, n in enumerate(("nks", "nkw"))]
                lq = [c.dma(*self.twice(q2[h], z[bass.ds(grp * 256 + C1["nq"] + h * HD, HD), :])) for h in range(H)]
                lv = c.dma((vf[0:HD, :], z[bass.ds(grp * HD + C1["nvs"], HD), :]), (vf[HD:P, :], z[bass.ds(grp * HD + C1["nvw"], HD), :]))
                lg = [c.dma((gf[i][:, :], z[bass.ds(grp * 256 + C1["ng"] + i * P, P), :])) for i in range(2)]
                one = lambda x: x[:, bass.ds(grp, 1), :].rearrange("p a n -> p (a n)")
                mg1 = [c.dve(nc.vector.tensor_copy, kc[0][:, :], one(kcmp[0])),
                       c.dve(nc.vector.tensor_copy, kc[1][:, :], one(kcmp[1])),
                       c.dve(nc.vector.tensor_copy, vc[:, :], one(vcmp)),
                       c.dve(nc.vector.tensor_copy, gg[:, :, :], gl[:, :, bass.ds(grp * 12, 12)])]
                rot = (self.k("rot1"), self.k("cos1"), self.k("sin1"))
                ready, tmp_free = [], [None, None]
                n = 0
                for i in range(2):
                    m = self.rope(k2[i][:, :], rt[n % 2][:, :], self.bank[n % 2], *rot, [lk[i], tmp_free[n % 2]])
                    tmp_free[n % 2] = m
                    ready.append(self.split(kh[i][:, :], self.low(k2[i])[:, :], k2[i][:, :], [m]))
                    n += 1
                for h in range(H):
                    m = self.rope(q2[h][:, :], rt[n % 2][:, :], self.bank[n % 2], *rot, [lq[h], tmp_free[n % 2]])
                    tmp_free[n % 2] = m
                    ready.append(self.stack(q2[h], qs[h], HD ** -0.5, [m]))
                    n += 1
                mv = self.to_tokens(v[:, :, :], vf, self.bank[6], [lv])
                mg = None
                for i in range(2):
                    m = c.transposes([(self.bank[7][:, t * P:(t + 1) * P], gf[i][:, t * P:(t + 1) * P]) for t in range(NT)],
                                     self.k("ident"), [lg[i], mg])
                    mg = self.silu(gate[:, :, i, :], self.bank[7][:, :].rearrange("p (t n) -> p t n", n=P), gtmp[:, :, :], [m])
                for h in range(H):
                    for t in range(NT):
                        at = (h * NT + t) * (N + 1)
                        m = c.products(self.bank[0][:, at:at + N + 1], [(qs[h][:, t * P:(t + 1) * P], kc[0][:, :]),
                                                                    (qs[h][:, t * P:(t + 1) * P], kc[1][:, :])], [ready, mg1])
                neg, one = self.k("cmpneg").rearrange("p (t n) -> p t n", n=N).unsqueeze(1), self.k("cmpone").unsqueeze(1)
                wide = [P, H, NT * N]
                m = c.dve(nc.vector.tensor_tensor, pc[:, :, :].rearrange("p h (t n) -> p h t n", n=N),
                          self.bank[0][:, :].rearrange("p (h t n) -> p h t n", h=H, t=NT)[:, :, :, 0:N],
                          neg.to_broadcast([P, H, NT, N]), ALU.add, after=[m])
                p4 = pc[:, :, :].rearrange("p h (t n) -> p (h t) n", n=N)
                st = [cst[:, i, :, :].rearrange("p h t -> p (h t)") for i in range(3)]
                m = c.dve(nc.vector.tensor_reduce, st[0], p4, AX.X, ALU.max, after=[m])
                m = c.dve(nc.vector.tensor_tensor, p4, p4, st[0].unsqueeze(2).to_broadcast([P, H * NT, N]), ALU.subtract, after=[m])
                m = c.act(nc.scalar.activation, p4, p4, ACT.Exp, after=[m])
                m = c.dve(nc.vector.tensor_reduce, st[1], p4, AX.X, ALU.add, after=[m])
                mi = c.dve(nc.vector.reciprocal, st[2], st[1], after=[m])
                mp = c.dve(nc.vector.tensor_tensor, pc[:, :, :], pc[:, :, :], one.to_broadcast(wide), ALU.mult, after=[m])
                mf = c.dve(nc.vector.tensor_tensor, coef[:, :, :], gg[:, :, :].rearrange("p t (h b) -> p h t b", b=3)[:, :, :, 0],
                           cst[:, 2, :, :], ALU.mult, after=[mi, mg1])
                mc = [None, None]
                for h in range(H):
                    bt, bv, pT = self.bank[1 + h % 2], self.bank[4 + h % 2], pcT[h % 2]
                    m = c.transposes([(bt[0:N, t * P:(t + 1) * P], pc[:, h, t * N:(t + 1) * N]) for t in range(NT)],
                                     self.k("ident"), after=[mp, mc[h % 2]])
                    m = c.act(nc.scalar.copy, pT[:, :, :].rearrange("p t n -> p (t n)"), bt[0:N, :], after=[m])
                    for t in range(NT):
                        m2 = c.products(bv[:, t * HD:(t + 1) * HD], [(pT[:, t, :], vc[:, :])], [m, mg1])
                    mc[h % 2] = c.dve(nc.vector.tensor_tensor, y[:, :, h * HD:(h + 1) * HD],
                                      bv[:, 0:NT * HD].rearrange("p (t d) -> p t d", d=HD),
                                      coef[:, h, :].unsqueeze(2).to_broadcast([P, NT, HD]), ALU.mult, after=[m2, mf])
                cmp_done = mc
                units = []
                n = 0
                for br in range(2):
                    for h in range(H):
                        for t in range(NT):
                            W = (t + 1) * P

                            def out(o, scale, marks, h=h, t=t):
                                w = y[:, t, h * HD:(h + 1) * HD]
                                return c.dve(nc.vector.scalar_tensor_tensor, w, o, scale, w, ALU.mult, ALU.add, after=marks)
                            units.append(dict(
                                maps=[(qs[h][:, t * P:(t + 1) * P], (kh[br][:, 0:W], self.low(k2[br])[:, 0:W]))], width=W,
                                extra=[(self.r("ident"), self.r("later"), t * P, P)], decay=None, sink=None,
                                coef=gg[:, t, 3 * h + 1 + br:3 * h + 2 + br], mix=None,
                                values=[v[:, i, br * HD:(br + 1) * HD] for i in range(t + 1)], out=out))
                self.attention(units, [ready, mv, mg, cmp_done])
                m = c.dve(nc.vector.tensor_tensor, y[:, :, :], y[:, :, :], gate[:, :, :, :].rearrange("p t i n -> p t (i n)"),
                          ALU.mult, after=[c.dve.mark()])
                self.store_T(y, 2, [self.bank[6], self.bank[7]], grp * 2 + 4, [m])
                c.barrier()

    def stream(self, sb, trips, slots, parts, kt, load, products, drain, tail=()):
        nc, c = self.nc, self.c
        w = [sb(f"w{s}", [P, kt, P]) for s in range(slots)]
        wh = [sb(f"w_hi{s}", [P, kt, P], F32R) for s in range(slots)]
        for s in range(slots):
            nc.tensor.sem_inc(c.mm[s], 1)
            nc.vector.sem_inc(c.ev[s], 1)

        def fetch(i, s, width=P):
            nc.sync.wait_ge(c.mm[s], i + 1)
            for out, in_ in load(i, s, w[s], width):
                nc.sync.dma_start(out, in_).then_inc(c.ld[s], 16)

        def split(i, s, width=P):
            nc.scalar.wait_ge(c.ld[s], i * (16 * parts) + 16 * parts)
            nc.scalar.copy(wh[s][:, :, 0:width], w[s][:, :, 0:width]).then_inc(c.hi[s], 1)
            nc.vector.wait_ge(c.hi[s], i + 1)
            nc.vector.tensor_tensor(self.low(w[s])[:, :, 0:width], w[s][:, :, 0:width],
                                    wh[s][:, :, 0:width].bitcast(F32), ALU.subtract).then_inc(c.lo[s], 1)

        def multiply(i, s, width=P):
            nc.tensor.wait_ge(c.lo[s], i + 1)
            nc.tensor.wait_ge(c.ev[s], i + 1)
            products(s, wh[s], self.low(w[s])[:, :, :], width).then_inc(c.mm[s], 1)

        tiles = [(trips - 1, s, P) for s in range(slots)] + [(trips + j // slots, j % slots, wd) for j, wd in enumerate(tail)]
        fetch(0, 0)
        split(0, 0)
        with nc.Fori(0, trips - 1) as i:
            for s in range(slots):
                nxt = (i, s + 1) if s + 1 < slots else (i + 1, 0)
                fetch(*nxt)
                split(*nxt)
                multiply(i, s)
                drain(i, s, i * slots + s, P)
        for n, (i, s, wd) in enumerate(tiles):
            if n + 1 < len(tiles):
                fetch(*tiles[n + 1])
                split(*tiles[n + 1])
            multiply(i, s, wd)
            drain(i, s, i * slots + s, wd)

    def three_passes(self, bank, width, terms):
        nc = self.nc
        for n, (wh, wl, xh, xl) in enumerate(terms):
            nc.tensor.matmul(bank[0:width, :], wh, xh, start=n == 0, stop=False)
            nc.tensor.matmul(bank[0:width, :], wh, xl, start=False, stop=False)
            m = nc.tensor.matmul(bank[0:width, :], wl, xh, start=False, stop=n == len(terms) - 1)
        return m

    def in_projection(self, l, w_in, n, z):
        nc, c = self.nc, self.c
        S = 4
        full = n // P
        trips = full // S
        tail = [P] * (full - trips * S) + [n % P]
        with ExitStack() as es:
            sb = self.allocator(es)
            zt = [sb(f"z_tile{s}", [P, T]) for s in range(S)]

            def products(s, wh, wl, width):
                return self.three_passes(self.bank[s], width, [
                    (wh[:, k, 0:width], wl[:, k, 0:width], self.hH[:, k, :], self.hL[:, k, :]) for k in range(KD)])

            def load(i, s, out, width):
                return [(out[:, :, 0:width], w_in[l, :, bass.ds(i * (S * P) + s * P, width)].rearrange("(k p) n -> p k n", p=P))]

            def drain(i, s, tile, width):
                nc.scalar.wait_ge(c.mm[s], i + 2)
                nc.scalar.wait_ge(c.st[s], i * 16 + 1)
                nc.scalar.copy(zt[s][0:width, :], self.bank[s][0:width, :]).then_inc(c.ev[s], 1)
                nc.scalar.wait_ge(c.ev[s], i + 2)
                nc.scalar.dma_start(z[bass.ds(tile * P, width), :], zt[s][0:width, :]).then_inc(c.st[s], 16)

            for s in range(S):
                nc.gpsimd.sem_inc(c.st[s], 1)
            self.stream(sb, trips, S, 1, KD, load, products, drain, tail)
            for s in range(S):
                stored = trips + sum(1 for j in range(len(tail)) if j % S == s)
                nc.gpsimd.wait_ge(c.st[s], 16 * stored + 1)
            c.barrier()

    def stream_add(self, load_cols, xh, xl, kt):
        nc, c = self.nc, self.c
        with ExitStack() as es:
            sb = self.allocator(es)

            def load(i, s, out, width):
                return [(out[:, :, :], load_cols(i * 2 + s))]

            def products(s, wh, wl, width):
                return self.three_passes(self.bank[s], P, [(wh[:, k, :], wl[:, k, :], xh[:, k, :], xl[:, k, :]) for k in range(kt)])

            def drain(i, s, tile, width):
                nc.vector.wait_ge(c.mm[s], i + 2)
                x = self.xT[:, bass.ds(tile, 1), :].rearrange("p a t -> p (a t)")
                nc.vector.tensor_tensor(x, x, self.bank[s][:, :], ALU.add).then_inc(c.ev[s], 1)
            self.stream(sb, KD // 2, 2, 1, kt, load, products, drain)
            c.barrier()

    def split_y(self, sb, n):
        yh = sb("y_hi", [P, n, T], F32R)
        yl = self.low(self.yT)[:, :, :]
        return yh, yl, [self.split(yh[:, j, :], yl[:, j, :], self.yT[:, j, :]) for j in range(n)]

    def load_x(self, x):
        nc, c = self.nc, self.c
        with ExitStack() as es:
            xt = self.allocator(es)("x_tok", [P, NT, D])
            lc = self.load_tables("all", self.resident)
            for name in ("ident", "nident", "later", "far"):
                c.dve(nc.vector.tensor_copy, self.r(name), self.k(name), after=[lc])
            lx = c.dma((xt[:, :, :], x.rearrange("(t p) d -> p t d", p=P)))
            for k in range(KD):
                m = c.transposes([(self.bank[k][:, t * P:(t + 1) * P], xt[:, t, k * P:(k + 1) * P]) for t in range(NT)],
                                 self.k("ident"), after=[lc, lx])
                c.dve(nc.vector.tensor_copy, self.xT[:, k, :], self.bank[k][:, :], after=[m])
            c.barrier()

    def store(self, out, src):
        nc, c = self.nc, self.c
        with ExitStack() as es:
            xt = self.allocator(es)("x_tok", [P, NT, D])
            for k in range(KD):
                m = c.transposes([(self.bank[k][:, t * P:(t + 1) * P], src[:, k, t * P:(t + 1) * P]) for t in range(NT)],
                                 self.k("ident"))
                for t in range(NT):
                    m2 = c.dve(nc.vector.tensor_copy, xt[:, t, k * P:(k + 1) * P], self.bank[k][:, t * P:(t + 1) * P], after=[m])
            c.dma((out.rearrange("(t p) d -> p t d", p=P), xt[:, :, :]), after=[m2])
            c.barrier()

    def first_block(self):
        A = self.A
        with self.nc.Fori(0, DEPTH) as l:
            self.norm(None, A["norm_g"][l])
            self.in_projection(l, A["w_in"], C1_WIDTH, self.z1)
            self.fox(l)
            self.conv(l)
            self.nsa(l)
            with ExitStack() as es:
                yh, yl, _ = self.split_y(self.allocator(es), KD)
                self.c.barrier()
                self.stream_add(lambda e: cols_of(A["w_out"], l, e * P, P), yh, yl, KD)
        self.norm(self.xT, A["final_g"])

    def scan_rows(self, out, rows, keep, op, backward, after):
        nc, c = self.nc, self.c
        if backward:
            out, rows, keep = out[:, ::-1], rows[:, ::-1], keep[:, ::-1]
        return c.dve(nc.vector.tensor_tensor_scan, out, keep, rows, 0.0, ALU.mult, op, after=after)

    def to_cols(self, dst, rows, bank, after):
        n = rows.shape[0]
        m = self.c.transposes([(bank[:, t * n:(t + 1) * n], rows[:, t * P:(t + 1) * P]) for t in range(NT)],
                              self.k("ident"), after)
        return self.c.dve(self.nc.vector.tensor_copy, dst, bank[:, 0:NT * n].rearrange("p (t n) -> p t n", n=n), after=[m])

    def norm_blocks(self, y, n, gain, sq, ss, eps, after):
        nc, c = self.nc, self.c
        for i in range(n):
            m = c.act(nc.scalar.activation, sq[:, i, :], y[:, i, :], ACT.Square, accum_out=ss[:, i:i + 1], after=after)
        m = c.act(nc.scalar.activation, ss[:, 0:n], ss[:, 0:n], ACT.Ln, bias=eps, scale=1.0 / P, after=[m])
        m = c.act(nc.scalar.activation, ss[:, 0:n], ss[:, 0:n], ACT.Exp, scale=-0.5, after=[m])
        for i in range(n):
            m2 = c.dve(nc.vector.scalar_tensor_tensor, y[:, i, :], y[:, i, :], ss[:, i:i + 1], gain(i), ALU.mult, ALU.mult,
                       after=[m, *after])
        return m2

    def gdn(self, l):
        nc, c, A = self.nc, self.c, self.A
        H = 4
        W4 = [P, NT, P]
        with ExitStack() as es:
            sb = self.allocator(es)
            par = [sb(f"gdn_params{d}", [H, 2]) for d in range(2)]
            q5 = sb("chunk_scalars", [P, 6, NT, 2, H])
            g = sb("log_decay", [P, NT, 8])
            tot = sb("chunk_total", [P, NT, 8])
            ar, br, tmp, gcr = [[sb(f"{n}_rows{d}", [H, T]) for d in range(2)] for n in ("a", "beta", "a_tmp", "gc")]
            table = self.load_tables("gdn", sb("gdn_tables", [P, self.group_width("gdn")]))
            gain = sb("gdn_gain", [P, P])
            eps = sb("gdn_eps", [P, 1])
            pad = sb("qkv_padded", [P, 3, T + 4])
            z = self.z2
            lg = c.dma((gain[:, :], A["gdn_norm_g_2"][l].partition_broadcast(P)))
            c.dve(nc.vector.memset, eps[:, :], EPS)
            mb, mc, mg = [], [], []
            c.dve.wait(table)
            for d in range(2):
                hs = slice(d * H, (d + 1) * H)
                at = C2["a_ab"] + d * H
                ld = c.dma((ar[d][:, :], z[at:at + H, :]), (br[d][:, :], z[at + 8:at + 8 + H, :]),
                           (par[d][:, 0:1], A["gdn_a_log_2"][l, d].unsqueeze(1)), (par[d][:, 1:2], A["gdn_dt_bias_2"][l, d].unsqueeze(1)), slow=True)
                m = self.sigmoid(br[d][:, :], br[d][:, :], [ld])
                mb.append(self.to_cols(q5[:, 0, :, d, :], br[d][:, :], self.bank[0], [m, c.dve.mark()]))
                m = c.dve(nc.vector.tensor_scalar, ar[d][:, :], ar[d][:, :], par[d][:, 1:2], None, ALU.add, after=[ld])
                m = c.act(nc.scalar.activation, tmp[d][:, :], ar[d][:, :], ACT.Abs, after=[m])
                m = c.act(nc.scalar.activation, tmp[d][:, :], tmp[d][:, :], ACT.Exp, scale=-1.0, after=[m])
                m = c.act(nc.scalar.activation, tmp[d][:, :], tmp[d][:, :], ACT.Ln, bias=1.0, after=[m])
                ma = c.act(nc.scalar.activation, par[d][:, 0:1], par[d][:, 0:1], ACT.Exp, after=[ld])
                m = c.dve(nc.vector.scalar_tensor_tensor, ar[d][:, :], ar[d][:, :], 0.0, tmp[d][:, :], ALU.max, ALU.add, after=[m])
                m = c.dve(nc.vector.tensor_scalar, ar[d][:, :], ar[d][:, :], par[d][:, 0:1], -1.0, ALU.mult, ALU.mult, after=[m, ma])
                mg.append(self.to_cols(g[:, :, hs], ar[d][:, :], self.bank[1], [m, c.dve.mark()]))
                m = self.scan_rows(gcr[d][:, :], ar[d][:, :], self.k("carryb" if d else "carryf", H), ALU.add, d, [m])
                mc.append(self.to_cols(q5[:, 5, :, d, :], gcr[d][:, :], self.bank[2], [m, c.dve.mark()]))
                c.dma((self.rows[hs, :], gcr[d][:, :]), after=[m])
            m = c.products(self.bank[3][:, 0:32], [(self.k("ones"), g[:, :, :].rearrange("p t n -> p (t n)"))], mg)
            mt = c.dve(nc.vector.tensor_copy, tot[:, :, :].rearrange("p t n -> p (t n)"), self.bank[3][:, 0:32], after=[m])
            q = [q5[:, i, :, :, :].rearrange("p t d h -> p t (d h)") for i in range(6)]
            c.act(nc.scalar.activation, q[4], tot[:, :, :], ACT.Exp, after=[mt])
            me = c.act(nc.scalar.activation, q[2], q[5], ACT.Exp, after=mc)
            m = c.dve(nc.vector.tensor_tensor, q[3], tot[:, :, :], q[5], ALU.subtract, after=[*mc, mt])
            c.act(nc.scalar.activation, q[3], q[3], ACT.Exp, after=[m])
            c.dve(nc.vector.tensor_tensor, q[1], q[2], q[0], ALU.mult, after=[me, *mb])
            c.dve(nc.vector.memset, pad[:, :, 0:2], 0.0)
            c.dve(nc.vector.memset, pad[:, :, T + 2:], 0.0)
            c.barrier()

            wide = sb("gc_wide", [P, 2, T])
            zf = sb("z_rows", [P, T])
            taps = sb("qkv_taps", [P, 3, 5])
            acc = sb("qkv", [P, 3, T])
            sqt = sb("qkv_tmp", [P, 3, T])
            zt = sb("z_gate", W4)
            ktok, vtok = sb("k_tok", W4), sb("v_tok", W4)
            osum = sb("o_sum", W4)
            ss = sb("sum_sq", [P, 8])
            hq = sb("head_scalars", [P, 6, NT, 2])
            buf = {n: [sb(f"{n}{d}", W4) for d in range(2)] for n in
                   ("A", "AT", "aT", "M", "MT", "LT", "X", "vb", "kbe", "kdec")}
            S = [sb(f"state{d}", [P, P]) for d in range(2)]
            vn = [sb(f"v_new{d}", [P, P]) for d in range(2)]
            q_now, z_now, z_tmp = sb("q_now", [P, T]), sb("z_gate_now", W4), sb("z_gate_tmp", W4)
            flat = lambda x: x[:, :, :].rearrange("p t n -> p (t n)")
            ch = [slice(t * P, (t + 1) * P) for t in range(NT)]
            wide3 = lambda name: self.k(name).unsqueeze(1).to_broadcast(W4)
            lev = lambda name, s: self.k(name)[:, s * P:(s + 1) * P].unsqueeze(1).to_broadcast(W4)

            def prepare(h, acc_free, wide_free, bank_free):
                lw = [c.dma((pad[:, i, 2:2 + T], z[bass.ds(h * P + C2["a_qkv"] + 512 * i, P), :])) for i in range(3)]
                lt = c.dma(*[(taps[:, i, :], A["gdn_conv_w_2"][l, :, bass.ds(h * P + 512 * i, P)].rearrange("w p -> p w"))
                             for i in range(3)], slow=True)
                lz = c.dma((zf[:, :], z[bass.ds(h * P + C2["a_z"], P), :]))
                c.dma(*[(wide[:, d, :], self.row(h + d * H)) for d in range(2)], after=wide_free)
                yield
                free = list(bank_free)
                for i in range(3):
                    m = c.dve(nc.vector.tensor_scalar, acc[:, i, :], pad[:, i, 0:T], taps[:, i, 0:1], None, ALU.mult,
                              after=[lw[i], lt, acc_free])
                    yield
                    for w in range(1, 5):
                        m = c.dve(nc.vector.scalar_tensor_tensor, acc[:, i, :], pad[:, i, w:w + T], taps[:, i, w:w + 1],
                                  acc[:, i, :], ALU.mult, ALU.add, after=[m])
                        yield
                    m = c.act(nc.scalar.activation, sqt[:, i, :], acc[:, i, :], ACT.Tanh, scale=0.5, after=[m])
                    yield
                    m = c.dve(nc.vector.scalar_tensor_tensor, acc[:, i, :], sqt[:, i, :], 1.0, acc[:, i, :], ALU.add, ALU.mult, after=[m])
                    yield
                    m = c.dve(nc.vector.tensor_scalar, acc[:, i, :], acc[:, i, :], 0.5, None, ALU.mult, after=[m])
                    yield
                    if i < 2:
                        m = c.act(nc.scalar.activation, sqt[:, i, :], acc[:, i, :], ACT.Square, after=[m])
                        m = c.products(self.bank[i][:, :], [(self.k("ones"), sqt[:, i, :])], [m, free])
                        yield
                        m = c.act(nc.scalar.activation, sqt[:, i, :], self.bank[i][:, :], ACT.Ln, bias=eps[:, 0:1], after=[m])
                        free = [*free, m]
                        m = c.act(nc.scalar.activation, sqt[:, i, :], sqt[:, i, :], ACT.Exp, scale=-0.5, after=[m])
                        yield
                        c.dve(nc.vector.scalar_tensor_tensor, acc[:, i, :], acc[:, i, :],
                              P ** -0.5 if i == 0 else 1.0, sqt[:, i, :], ALU.mult, ALU.mult, after=[m])
                        yield
                m = c.transposes([(self.bank[0][:, ch[t]], zf[:, ch[t]]) for t in range(NT)], self.k("ident"), [lz, free])
                yield
                m = self.silu(flat(zt), self.bank[0][:, :], flat(z_tmp), [m, acc_free])
                yield
                c.pool(nc.gpsimd.tensor_tensor, zt[:, :, :], zt[:, :, :], gain[:, :].unsqueeze(1).to_broadcast(W4),
                       ALU.mult, after=[m])

            def head(h, ahead):
                side = None

                def turn(n=1):
                    for _ in range(n if side is not None else 0):
                        next(side, None)
                mh = c.dve(nc.vector.tensor_copy, hq[:, :, :, :].rearrange("p i t d -> p (i t d)"),
                           q5[:, :, :, :, bass.ds(h, 1)].rearrange("p i t d o -> p (i t d o)"))
                qn = c.dve(nc.vector.tensor_copy, q_now[:, :], acc[:, 0, :])
                mz = c.pool(nc.gpsimd.tensor_copy, z_now[:, :, :], zt[:, :, :])
                qT, kT, vT = q_now[:, :], acc[:, 1, :], acc[:, 2, :]
                tok = []
                for bb, dst, src in ((self.bank[6], ktok, kT), (self.bank[7], vtok, vT)):
                    m = c.transposes([(bb[:, ch[t]], src[:, ch[t]]) for t in range(NT)], self.k("ident"))
                    tok.append(c.act(nc.scalar.copy, flat(dst), bb[:, :], after=[m]))
                for t in range(NT):
                    mkk = c.products(self.bank[0][:, ch[t]], [(kT[:, ch[t]], kT[:, ch[t]])])
                for t in range(NT):
                    mkq = c.products(self.bank[1][:, ch[t]], [(kT[:, ch[t]], qT[:, ch[t]])], [qn])
                mAT, mM, mMT, maT, mA, used = [None] * 2, [None] * 2, [None] * 2, [None] * 2, [None] * 2, [None] * 2
                mvb = [None] * 2
                for d in range(2):
                    A_, AT, aT = buf["A"][d], buf["AT"][d], buf["aT"][d]
                    for t in range(NT):
                        gc = hq[:, 5, t, d:d + 1]
                        row = wide[:, d, ch[t]]
                        m1 = c.dve(nc.vector.tensor_scalar, A_[:, t, :], row, gc, 0.0, ALU.subtract, ALU.max, after=[mh])
                        m2 = c.dve(nc.vector.tensor_scalar, aT[:, t, :], row, gc, 0.0, ALU.subtract, ALU.min, after=[mh])
                    m1 = c.act(nc.scalar.activation, flat(A_), flat(A_), ACT.Exp, scale=-1.0, after=[m1])
                    m2 = c.act(nc.scalar.activation, flat(aT), flat(aT), ACT.Exp, after=[m2])
                    m1 = c.dve(nc.vector.tensor_tensor, A_[:, :, :], A_[:, :, :], wide3("sup" if d else "slow"), ALU.mult, after=[m1])
                    m2 = c.pool(nc.gpsimd.tensor_tensor, aT[:, :, :], aT[:, :, :], wide3("low" if d else "up"), ALU.mult, after=[m2])
                    maT[d] = c.dve(nc.vector.tensor_tensor, flat(aT), flat(aT), self.bank[1][:, :], ALU.mult, after=[m2, mkq])
                    for t in range(NT):
                        mA[d] = c.dve(nc.vector.scalar_tensor_tensor, A_[:, t, :], self.bank[0][:, ch[t]], hq[:, 0, t, d:d + 1],
                                      A_[:, t, :], ALU.mult, ALU.mult, after=[m1, mkk])
                    bb = self.bank[2 + d]
                    m = c.transposes([(bb[:, ch[t]], A_[:, t, :]) for t in range(NT)], self.k("ident"), [mA[d]])
                    mAT[d] = c.act(nc.scalar.copy, flat(AT), bb[:, :], after=[m])
                    for n, src, i in (("vb", vtok, 0), ("kbe", ktok, 1), ("kdec", ktok, 3)):
                        mvb[d] = c.pool(nc.gpsimd.tensor_tensor, buf[n][d][:, :, :], src[:, :, :],
                                        hq[:, i, :, d:d + 1].to_broadcast(W4), ALU.mult, after=[tok, mh])
                if ahead:
                    side = prepare(h + 1, [qn, mz, tok, mkk, mkq], [mA, maT], [mA, maT])
                for d in range(2):
                    A_, AT, M, MT = buf["A"][d], buf["AT"][d], buf["M"][d], buf["MT"][d]
                    lo, up = ("levup", "levlow") if d else ("levlow", "levup")
                    m1 = c.dve(nc.vector.tensor_tensor, M[:, :, :], A_[:, :, :], lev(lo, 0), ALU.mult, after=[mA[d]])
                    m2 = c.dve(nc.vector.tensor_tensor, MT[:, :, :], AT[:, :, :], lev(up, 0), ALU.mult, after=[mAT[d]])
                    mM[d] = c.dve(nc.vector.tensor_tensor, M[:, :, :], wide3("ident"), M[:, :, :], ALU.subtract, after=[m1])
                    mMT[d] = c.dve(nc.vector.tensor_tensor, MT[:, :, :], wide3("ident"), MT[:, :, :], ALU.subtract, after=[m2])
                for s in range(1, LEVELS):
                    for d in range(2):
                        A_, AT, M, MT = buf["A"][d], buf["AT"][d], buf["M"][d], buf["MT"][d]
                        LT, X = buf["LT"][d], buf["X"][d]
                        bx, by, bz = self.bank[2 + 3 * d], self.bank[3 + 3 * d], self.bank[4 + 3 * d]
                        up = "levlow" if d else "levup"
                        ml = c.pool(nc.gpsimd.tensor_tensor, LT[:, :, :], AT[:, :, :], lev(up, s), ALU.mult, after=[mAT[d], used[d]])
                        for t in range(NT):
                            m = c.products(bx[:, ch[t]], [(LT[:, t, :], M[:, t, :])], [ml, mM[d], mMT[d], mAT])
                        used[d] = m
                        mx = c.act(nc.scalar.copy, flat(X), bx[:, :], after=[m])
                        if s < LEVELS - 1:
                            for t in range(NT):
                                m = c.products(by[:, ch[t]], [(MT[:, t, :], X[:, t, :])], [mx])
                            my = m
                        for t in range(NT):
                            m = c.products(bz[:, ch[t]], [(X[:, t, :], MT[:, t, :])], [mx])
                        if s < LEVELS - 1:
                            mM[d] = c.dve(nc.vector.tensor_tensor, flat(M), flat(M), by[:, :], ALU.subtract, after=[my])
                        mMT[d] = c.dve(nc.vector.tensor_tensor, flat(MT), flat(MT), bz[:, :], ALU.subtract, after=[m])
                        turn(2)
                U, WT = buf["A"], buf["LT"]
                mu, mw = [None] * 2, [None] * 2
                for d in range(2):
                    bu, bw = self.bank[2 + 3 * d], self.bank[3 + 3 * d]
                    for t in range(NT):
                        m = c.products(bu[:, ch[t]], [(buf["MT"][d][:, t, :], buf["vb"][d][:, t, :])], [mMT[d], mvb[d]])
                    mu[d] = c.act(nc.scalar.copy, flat(U[d]), bu[:, :], after=[m])
                    for t in range(NT):
                        m = c.products(bw[:, ch[t]], [(buf["kbe"][d][:, t, :], buf["MT"][d][:, t, :])], [mMT[d], mvb[d]])
                    mw[d] = c.dve(nc.vector.tensor_copy, flat(WT[d]), bw[:, :], after=[m])
                    turn(2)
                mS, mo, last = [None] * 2, [None] * NT, [None] * 2
                for n in range(NT):
                    for d in range(2):
                        t = NT - 1 - n if d else n
                        o = osum[:, t, :]
                        b1, b2, b3 = [self.bank[3 * d + j] for j in (2, 3, 4)]
                        if n == 0:
                            V, mv = U[d][:, t, :], mu[d]
                        else:
                            m = c.products(b1[:, 0:P], [(WT[d][:, t, :], S[d][:, :])], [mw, mS[d], mu, last[d]])
                            mv = c.dve(nc.vector.tensor_tensor, vn[d][:, :], U[d][:, t, :], b1[:, 0:P], ALU.subtract, after=[m, mS[d]])
                            V = vn[d][:, :]
                            mq = c.products(b2[:, 0:P], [(qT[:, ch[t]], S[d][:, :])], [mS[d], last[d]])
                        mi = c.products(b3[:, 0:P], [(buf["aT"][d][:, t, :], V)], [mv, maT[d], mw, mu, last[d]])
                        if mo[t] is None:
                            mo[t] = c.dve(nc.vector.tensor_copy, o, b3[:, 0:P], after=[mi, mz])
                        else:
                            mo[t] = c.dve(nc.vector.tensor_tensor, o, o, b3[:, 0:P], ALU.add, after=[mi, mo[t]])
                        if n > 0:
                            mo[t] = c.dve(nc.vector.scalar_tensor_tensor, o, b2[:, 0:P], hq[:, 2, t, d:d + 1], o,
                                          ALU.mult, ALU.add, after=[mq, mo[t]])
                        last[d] = mo[t]
                        if n < NT - 1:
                            ms = c.products(b3[:, P:2 * P], [(buf["kdec"][d][:, t, :], V)], [mo[t]])
                            if n == 0:
                                mS[d] = c.dve(nc.vector.tensor_copy, S[d][:, :], b3[:, P:2 * P], after=[ms])
                            else:
                                mS[d] = c.dve(nc.vector.scalar_tensor_tensor, S[d][:, :], S[d][:, :], hq[:, 4, t, d:d + 1],
                                              b3[:, P:2 * P], ALU.mult, ALU.add, after=[ms])
                            last[d] = mS[d]
                        turn()
                turn(100)
                m = self.norm_blocks(osum, NT, lambda i: z_now[:, i, :], vtok, ss, eps[:, 0:1],
                                     [mo, mz, mvb])
                self.store_T(osum, 1, [self.bank[7]], h, [m])
                c.barrier()

            for _ in prepare(0, [], [], []):
                pass
            c.barrier()
            with nc.Fori(0, H - 1) as h:
                head(h, True)
            head(H - 1, False)

    def diff(self, l):
        nc, c, A = self.nc, self.c, self.A
        with ExitStack() as es:
            sb = self.allocator(es)
            table = self.load_tables("rope", sb("rope_tables", [P, self.group_width("rope")]))
            lp = sb("lambda_params", [P, 4, HD])
            lam = sb("lambda", [P, 4])
            gain = sb("diff_gain", [P, P])
            eps = sb("diff_eps", [P, 1])
            ld = c.dma((lp[:, :, :].rearrange("p a d -> p (a d)"), A["diff_lambda_2"][l].rearrange("a d -> (a d)").partition_broadcast(P)),
                       (gain[:, :], A["diff_norm_g_2"][l].partition_broadcast(P)), slow=True)
            c.dve(nc.vector.memset, eps[:, :], EPS)
            for i in range(2):
                m = c.dve(nc.vector.tensor_tensor, lp[:, 2 * i, :], lp[:, 2 * i, :], lp[:, 2 * i + 1, :], ALU.mult, after=[ld])
                m = c.dve(nc.vector.tensor_reduce, lam[:, i:i + 1], lp[:, 2 * i, :], AX.X, ALU.add, after=[m])
            m = c.act(nc.scalar.activation, lam[:, 0:2], lam[:, 0:2], ACT.Exp, after=[m])
            m = c.dve(nc.vector.tensor_tensor, lam[:, 2:3], lam[:, 0:1], lam[:, 1:2], ALU.subtract, after=[m])
            m = c.dve(nc.vector.tensor_tensor, lam[:, 2:3], lam[:, 2:3], self.k("lam")[:, bass.ds(l, 1)], ALU.add, after=[m, table])
            m = c.dve(nc.vector.tensor_copy, lam[:, 3:4], self.k("lam")[:, bass.ds(l + DEPTH, 1)])
            c.dve(nc.vector.tensor_scalar, gain[:, :], gain[:, :], lam[:, 3:4], None, ALU.mult, after=[m, ld])
            c.barrier()
            q2, k2 = [[sb(f"{n}_twice{i}", [P, T]) for i in range(4)] for n in "qk"]
            qs, kh = [[sb(f"{n}{i}", [P, T], F32R) for i in range(4)] for n in ("q_stacked", "k_hi")]
            vf, rt = [sb(f"v_rows{j}", [P, T]) for j in range(2)], [sb(f"rope_tmp{i}", [P, T]) for i in range(4)]
            v, y = [sb(f"v_tok{j}", [P, NT, P]) for j in range(2)], sb("y_tok", [P, NT * 2, P])
            sq = sb("y_squared", [P, NT * 2, P])
            ss = sb("sum_sq", [P, 8])
            self.attention_buffers(es, 2)
            with nc.Fori(0, 2) as pair:
                lk, lq = [[c.dma(*self.twice(x[i], self.z2[bass.ds(pair * 2 * P + C2[n] + i * HD, HD), :])) for i in range(4)]
                          for x, n in ((k2, "b_k"), (q2, "b_q"))]
                lv = [c.dma((vf[j][:, :], self.z2[bass.ds(pair * 2 * P + C2["b_v"] + j * P, P), :])) for j in range(2)]
                rot = (self.k("rot2"), self.k("cos2"), self.k("sin2"))
                ready, free = [], [None] * 4
                for i in range(4):
                    for n, x in enumerate((k2[i], q2[i])):
                        b = 2 * (i % 2) + n
                        free[b] = self.rope(x[:, :], rt[b][:, :], self.bank[b], *rot, [(lk, lq)[n][i], free[b]])
                        if n == 0:
                            ready.append(self.split(kh[i][:, :], self.low(x)[:, :], x[:, :], [free[b]]))
                        else:
                            ready.append(self.stack(x, qs[i], HD ** -0.5, [free[b]]))
                mv = [self.to_tokens(v[j][:, :, :], vf[j], self.bank[6 + j], [lv[j]]) for j in range(2)]

                def mix(p0, p1, rinv, marks):
                    m = c.dve(nc.vector.tensor_tensor, rinv[1], rinv[1], lam[:, 2:3], ALU.mult, after=marks)
                    m = c.dve(nc.vector.tensor_scalar, p1, p1, rinv[1], None, ALU.mult, after=[m])
                    return c.dve(nc.vector.scalar_tensor_tensor, p0, p0, rinv[0], p1, ALU.mult, ALU.subtract, after=[m])
                units = []
                for j in range(2):
                    for t in range(NT):
                        def out(o, rinv, marks, at=2 * t + j):
                            return c.dve(nc.vector.tensor_copy, y[:, at, :], o, after=marks)
                        units.append(dict(maps=[(qs[i][:, t * P:(t + 1) * P], (kh[i][:, :], self.low(k2[i])[:, :])) for i in (2 * j, 2 * j + 1)],
                                          width=T, extra=[], decay=None, sink=None, coef=None, mix=mix,
                                          values=[v[j][:, i, :] for i in range(NT)], out=out))
                self.attention(units, [ready, mv])
                m = self.norm_blocks(y, NT * 2, lambda i: gain[:, :], sq, ss, eps[:, 0:1], [c.dve.mark()])
                self.store_T(y[:, :, :].rearrange("p (t j) d -> p t (j d)", j=2), 2, [self.bank[6], self.bank[7]], pair * 2 + 4, [m])
                c.barrier()

    def swa(self, l):
        nc, c, A = self.nc, self.c, self.A
        with ExitStack() as es:
            sb = self.allocator(es)
            self.load_tables("rope", sb("rope_tables", [P, self.group_width("rope")]))
            sinks = sb("sinks", [P, 8])
            q2, qs = [sb(f"q_twice{h}", [P, T]) for h in range(4)], [sb(f"q_stacked{h}", [P, T], F32R) for h in range(4)]
            k2, kh = sb("k_twice", [P, T]), sb("k_hi", [P, T], F32R)
            vf, rt = sb("v_rows", [HD, T]), [sb(f"rope_tmp{i}", [P, T]) for i in range(2)]
            v, y = sb("v_tok", [P, NT, HD]), sb("y_tok", [P, NT, 2 * P])
            sk, nsk = sb("group_sinks", [P, 4]), sb("group_sinks_neg", [P, 4])
            self.attention_buffers(es, 1)
            c.dma((sinks[:, :], A["swa_sink_2"][l].partition_broadcast(P)), slow=True)
            c.barrier()
            with nc.Fori(0, 2) as grp:
                z = self.z2
                lk = c.dma(*self.twice(k2, z[bass.ds(grp * HD + C2["c_k"], HD), :]))
                lq = [c.dma(*self.twice(q2[h], z[bass.ds(grp * 256 + C2["c_q"] + h * HD, HD), :])) for h in range(4)]
                lv = c.dma((vf[:, :], z[bass.ds(grp * HD + C2["c_v"], HD), :]))
                m = c.dve(nc.vector.tensor_copy, sk[:, :], sinks[:, bass.ds(grp * 4, 4)])
                ms = c.dve(nc.vector.tensor_scalar, nsk[:, :], sk[:, :], -1.0, None, ALU.mult, after=[m])
                rot = (self.k("rot2"), self.k("cos2"), self.k("sin2"))
                tmp_free = [None, None]
                m = self.rope(k2[:, :], rt[0][:, :], self.bank[0], *rot, [lk])
                tmp_free[0] = m
                ready = [ms, self.split(kh[:, :], self.low(k2)[:, :], k2[:, :], [m])]
                for h in range(4):
                    n = (h + 1) % 2
                    m = self.rope(q2[h][:, :], rt[n][:, :], self.bank[n], *rot, [lq[h], tmp_free[n]])
                    tmp_free[n] = m
                    ready.append(self.stack(q2[h], qs[h], HD ** -0.5, [m]))
                mv = self.to_tokens(v[:, :, :], vf, self.bank[6], [lv], HD)
                units = []
                for h in range(4):
                    for t in range(NT):
                        lo, hi = max(t - 1, 0), min(t + 2, NT)
                        extra = [(self.r("ident"), self.r("far"), 0, P)] if t > 0 else []
                        extra += [(self.r("ident"), self.r("later"), (hi - lo - 1) * P, P)] if t < NT - 1 else []

                        def out(o, rinv, marks, h=h, t=t):
                            return c.dve(nc.vector.tensor_scalar, y[:, t, h * HD:(h + 1) * HD], o, rinv, None, ALU.mult, after=marks)
                        units.append(dict(maps=[(qs[h][:, t * P:(t + 1) * P], (kh[:, lo * P:hi * P], self.low(k2)[:, lo * P:hi * P]))], width=(hi - lo) * P,
                                          extra=extra, decay=None, sink=(sk[:, h:h + 1], nsk[:, h:h + 1]), coef=None, mix=None,
                                          values=[v[:, i, :] for i in range(lo, hi)], out=out))
                self.attention(units, [ready, mv])
                self.store_T(y, 2, [self.bank[6], self.bank[7]], grp * 2 + 8, [c.dve.mark()])
                c.barrier()

    def mlstm(self, l):
        nc, c, A = self.nc, self.c, self.A
        with ExitStack() as es:
            sb = self.allocator(es)
            bias = [sb(f"gate_bias{d}", [4, 2]) for d in range(2)]
            gain = sb("mlstm_gain", [P, P])
            eps = sb("mlstm_eps", [P, 1])
            cols = sb("r_and_exp_m", [P, 2, NT, 8])
            ir, fr, tmp, Br, rr, Rr = [[sb(f"{n}{d}", [4, T]) for d in range(2)]
                                       for n in ("i_rows", "f_rows", "f_tmp", "B_rows", "r_rows", "R_rows")]
            z = self.z2
            lg = c.dma((gain[:, :], A["mlstm_norm_g_2"][l].partition_broadcast(P)))
            c.dve(nc.vector.memset, eps[:, :], EPS)
            for d in range(2):
                hs = slice(4 * d, 4 * d + 4)
                at = C2["d_if"] + 4 * d
                ld = c.dma((ir[d][:, :], z[at:at + 4, :]), (fr[d][:, :], z[at + 8:at + 12, :]),
                           (bias[d][:, 0:1], A["mlstm_gate_b_2"][l, 0, d].unsqueeze(1)),
                           (bias[d][:, 1:2], A["mlstm_gate_b_2"][l, 1, d].unsqueeze(1)), slow=True)
                m1 = c.dve(nc.vector.tensor_scalar, ir[d][:, :], ir[d][:, :], bias[d][:, 0:1], None, ALU.add, after=[ld])
                m2 = c.dve(nc.vector.tensor_scalar, fr[d][:, :], fr[d][:, :], bias[d][:, 1:2], None, ALU.add, after=[ld])
                m2 = self.log_sigmoid(fr[d][:, :], tmp[d][:, :], [m2])
                m2 = self.scan_rows(Br[d][:, :], fr[d][:, :], self.k("onesrow", 4), ALU.add, d, [m2])
                m1 = c.dve(nc.vector.tensor_tensor, rr[d][:, :], ir[d][:, :], Br[d][:, :], ALU.subtract, after=[m1, m2])
                mR = self.scan_rows(Rr[d][:, :], rr[d][:, :], self.k("onesrow", 4), ALU.max, d, [m1])
                m2 = c.dve(nc.vector.tensor_tensor, Br[d][:, :], Br[d][:, :], Rr[d][:, :], ALU.add, after=[mR])
                self.to_cols(cols[:, 0, :, hs], rr[d][:, :], self.bank[3], [m1, c.dve.mark()])
                m2 = self.to_cols(cols[:, 1, :, hs], Br[d][:, :], self.bank[4], [m2, c.dve.mark()])
                c.dma((self.rows[hs, :], Rr[d][:, :]), after=[mR])
            c.act(nc.scalar.activation, cols[:, 1, :, :], cols[:, 1, :, :], ACT.Exp, scale=-1.0, after=[m2])
            c.barrier()
            q2, k2 = [[sb(f"{n}_twice{i}", [P, T]) for i in range(2)] for n in "qk"]
            qh, ks = [[sb(f"{n}{i}", [P, T], F32R) for i in range(2)] for n in ("q_hi", "k_stacked")]
            vf, of = [[sb(f"{n}_rows{i}", [P, T]) for i in range(2)] for n in ("v", "o")]
            V = P + 1
            va = sb("v_and_one", [P, NT, 2, V])
            og, y = sb("o_gate", [P, NT, 2, P]), sb("y_tok", [P, NT, 2, P])
            pc = sb("pair_cols", [P, 2, NT, 2, 2])
            pR = sb("pair_R", [P, 2, 2, T])
            WT = [[sb(f"weights{i}_{d}", [P, NT, T]) for d in range(2)] for i in range(1)]
            den = sb("den", [P, 2, 2, NT])
            ss = sb("sum_sq", [P, 8])
            with nc.Fori(0, 2) as pair:
                lq, lk = [[c.dma(*self.twice(x[h], z[bass.ds(pair * P + C2[n] + h * HD, HD), :])) for h in range(2)]
                          for x, n in ((q2, "d_q"), (k2, "d_k"))]
                lv, lo = [[c.dma((x[h][:, :], z[bass.ds(pair * 256 + C2[n] + h * P, P), :])) for h in range(2)]
                          for x, n in ((vf, "d_v"), (of, "d_o"))]
                mc = []
                for i in range(2):
                    for d in range(2):
                        mc.append(c.dve(nc.vector.tensor_copy, pc[:, i, :, d, :], cols[:, i, :, bass.ds(pair * 2 + 4 * d, 2)]))
                mc.append(c.dma(*[(pR[:, d, h, :], self.row(pair * 2 + 4 * d + h)) for d in range(2) for h in range(2)]))
                m1 = c.dve(nc.vector.memset, va[:, :, :, P:V], 1.0)
                mv, mq = [m1], []
                for h in range(2):
                    mq.append(self.split(qh[h][:, :], self.low(q2[h])[:, :], q2[h][:, :], [lq[h]]))
                    mq.append(self.stack(k2[h], ks[h], HD ** -0.5, [lk[h]]))
                    mv.append(self.to_tokens(va[:, :, h, 0:P], vf[h], self.bank[2 + h], [lv[h]]))
                    m = self.sigmoid(of[h][:, :], of[h][:, :], [lo[h]])
                    mo = self.to_tokens(og[:, :, h, :], of[h], self.bank[4 + h], [m])
                mo = c.pool(nc.gpsimd.tensor_tensor, og[:, :, :, :].rearrange("p t h n -> p (t h) n"),
                            og[:, :, :, :].rearrange("p t h n -> p (t h) n"),
                            gain[:, :].unsqueeze(1).to_broadcast([P, 2 * NT, P]), ALU.mult, after=[mo])
                used, my = [None, None], None
                free = [[mv, mo]] * 4
                fs = [[], []]
                for h in range(2):
                    mw = [[None] * NT for _ in range(2)]
                    for j in range(NT):
                        bs = self.bank[j % 2]
                        kk = ks[h][:, j * P:(j + 1) * P]
                        m = c.products(bs[:, :], [(kk, qh[h][:, :]), (kk, self.low(q2[h])[:, :])], [mq, fs[j % 2]])
                        for d in range(2):
                            rng = slice(0, (j + 1) * P) if d else slice(j * P, T)
                            w = WT[0][d][:, j, rng]
                            diag = WT[0][d][:, j, j * P:(j + 1) * P]
                            a = c.dve(nc.vector.tensor_scalar, w, pR[:, d, h, rng], pc[:, 0, j, d, h:h + 1], 0.0,
                                      ALU.subtract, ALU.max, after=[mc, used[d]])
                            a = c.act(nc.scalar.activation, w, w, ACT.Exp, scale=-1.0, after=[a])
                            a = c.pool(nc.gpsimd.tensor_tensor, diag, diag, self.k("low" if d else "up"), ALU.mult, after=[a])
                            mw[d][j] = c.dve(nc.vector.tensor_tensor, w, w, bs[:, rng], ALU.mult, after=[a, m])
                        fs[j % 2] = [mw[0][j], mw[1][j]]
                    for d in range(2):
                        mo2 = []
                        for t in range(NT):
                            bo = self.bank[2 + 2 * d + t // 2]
                            js = range(t, NT) if d else range(0, t + 1)
                            m = c.products(bo[:, (t % 2) * V:(t % 2) * V + V],
                                           [(WT[0][d][:, j, t * P:(t + 1) * P], va[:, j, h, :]) for j in js],
                                           [mw[d], mv, free[2 * d + t // 2], free[2 * d + t // 2]])
                            mo2.append(m)
                        used[d] = m
                        dn = den[:, d, h, :]
                        for i in range(2):
                            bo = self.bank[2 + 2 * d + i]
                            mm = c.act(nc.scalar.activation, dn[:, 2 * i:2 * i + 2],
                                       bo[:, 0:2 * V].rearrange("p (t v) -> p t v", v=V)[:, :, P], ACT.Abs, after=[m])
                        mm = c.dve(nc.vector.tensor_tensor, dn, dn, pc[:, 1, :, d, h], ALU.max, after=[mm, mc])
                        mm = c.dve(nc.vector.reciprocal, dn, dn, after=[mm])
                        for t in range(NT):
                            bo = self.bank[2 + 2 * d + t // 2]
                            num = bo[:, (t % 2) * V:(t % 2) * V + P]
                            if d == 0:
                                my = c.dve(nc.vector.tensor_scalar, y[:, t, h, :], num, dn[:, t:t + 1], None, ALU.mult, after=[mm])
                            else:
                                my = c.dve(nc.vector.scalar_tensor_tensor, y[:, t, h, :], num, dn[:, t:t + 1], y[:, t, h, :],
                                           ALU.mult, ALU.add, after=[mm, my])
                            free[2 * d + t // 2] = my
                fold = lambda x: x[:, :, :, :].rearrange("p t h n -> p (t h) n")
                m = self.norm_blocks(fold(y), 2 * NT, lambda i: fold(og)[:, i, :], pR[:, :, :, :].rearrange("p d h (a n) -> p (d h a) n", n=P),
                                     ss, eps[:, 0:1], [my, mo])
                self.store_T(y[:, :, :, :].rearrange("p t h n -> p t (h n)"), 2, [self.bank[6], self.bank[7]], pair * 2 + 12, [m])
                c.barrier()

    def gate_branches(self, l, mT):
        nc, c, A = self.nc, self.c, self.A
        B = 4
        KB = 4
        with ExitStack() as es:
            sb = self.allocator(es)
            yh, yl, ready = self.split_y(sb, 16)
            sg = [sb(f"gate{s}", [P, T]) for s in range(B)]

            def load(e, s, out, width):
                return [(out[:, 0:KD, :], A["w_gate_2"][l, :, s, bass.ds(e * P, P)].rearrange("(k p) n -> p k n", p=P)),
                        (out[:, KD:, :], A["w_branch_2"][l, s, :, bass.ds(e * P, P)].rearrange("(k p) n -> p k n", p=P))]

            def products(s, wh, wl, width):
                self.three_passes(self.bank[s], P, [(wh[:, k, :], wl[:, k, :], self.hH[:, k, :], self.hL[:, k, :]) for k in range(KD)])
                return self.three_passes(self.bank[4 + s], P, [
                    (wh[:, KD + k, :], wl[:, KD + k, :], yh[:, KB * s + k, :], yl[:, KB * s + k, :]) for k in range(KB)])

            def drain(e, s, tile, width):
                nc.scalar.wait_ge(c.mm[s], e + 2)
                nc.scalar.wait_ge(c.ev[s], e + 1)
                nc.scalar.activation(sg[s][:, :], self.bank[s][:, :], ACT.Tanh, scale=0.5).then_inc(c.mid[s], 1)
                nc.vector.wait_ge(c.mid[s], e + 1)
                nc.vector.scalar_tensor_tensor(sg[s][:, :], sg[s][:, :], 1.0, self.bank[4 + s][:, :], ALU.add, ALU.mult)\
                    .then_inc(c.fin[s], 1)
                nc.vector.wait_ge(c.fin[s], e + 1)
                acc = mT[:, bass.ds(e, 1), :].rearrange("p a t -> p (a t)")
                if s == 0:
                    m = nc.vector.tensor_scalar(acc, sg[s][:, :], 0.5, None, ALU.mult)
                else:
                    nc.vector.wait_ge(c.ev[s - 1], e + 2)
                    m = nc.vector.scalar_tensor_tensor(acc, sg[s][:, :], 0.5, acc, ALU.mult, ALU.add)
                m.then_inc(c.ev[s], 1)

            c.pe.wait(ready)
            c.dve.wait(ready)
            self.stream(sb, KD, B, 2, KD + KB, load, products, drain)
            c.barrier()

    def mlp(self, l):
        nc, c, A = self.nc, self.c, self.A
        F = 4 * KD // 2
        S = 4
        with nc.Fori(0, 2) as half, ExitStack() as es:
            sb = self.allocator(es)
            uh, ul = sb("hidden_hi", [P, F, T], F32R), sb("hidden_lo", [P, F, T], F32R)
            with ExitStack() as ws:
                sw = self.allocator(ws)
                relu = [sw(f"relu{s}", [P, T]) for s in range(S)]

                def load(i, s, out, width):
                    return [(out[:, :, :], cols_of(A["w_mlp1_2"], l, half * (F * P) + i * (S * P) + s * P, P))]

                def products(s, wh, wl, width):
                    return self.three_passes(self.bank[s], P, [
                        (wh[:, k, :], wl[:, k, :], self.hH[:, k, :], self.hL[:, k, :]) for k in range(KD)])

                def drain(i, s, tile, width):
                    hi = uh[:, bass.ds(tile, 1), :].rearrange("p a t -> p (a t)")
                    lo = ul[:, bass.ds(tile, 1), :].rearrange("p a t -> p (a t)")
                    nc.vector.wait_ge(c.mm[s], i + 2)
                    nc.vector.wait_ge(c.fin[s], i + 1)
                    nc.vector.tensor_scalar(relu[s][:, :], self.bank[s][:, :], 0.0, None, ALU.max).then_inc(c.mid[s], 1)
                    nc.scalar.wait_ge(c.mid[s], i + 1)
                    nc.scalar.activation(relu[s][:, :], relu[s][:, :], ACT.Square).then_inc(c.ev[s], 1)
                    nc.scalar.wait_ge(c.ev[s], i + 2)
                    nc.scalar.copy(hi, relu[s][:, :]).then_inc(c.st[s], 1)
                    nc.gpsimd.wait_ge(c.st[s], i + 1)
                    nc.gpsimd.tensor_tensor(lo, relu[s][:, :], hi.bitcast(F32), ALU.subtract).then_inc(c.fin[s], 1)
                for s in range(S):
                    nc.gpsimd.sem_inc(c.fin[s], 1)
                self.stream(sw, F // S, S, 1, KD, load, products, drain)
                c.barrier()
            self.stream_add(lambda e: A["w_mlp2_2"][l, bass.ds(half * (F * P), F * P), bass.ds(e * P, P)].rearrange("(k p) n -> p k n", p=P),
                            uh, ul, F)

    def second_block(self):
        nc, A = self.nc, self.A
        with nc.Fori(0, DEPTH) as l:
            self.norm(None, A["norm1_g_2"][l])
            self.in_projection(l, A["w_in_2"], C2_WIDTH, self.z2)
            self.gdn(l)
            self.diff(l)
            self.swa(l)
            self.mlstm(l)
            with ExitStack() as es:
                sb = self.allocator(es)
                mT = sb("mixed", [P, KD, T])
                self.gate_branches(l, mT)
                mh, ml = sb("mixed_hi", [P, KD, T], F32R), self.low(mT)[:, :, :]
                for k in range(KD):
                    self.split(mh[:, k, :], ml[:, k, :], mT[:, k, :])
                self.c.barrier()
                self.stream_add(lambda e: cols_of(A["w_out_2"], l, e * P, P), mh, ml, KD)
            self.norm(None, A["norm2_g_2"][l])
            self.mlp(l)
        self.norm(self.xT, A["final_norm_g_2"])


def build(nc, A, table, out):
    cols, _ = constants()
    p = Program(nc, A, out, table, cols)
    p.load_x(A["x"][0])
    p.first_block()
    p.second_block()
    p.store(out[0], p.xT)


NAMES = ["x", "norm_g", "w_in", "fox_b", "conv_w", "conv_b", "conv_ln_g", "conv_ln_b", "conv_pw", "cmp_pe_k",
         "cmp_pe_v", "cmp_k_w1", "cmp_k_w2", "cmp_v_w1", "cmp_v_w2", "w_out", "final_g", "norm1_g_2", "w_in_2",
         "gdn_conv_w_2", "gdn_a_log_2", "gdn_dt_bias_2", "gdn_norm_g_2", "diff_lambda_2", "diff_norm_g_2",
         "swa_sink_2", "mlstm_gate_b_2", "mlstm_norm_g_2", "w_branch_2", "w_gate_2", "w_out_2", "norm2_g_2",
         "w_mlp1_2", "w_mlp2_2", "final_norm_g_2"]


def kernel(**inputs):
    import concourse.bacc as bacc
    from concourse.bass_utils import run_bass_kernel_spmd

    nc = bacc.Bacc("TRN2", target_bir_lowering=False, num_devices=1)
    arrays, A = {}, {}
    for name in NAMES:
        arrays["in_" + name] = np.ascontiguousarray(inputs[name])
        A[name] = nc.dram_tensor("in_" + name, arrays["in_" + name].shape, F32, kind="ExternalInput").ap()
    arrays["table"] = constants()[1]
    table = nc.dram_tensor("table", arrays["table"].shape, F32, kind="ExternalInput").ap()
    out = nc.dram_tensor("out", (1, T, D), F32, kind="ExternalOutput").ap()
    build(nc, A, table, out)
    r = run_bass_kernel_spmd(nc, [arrays], core_ids=[0])
    return r.results[0]["out"]
```

```python
import numpy as np
from contextlib import ExitStack

import concourse.bass as bass
from concourse import mybir

F32 = mybir.dt.float32
F32R = mybir.dt.float32r
ACT = mybir.ActivationFunctionType
ALU = mybir.AluOpType
AX = mybir.AxisListType
ET = mybir.EngineType

P = 128
T = 512
NT = T // P
D = 1024
KD = D // P
DEPTH = 2
EPS = 1e-6
NEG = -1e30
HD = 64

FOX_W, CONV_CH, TAPS, CMP_LEN, CMP_STRIDE = 256, 256, 31, 32, 16
N_CMP = (T - CMP_LEN) // CMP_STRIDE + 1
C1 = {}
_at = 0
for _name, _size in (("fq", 256), ("fk", 256), ("fv", 256), ("ff", 4), ("fg", 256), ("glu", 512), ("cg", 256),
                     ("nq", 512), ("nkc", 128), ("nvc", 128), ("nks", 128), ("nvs", 128), ("nkw", 128),
                     ("nvw", 128), ("ngl", 24), ("ng", 512)):
    C1[_name] = _at
    _at += _size
C1_WIDTH = _at
C2 = {}
_at = 0
for _name, _size in (("a_qkv", 1536), ("a_z", 512), ("a_ab", 16), ("b_q", 512), ("b_k", 512), ("b_v", 512),
                     ("c_q", 512), ("c_k", 128), ("c_v", 128), ("d_q", 256), ("d_k", 256), ("d_v", 512),
                     ("d_if", 16), ("d_o", 512)):
    C2[_name] = _at
    _at += _size

C2_WIDTH = _at

LEVELS = 7


GROUPS = {"all": ("ident", "nident", "later", "far", "up", "low", "ones", "onesrow"),
          "nsa": ("cos1", "sin1", "rot1", "cosc", "sinc", "cmpneg", "cmpone"),
          "rope": ("cos2", "sin2", "rot2", "lam"),
          "gdn": ("levlow", "levup", "sup", "slow", "carryf", "carryb")}


def constants():
    f = np.float32
    i = np.arange(P)[:, None]
    j = np.arange(P)[None, :]
    out = {}
    out["ident"] = (i == j)
    out["nident"] = -(i == j).astype(f)
    out["later"] = np.where(j > i, NEG, 0.0)
    out["far"] = np.where(j < i, NEG, 0.0)
    out["up"] = (j >= i)
    out["low"] = (j <= i)
    out["sup"] = (j > i)
    out["slow"] = (j < i)
    out["ones"] = np.ones((P, P))
    low = [((i // (2 << s)) == (j // (2 << s))) & (i % (2 << s) >= (1 << s)) & (j % (2 << s) < (1 << s))
           for s in range(LEVELS)]
    out["levlow"] = np.concatenate(low, 1)
    out["levup"] = np.concatenate([m.T for m in low], 1)

    def rope(theta, dim, pos):
        half = dim // 2
        inv = (f(theta) ** (-np.arange(0, dim, 2, dtype=f) / f(dim))).astype(f)
        ang = pos.astype(f)[:, None] * inv[None, :]
        cos = np.ones((P, len(pos)), f)
        sin = np.zeros((P, len(pos)), f)
        rot = np.zeros((P, P), f)
        for p in range(P):
            d = p % HD
            if d < dim:
                cos[p], sin[p] = np.cos(ang[:, d % half]), np.sin(ang[:, d % half])
                if d < half:
                    rot[p + half, p] = -1.0
                else:
                    rot[p - half, p] = 1.0
        return cos, sin, rot

    ends = np.arange(N_CMP) * CMP_STRIDE + CMP_LEN - 1
    out["cos1"], out["sin1"], out["rot1"] = rope(500000.0, 16, np.arange(T))
    out["cosc"], out["sinc"], _ = rope(500000.0, 16, ends)
    out["cos2"], out["sin2"], out["rot2"] = rope(10000.0, 64, np.arange(T))
    tq = np.arange(NT)[None, :, None] * P + np.arange(P)[:, None, None]
    seen = ends[None, None, :] <= tq
    out["cmpneg"] = np.where(seen, 0.0, NEG).reshape(P, -1)
    out["cmpone"] = seen.reshape(P, -1)
    t = np.arange(T)[None, :]
    out["carryf"] = np.repeat(t % P != 0, P, 0)
    out["carryb"] = np.repeat(t % P != P - 1, P, 0)
    out["onesrow"] = np.ones((P, T))
    lam = 0.8 - 0.6 * np.exp(-0.3 * np.arange(DEPTH))
    out["lam"] = np.repeat(np.concatenate([lam, 1 - lam])[None, :], P, 0)
    cols, at, parts = {}, 0, []
    for group, names in GROUPS.items():
        first, cols[group] = at, {}
        for name in names:
            a = np.ascontiguousarray(out[name], f)
            cols[group][name] = (at - first, at - first + a.shape[1])
            at += a.shape[1]
            parts.append(a)
        cols[group][""] = (first, at)
    return cols, np.concatenate(parts, 1)


class Queue:

    def __init__(self, eng, sem):
        self.eng, self.sem = eng, sem
        self.fresh()

    def fresh(self):
        self.n, self.seen = 0, {}

    def wait(self, *marks):
        for m in marks:
            if m is None:
                continue
            if isinstance(m, list):
                self.wait(*m)
            elif self.seen.get(m[0], 0) < m[1]:
                self.eng.wait_ge(m[0], m[1])
                self.seen[m[0]] = m[1]

    def __call__(self, instr, *args, after=(), **kw):
        self.wait(*after)
        instr(*args, **kw).then_inc(self.sem, 1)
        self.n += 1
        return (self.sem, self.n)

    def mark(self):
        return (self.sem, self.n)


class Core:

    N_DMA = 40

    def __init__(self, nc):
        self.nc = nc
        names = ["pe", "dve", "act", "pool"] + [f"dma{i}" for i in range(self.N_DMA)]
        self.sems = [nc.alloc_semaphore(n) for n in names]
        self.pe = Queue(nc.tensor, self.sems[0])
        self.dve = Queue(nc.vector, self.sems[1])
        self.act = Queue(nc.scalar, self.sems[2])
        self.pool = Queue(nc.gpsimd, self.sems[3])
        self.sp = Queue(nc.sync, None)
        self.used = 0
        self.ld, self.hi, self.lo, self.mm, self.mid, self.fin, self.ev, self.st = [
            [nc.alloc_semaphore(f"{n}{i}") for i in range(4)] for n in ("ld", "hi", "lo", "mm", "mid", "fin", "ev", "st")]
        self.own = nc.alloc_semaphore("own")
        self.zeroed = range(self.sems[0].num, self.own.num + 1)
        self.barrier()

    def barrier(self):
        for i in range(self.used):
            self.sp.wait((self.sems[4 + i], self.total[i]))
        self.nc.multi_engine_barrier([ET.SP, ET.PE, ET.DVE, ET.Activation, ET.Pool], sems_to_clear=self.zeroed)
        for q in (self.pe, self.dve, self.act, self.pool, self.sp):
            q.fresh()
        self.used, self.total = 0, []

    def dma(self, *pairs, after=(), slow=False, on=None):
        q = on or self.sp
        q.wait(*after)
        sem = self.sems[4 + self.used]
        for out, in_ in pairs:
            q.eng.dma_start(out, in_, allow_slow_non_contiguous=slow).then_inc(sem, 16)
        self.used += 1
        self.total.append(16 * len(pairs))
        return (sem, 16 * len(pairs))

    def products(self, out, terms, after=()):
        self.pe.wait(*after)
        for n, (l, r, *marks) in enumerate(terms):
            self.pe.wait(*marks)
            m = self.nc.tensor.matmul(out, l, r, start=n == 0, stop=n == len(terms) - 1)
        m.then_inc(self.pe.sem, 1)
        self.pe.n += 1
        return self.pe.mark()

    def transposes(self, pairs, ident, after=()):
        self.pe.wait(*after)
        for out, in_ in pairs:
            m = self.nc.tensor.transpose(out, in_, ident[0:in_.shape[0], 0:in_.shape[0]])
        m.then_inc(self.pe.sem, 1)
        self.pe.n += 1
        return self.pe.mark()


def cols_of(w, l, c, n):
    return w[l, :, bass.ds(c, n)].rearrange("(k p) n -> p k n", p=P)


class Program:
    def __init__(self, nc, A, out, C, cols):
        self.nc, self.A, self.out, self.cols = nc, A, out, cols
        self.stage = 0
        self.c = Core(nc)
        sb = nc.alloc_sbuf_tensor
        self.tables, self.place, self.lows = {}, {}, {}
        self.xT = sb("xT", [P, KD, T], F32)
        self.hH = sb("hH", [P, KD, T], F32R)
        self.hL = sb("hL", [P, KD, T], F32R)
        self.yT = self.note(sb("yT", [P, 16, T], F32))
        self.rstd = sb("rstd", [P, T], F32)
        self.one_pass = sb("one_pass_tables", [P, 4, P], F32R)
        self.z1 = nc.dram_tensor("z1", [C1_WIDTH, T], F32, kind="Internal").ap()
        self.z2 = nc.dram_tensor("z2", [C2_WIDTH, T], F32, kind="Internal").ap()
        self.rows, self.rows_R = [nc.dram_tensor(n, [8, T], F32, kind="Internal").ap() for n in ("rows", "rows_R")]
        self.bank = [nc.alloc_psum_tensor(f"bank{i}", [P, T], F32) for i in range(8)]
        self.tables_dram = C
        self.resident = sb("tables", [P, cols["all"][""][1]], F32)

    def allocator(self, stack):
        self.stage += 1
        n = self.stage

        def sb(name, shape, dt=F32):
            return self.note(stack.enter_context(self.nc.sbuf_tensor(f"{name}_{n}", shape, dt)))
        return sb

    def note(self, t):
        self.place[t.name] = self.nc.sbuf_base - 4 * int(np.prod(t.shape[1:]))
        return t

    def low(self, t):
        if t.name not in self.lows:
            self.lows[t.name] = self.nc.alloc_sbuf_tensor_at(f"{t.name}_low", list(t.shape), F32R, offset=self.place[t.name])
        return self.lows[t.name]

    def row(self, h, rows=None):
        return (self.rows if rows is None else rows)[bass.ds(h, 1), :].rearrange("a t -> (a t)").partition_broadcast(P)

    def r(self, name):
        return self.one_pass[:, ("ident", "nident", "later", "far").index(name), :]

    def k(self, name, rows=P):
        return self.tables[name][0:rows, :]

    def load_tables(self, group, dst):
        first, end = self.cols[group][""]
        for name, (a, b) in self.cols[group].items():
            if name:
                self.tables[name] = dst[:, a:b]
        return self.c.dma((dst[:, 0:end - first], self.tables_dram[:, first:end]))

    def group_width(self, group):
        first, end = self.cols[group][""]
        return end - first

    def split(self, hi, lo, x, after=(), high=None, low=None):
        nc, c = self.nc, self.c
        m = c.act(nc.scalar.copy, hi, x, after=after)
        return [m, (low or c.dve)((nc.gpsimd if low is c.pool else nc.vector).tensor_tensor, lo, x, hi.bitcast(F32),
                                  ALU.subtract, after=[m, *after])]

    def norm(self, dst, g_dram):
        with ExitStack() as es:
            for _ in self.norm_pieces(self.allocator(es), dst, g_dram):
                pass
            self.c.barrier()

    def norm_pieces(self, sb, dst, g_dram):
        nc, c = self.nc, self.c
        sq = self.yT
        g = sb("norm_gain", [P, KD])
        eps = sb("norm_eps", [P, 1])
        lg = c.dma((g[:, :], g_dram.rearrange("(k p) -> p k", p=P)), slow=True)
        me = c.dve(nc.vector.memset, eps[:, :], EPS)
        terms = []
        for k in range(KD):
            m = c.act(nc.scalar.activation, sq[:, k, :], self.xT[:, k, :], ACT.Square)
            terms.append((self.k("ones"), sq[:, k, :], m))
        m = c.products(self.bank[0][:, :], terms)
        yield [m]
        m = c.act(nc.scalar.activation, self.rstd[:, :], self.bank[0][:, :], ACT.Ln,
                  bias=eps[:, 0:1], scale=1.0 / D, after=[m, me])
        m = c.act(nc.scalar.activation, self.rstd[:, :], self.rstd[:, :], ACT.Exp, scale=-0.5, after=[m])
        marks = []
        for k in range(KD):
            if dst is not None:
                marks.append(c.dve(nc.vector.scalar_tensor_tensor, dst[:, k, :], self.xT[:, k, :], g[:, k:k + 1],
                                   self.rstd[:, :], ALU.mult, ALU.mult, after=[m, lg]))
            else:
                mk = c.dve(nc.vector.scalar_tensor_tensor, sq[:, k, :], self.xT[:, k, :], g[:, k:k + 1],
                           self.rstd[:, :], ALU.mult, ALU.mult, after=[m, lg])
                marks.append(self.split(self.hH[:, k, :], self.hL[:, k, :], sq[:, k, :], [mk], low=c.pool if k % 2 else None))
        yield marks

    def split_pieces(self, hi, lo, x, n, first):
        for tiles in (range(first), range(first, n)):
            yield [self.split(hi[:, j, :], lo[:, j, :], x[:, j, :]) for j in tiles]

    def twice(self, dst, src):
        return (dst[0:HD, :], src), (dst[HD:P, :], src)

    def stack(self, x, hi, scale, after):
        nc, c = self.nc, self.c
        m = c.act(nc.scalar.activation, hi[:, :], x[:, :], ACT.Copy, scale=scale, after=after)
        return c.dve(nc.vector.scalar_tensor_tensor, hi[HD:P, :], x[HD:P, :], scale, hi[HD:P, :].bitcast(F32),
                     ALU.mult, ALU.subtract, after=[m])

    def to_tokens(self, dst, src, bank, after, n=P):
        m = self.c.transposes([(bank[:, t * n:(t + 1) * n], src[:, t * P:(t + 1) * P]) for t in range(NT)],
                              self.k("ident"), after)
        return self.c.act(self.nc.scalar.copy, dst, bank[:, 0:NT * n].rearrange("p (t n) -> p t n", n=n), after=[m])

    def log_sigmoid(self, x, tmp, after, negate=False):
        nc, c = self.nc, self.c
        m = c.act(nc.scalar.activation, tmp, x, ACT.Abs, after=after)
        m = c.act(nc.scalar.activation, tmp, tmp, ACT.Exp, scale=-1.0, after=[m])
        m = c.act(nc.scalar.activation, tmp, tmp, ACT.Ln, bias=1.0, after=[m])
        return c.dve(nc.vector.scalar_tensor_tensor, x, x, 0.0, tmp, ALU.min, ALU.subtract, after=[m])

    def silu(self, out, x, tmp, after, half=0.5):
        nc, c = self.nc, self.c
        m = c.act(nc.scalar.activation, tmp, x, ACT.Tanh, scale=0.5, after=after)
        m = c.dve(nc.vector.scalar_tensor_tensor, out, tmp, 1.0, x, ALU.add, ALU.mult, after=[m])
        return c.dve(nc.vector.tensor_scalar, out, out, half, None, ALU.mult, after=[m])

    def sigmoid(self, out, x, after):
        nc, c = self.nc, self.c
        m = c.act(nc.scalar.activation, out, x, ACT.Tanh, scale=0.5, after=after)
        return c.dve(nc.vector.tensor_scalar, out, out, 0.5, 0.5, ALU.mult, ALU.add, after=[m])

    def rope(self, x, tmp, bank, rot, cos, sin, after):
        nc, c = self.nc, self.c
        n = x.shape[-1]
        mr = c.products(bank[:, 0:n], [(rot, x)], after)
        ms = c.dve(nc.vector.tensor_tensor, tmp, bank[:, 0:n], sin, ALU.mult, after=[mr])
        mc = c.pool(nc.gpsimd.tensor_tensor, x, x, cos, ALU.mult, after=[mr])
        return c.dve(nc.vector.tensor_tensor, x, x, tmp, ALU.add, after=[ms, mc])

    def attention_buffers(self, es, maps):
        sb = self.allocator(es)
        self.scores = [self.bank[0], self.bank[1], self.bank[2]]
        self.ptp = [self.bank[3], self.bank[6]]
        self.obanks = [self.bank[4], self.bank[5]]
        self.prob = [[sb(f"prob{i}_{m}", [P, T]) for m in range(maps)] for i in range(3)]
        self.pt = [sb(f"prob_T{i}", [P, T]) for i in range(3)]
        self.stat = sb("softmax_stat", [P, 32, maps, 4])
        self.shifted = [sb(f"shifted{i}", [P, T]) for i in range(2)]

    def attention(self, units, ready, beside=None):
        nc, c = self.nc, self.c
        N = len(units)
        assert N <= 32
        c.dve.wait(ready)
        S_free, P_free, PT_free, O_free, shift_free = [None] * 3, [None] * 3, [None] * 2, [None] * 2, [None] * 2
        expd, scaled, transposed, PT_ready, valued = {}, {}, {}, {}, {}
        calls = 0
        for step in range(N + 4):
            if step < N:
                u, ring = units[step], step % 3
                W = u["width"]
                expd[step] = []
                for m, (q, kk) in enumerate(u["maps"]):
                    b = calls % 3
                    sh = calls % 2
                    calls += 1
                    S = self.scores[b]
                    c.pe.wait(ready, S_free[b])
                    terms = [(q, kk[0], 0, W), (q, kk[1], 0, W)] + u["extra"]
                    for n, (l, r, o, w) in enumerate(terms):
                        mm = nc.tensor.matmul(S[:, o:o + w], l, r, start=n == 0, stop=n == len(terms) - 1,
                                              skip_group_check=True)
                    mm.then_inc(c.pe.sem, 1)
                    c.pe.n += 1
                    ms = c.pe.mark()
                    nmax, rsum = self.stat[:, step, m, 0:1], self.stat[:, step, m, 1:2]
                    Pm = self.prob[ring][m][:, 0:W]
                    if u["decay"] is not None:
                        x = self.shifted[sh][:, 0:W]
                        mx = c.dve(nc.vector.tensor_tensor_reduce, out=x, in0=S[:, 0:W],
                                   in1=u["decay"][:, 0:W], scale=1.0, scalar=3e38, op0=ALU.add, op1=ALU.min,
                                   accum_out=nmax, after=[ms, shift_free[sh]])
                        S_free[b] = mx
                        me = c.act(nc.scalar.activation, Pm, x, ACT.Exp, bias=nmax, scale=-1.0,
                                   accum_out=rsum, after=[mx, P_free[ring]])
                        shift_free[sh] = me
                    else:
                        mx = c.dve(nc.vector.tensor_reduce, nmax, S[:, 0:W], AX.X, ALU.max, negate=True, after=[ms])
                        if u["sink"] is not None:
                            mx = c.dve(nc.vector.tensor_scalar, nmax, nmax, u["sink"][1], None, ALU.min, after=[mx])
                        me = c.act(nc.scalar.activation, Pm, S[:, 0:W], ACT.Exp, bias=nmax, scale=1.0,
                                   accum_out=rsum, after=[mx, P_free[ring]])
                        S_free[b] = me
                        if u["sink"] is not None:
                            me = [me, c.act(nc.scalar.activation, self.stat[:, step, m, 3:4], u["sink"][0], ACT.Exp,
                                            bias=nmax, scale=1.0)]
                    expd[step].append(me)
            if 2 <= step < N + 2:
                n = step - 2
                u, ring, s = units[n], n % 3, n % 2
                W = u["width"]
                done = []
                for m in range(len(u["maps"])):
                    rsum, scale = self.stat[:, n, m, 1:2], self.stat[:, n, m, 2:3]
                    mr = expd[n][m]
                    if u["sink"] is not None:
                        mr = c.dve(nc.vector.tensor_tensor, rsum, rsum, self.stat[:, n, m, 3:4], ALU.add, after=[mr])
                    mr = c.dve(nc.vector.reciprocal, scale, rsum, after=[mr])
                    if u["coef"] is not None:
                        mr = c.dve(nc.vector.tensor_tensor, scale, scale, u["coef"], ALU.mult, after=[mr])
                    done.append(mr)
                before = expd[n]
                if u["mix"] is not None:
                    before = [u["mix"](self.prob[ring][0][:, 0:W], self.prob[ring][1][:, 0:W],
                                       [self.stat[:, n, m, 2:3] for m in range(2)], done)]
                scaled[n] = done
                mt = c.transposes([(self.ptp[s][:, i * P:(i + 1) * P], self.prob[ring][0][:, i * P:(i + 1) * P])
                                   for i in range(W // P)], self.k("ident"), after=[before, PT_free[s]])
                P_free[ring] = mt
                if n % 2:
                    PT_ready[n] = c.act(nc.scalar.copy, self.pt[ring][:, 0:W], self.ptp[s][:, 0:W], after=[mt, valued.get(n - 3)])
                else:
                    PT_ready[n] = c.dve(nc.vector.tensor_copy, self.pt[ring][:, 0:W], self.ptp[s][:, 0:W], after=[mt, valued.get(n - 3)])
                PT_free[s] = PT_ready[n]
            if step >= 4:
                n = step - 4
                u, s = units[n], n % 2
                o = self.obanks[s][:, 0:u["values"][0].shape[-1]]
                valued[n] = c.products(o, [(self.pt[n % 3][:, i * P:(i + 1) * P], v) for i, v in enumerate(u["values"])],
                                       after=[PT_ready[n], O_free[s]])
                O_free[s] = u["out"](o, self.stat[:, n, 0, 2:3], [valued[n], scaled[n]])
            if beside is not None:
                next(beside, None)
        for _ in beside or ():
            pass

    def store_T(self, y, n, banks, first, after):
        nc, c = self.nc, self.c
        free = [None] * len(banks)
        for j in range(n):
            b = j % len(banks)
            m = c.transposes([(banks[b][:, t * P:(t + 1) * P], y[:, t, j * P:(j + 1) * P]) for t in range(NT)],
                             self.k("ident"), after=[after, free[b]])
            free[b] = c.dve(nc.vector.tensor_copy, self.yT[:, bass.ds(first + j, 1), :].rearrange("p a t -> p (a t)"),
                            banks[b][:, :], after=[m])

    def fox(self, l):
        nc, c, A = self.nc, self.c, self.A
        with ExitStack() as es:
            sb = self.allocator(es)
            fb = sb("fox_bias", [4, 1])
            f, tmp, crow = sb("f_rows", [4, T]), sb("f_tmp", [4, T]), sb("c_rows", [4, T])
            q2, k2 = [[sb(f"{n}_twice{h}", [P, T]) for h in range(2)] for n in "qk"]
            qs, kh = [[sb(f"{n}{h}", [P, T], F32R) for h in range(2)] for n in ("q_stacked", "k_hi")]
            vf, gf = sb("v_rows", [P, T]), sb("gate_rows", [P, T])
            v, g, gt, y = [sb(n, [P, NT, P]) for n in ("v_tok", "gate", "gate_tmp", "y_tok")]
            cpair = sb("c_pair", [P, 2, T])
            self.attention_buffers(es, 1)
            ld = c.dma((f[:, :], self.z1[C1["ff"]:C1["ff"] + 4, :]), (fb[:, :], A["fox_b"][l].unsqueeze(1)), slow=True)
            m = c.dve(nc.vector.tensor_scalar, f[:, :], f[:, :], fb[:, 0:1], None, ALU.add, after=[ld])
            m = self.log_sigmoid(f[:, :], tmp[:, :], [m])
            m = c.dve(nc.vector.tensor_tensor_scan, crow[:, :], self.k("onesrow", 4), f[:, :], 0.0, ALU.mult, ALU.add, after=[m])
            c.dma((self.rows[0:4, :], crow[:, :]), after=[m])
            c.barrier()
            z = self.z1
            with nc.Fori(0, 2) as pair:
                lq, lk = [[c.dma(*self.twice(x[h], z[bass.ds(pair * P + C1[n] + h * HD, HD), :])) for h in range(2)]
                          for x, n in ((q2, "fq"), (k2, "fk"))]
                lc = [c.dma((cpair[:, h, :], self.row(pair * 2 + h))) for h in range(2)]
                lv, lg = [c.dma((x[:, :], z[bass.ds(pair * P + C1[n], P), :])) for x, n in ((vf, "fv"), (gf, "fg"))]
                ready = []
                for h in range(2):
                    ready.append(self.split(kh[h][:, :], self.low(k2[h])[:, :], k2[h][:, :], [lk[h]]))
                    ready.append(self.stack(q2[h], qs[h], -HD ** -0.5, [lq[h]]))
                mv = self.to_tokens(v[:, :, :], vf, self.bank[6], [lv])
                m = c.transposes([(self.bank[7][:, t * P:(t + 1) * P], gf[:, t * P:(t + 1) * P]) for t in range(NT)],
                                 self.k("ident"), [lg])
                fl = lambda x: x[:, :, :].rearrange("p t n -> p (t n)")
                mg = self.silu(fl(g), self.bank[7][:, :], fl(gt), [m])
                units = []
                for h in range(2):
                    for t in range(NT):
                        def out(o, rinv, marks, t=t, cs=slice(h * HD, h * HD + HD)):
                            return c.dve(nc.vector.scalar_tensor_tensor, y[:, t, cs], o, rinv, g[:, t, cs],
                                         ALU.mult, ALU.mult, after=[*marks, mg])
                        W = (t + 1) * P
                        units.append(dict(
                            maps=[(qs[h][:, t * P:(t + 1) * P], (kh[h][:, 0:W], self.low(k2[h])[:, 0:W]))], width=W,
                            extra=[(self.r("nident"), self.r("later"), t * P, P)], decay=cpair[:, h, :],
                            sink=None, coef=None, mix=None,
                            values=[v[:, i, h * HD:h * HD + HD] for i in range(t + 1)], out=out))
                self.attention(units, [ready, mv, mg, lc])
                self.store_T(y, 1, [self.bank[6]], pair, [c.dve.mark()])
                c.barrier()

    def conv(self, l, beside):
        nc, c, A = self.nc, self.c, self.A
        CT = CONV_CH // P
        PAD = TAPS - 1
        with ExitStack() as es:
            sb = self.allocator(es)
            za, zb, zg = [sb(n, [P, CT, T]) for n in ("glu_a", "glu_b", "conv_gate_rows")]
            wp = sb("w_pointwise", [P, CT, CONV_CH])
            taps = sb("taps", [P, TAPS, CT])
            small = sb("conv_params", [P, 3, CT])
            eps = sb("conv_eps", [P, 1])
            gl = sb("glu_padded", [P, CT, PAD + T])
            acc = sb("conv_acc", [P, CT, T])
            sq = sb("conv_sq", [P, CT, T])
            mean, rstd = sb("conv_mean", [P, T]), sb("conv_rstd", [P, T])
            gate, gtmp, y = [sb(n, [P, NT, CONV_CH]) for n in ("conv_gate", "conv_gate_tmp", "conv_y")]
            lw = [c.dma((x[:, :, :], self.z1[C1[n] + o:C1[n] + o + CONV_CH, :].rearrange("(j p) t -> p j t", p=P)))
                  for x, n, o in ((za, "glu", 0), (zb, "glu", CONV_CH), (zg, "cg", 0))]
            lp = c.dma((wp[:, :, :], A["conv_pw"][l].rearrange("(k p) n -> p k n", p=P)))
            lt = c.dma(*[(taps[:, :, j], A["conv_w"][l, :, j * P:(j + 1) * P].rearrange("w p -> p w")) for j in range(CT)],
                       *[(small[:, n, :], A[name][l].rearrange("(j p) -> p j", p=P))
                         for n, name in enumerate(("conv_b", "conv_ln_g", "conv_ln_b"))], slow=True)
            mz = [c.dve(nc.vector.memset, gl[:, :, 0:PAD], 0.0), c.dve(nc.vector.memset, eps[:, :], EPS)]
            ready = []
            for j in range(CT):
                m = c.act(nc.scalar.activation, sq[:, j, :], zb[:, j, :], ACT.Tanh, scale=0.5, after=[lw[1]])
                m = c.dve(nc.vector.tensor_scalar, sq[:, j, :], sq[:, j, :], 0.5, 0.5, ALU.mult, ALU.add, after=[m])
                ready.append(c.dve(nc.vector.tensor_tensor, gl[:, j, PAD:], sq[:, j, :], za[:, j, :], ALU.mult, after=[m, lw[0]]))
            for i in range(NT):
                bg = self.bank[4 + i // 2]
                m = c.transposes([(bg[:, (i % 2) * 256 + j * P:(i % 2) * 256 + (j + 1) * P], zg[:, j, i * P:(i + 1) * P])
                                  for j in range(CT)], self.k("ident"), [lw[2]])
            mt = [c.act(nc.scalar.activation, gtmp[:, 2 * i:2 * i + 2, :].rearrange("p a n -> p (a n)"),
                        self.bank[4 + i][:, :], ACT.Tanh, scale=0.5, after=[m]) for i in range(2)]
            marks = [[ready[j], mz, lt] for j in range(CT)]
            side = beside(sb)
            next(side)
            for w in range(TAPS):
                if w == TAPS // 5 or w > TAPS // 2:
                    next(side, None)
                for j in range(CT):
                    src = gl[:, j, w:w + T]
                    if w == 0:
                        marks[j] = [c.dve(nc.vector.tensor_scalar, acc[:, j, :], src, taps[:, w, j:j + 1],
                                          small[:, 0, j:j + 1], ALU.mult, ALU.add, after=marks[j])]
                    else:
                        marks[j] = [c.dve(nc.vector.scalar_tensor_tensor, acc[:, j, :], src, taps[:, w, j:j + 1],
                                          acc[:, j, :], ALU.mult, ALU.add, after=marks[j])]
            for _ in side:
                pass
            side_done = [c.dve.mark(), c.act.mark()]
            for i in range(2):
                mg = c.dve(nc.vector.scalar_tensor_tensor, gate[:, 2 * i:2 * i + 2, :].rearrange("p a n -> p (a n)"),
                           gtmp[:, 2 * i:2 * i + 2, :].rearrange("p a n -> p (a n)"), 1.0, self.bank[4 + i][:, :],
                           ALU.add, ALU.mult, after=mt)
            m = c.products(self.bank[0][:, :], [(self.k("ones"), acc[:, j, :]) for j in range(CT)], [marks, side_done])
            mm = c.act(nc.scalar.activation, mean[:, :], self.bank[0][:, :], ACT.Copy, scale=1.0 / CONV_CH, after=[m])
            md = [c.dve(nc.vector.tensor_tensor, acc[:, j, :], acc[:, j, :], mean[:, :], ALU.subtract, after=[mm])
                  for j in range(CT)]
            m = [c.act(nc.scalar.activation, sq[:, j, :], acc[:, j, :], ACT.Square, after=[md[j]]) for j in range(CT)]
            m = c.products(self.bank[1][:, :], [(self.k("ones"), sq[:, j, :]) for j in range(CT)], m)
            m = c.act(nc.scalar.activation, rstd[:, :], self.bank[1][:, :], ACT.Ln, bias=eps[:, 0:1],
                      scale=1.0 / CONV_CH, after=[m])
            m = c.act(nc.scalar.activation, rstd[:, :], rstd[:, :], ACT.Exp, scale=-0.5, after=[m])
            ms = []
            for j in range(CT):
                a = c.dve(nc.vector.scalar_tensor_tensor, acc[:, j, :], acc[:, j, :], small[:, 1, j:j + 1], rstd[:, :],
                          ALU.mult, ALU.mult, after=[m])
                a = c.dve(nc.vector.tensor_scalar, acc[:, j, :], acc[:, j, :], small[:, 2, j:j + 1], None, ALU.add, after=[a])
                a = self.silu(acc[:, j, :], acc[:, j, :], sq[:, j, :], [a])
                ms.append(a)
            for i in range(NT):
                m = c.products(self.bank[2 + i // 2][:, (i % 2) * 256:(i % 2) * 256 + 256],
                               [(acc[:, j, i * P:(i + 1) * P], wp[:, j, :]) for j in range(CT)], [ms, lp])
            for i in range(NT):
                md = c.dve(nc.vector.scalar_tensor_tensor, y[:, i, :], self.bank[2 + i // 2][:, (i % 2) * 256:(i % 2) * 256 + 256],
                          0.5, gate[:, i, :], ALU.mult, ALU.mult, after=[m, mg])
            for j in range(CT):
                b = self.bank[6 + j]
                mt = c.transposes([(b[:, t * P:(t + 1) * P], y[:, t, j * P:(j + 1) * P]) for t in range(NT)],
                                  self.k("ident"), after=[md])
                c.dve(nc.vector.tensor_copy, self.yT[:, FOX_W // P + j, :], b[:, :], after=[mt])
            c.barrier()

    def compress(self, l, kcmp, vcmp, table, sb):
        nc, c, A = self.nc, self.c, self.A
        M = CMP_LEN // 2
        N = N_CMP
        w1 = [sb(f"cmp_w1_{i}", [P, M, 256]) for i in range(2)]
        w2 = [sb(f"cmp_w2_{i}", [P, 2, 2, HD]) for i in range(2)]
        pe = [sb(f"cmp_pe{i}", [P, M]) for i in range(2)]
        two = sb("two_tokens", [P, 4, T])
        kc = sb("k_cmp_full", [P, 2, N + 1])
        blk = [sb(f"cmp_blocks{i}", [P, M, 2, N]) for i in range(2)]
        hid, cube, hidT = [[sb(f"{n}{i}", [P, 2, 2 * N]) for i in range(2)] for n in ("hid", "cube", "hid_gelu")]
        rtmp = sb("cmp_rope_tmp", [P, 2, N])
        rows, w1_in, small = [], [], []
        for i, (col, kv) in enumerate((("nkc", "k"), ("nvc", "v"))):
            rows.append(c.dma(*[(two[r * HD:(r + 1) * HD, 2 * i + g, 0:T - r], self.z1[C1[col] + g * HD:C1[col] + (g + 1) * HD, r:T])
                                for g in range(2) for r in range(2)]))
            w2d = A[f"cmp_{kv}_w2"][l].rearrange("(j p) o -> p j o", p=P)
            small.append(c.dma((w2[i][:, :, 0, :], w2d), (w2[i][:, :, 1, :], w2d),
                               (pe[i][0:HD, :], A[f"cmp_pe_{kv}"][l].rearrange("(m r) d -> r d m", r=2)[0]),
                               (pe[i][HD:P, :], A[f"cmp_pe_{kv}"][l].rearrange("(m r) d -> r d m", r=2)[1]), slow=True))
            w1_in.append(c.dma((w1[i][:, :, :], A[f"cmp_{kv}_w1"][l].rearrange("(m p) h -> p m h", p=P))))
        yield
        done = []
        for i in range(2):
            mb = []
            for g in range(2):
                for q in range(CMP_LEN // CMP_STRIDE):
                    h = M // 2
                    src = two[:, 2 * i + g, CMP_STRIDE * q:CMP_STRIDE * q + CMP_STRIDE * N].rearrange(
                        "p (n m r) -> p m n r", m=h, r=2)[:, :, :, 0]
                    mb.append(c.dve(nc.vector.tensor_tensor, blk[i][:, q * h:(q + 1) * h, g, :], src,
                                    pe[i][:, q * h:(q + 1) * h].unsqueeze(2).to_broadcast([P, h, N]), ALU.add,
                                    after=[rows[i], small[i]]))
            for j in range(2):
                m = c.products(self.bank[2 + i][:, j * 2 * N:(j + 1) * 2 * N],
                               [(w1[i][:, q, j * P:(j + 1) * P], blk[i][:, q, :, :].rearrange("p g n -> p (g n)"))
                                for q in range(M)], [w1_in[i], mb])
            done.append(m)
        yield
        mz = c.dve(nc.vector.memset, kc[:, :, N:N + 1], 0.0)
        for i in range(2):
            x = self.bank[2 + i][:, 0:4 * N].rearrange("p (j n) -> p j n", j=2)
            m = c.act(nc.scalar.activation, cube[i][:, :, :], x, ACT.Square, after=[done[i]])
            yield
            m = c.dve(nc.vector.tensor_scalar, cube[i][:, :, :], cube[i][:, :, :], 0.044715, 1.0, ALU.mult, ALU.add, after=[m])
            m = c.dve(nc.vector.tensor_tensor, cube[i][:, :, :], cube[i][:, :, :], x, ALU.mult, after=[m])
            m = c.act(nc.scalar.activation, hid[i][:, :, :], cube[i][:, :, :], ACT.Tanh, scale=float(np.sqrt(2 / np.pi)), after=[m])
            yield
            m = c.dve(nc.vector.scalar_tensor_tensor, hidT[i][:, :, :], hid[i][:, :, :], 1.0, x, ALU.add, ALU.mult, after=[m])
            m = c.dve(nc.vector.tensor_scalar, hidT[i][:, :, :], hidT[i][:, :, :], 0.5, None, ALU.mult, after=[m])
            yield
            if i == 0:
                m = c.products(self.bank[6][:, 0:2 * N],
                               [(w2[i][:, j, :, :].rearrange("p r d -> p (r d)"), hidT[i][:, j, :]) for j in range(2)], [m, small[i]])
                mk = c.act(nc.scalar.copy, kc[:, :, 0:N], self.bank[6][:, 0:2 * N].rearrange("p (g n) -> p g n", g=2), after=[m])
                for g in range(2):
                    yield
                    mk = self.rope(kc[:, g, 0:N], rtmp[:, g, :], self.bank[6], self.k("rot1"), self.k("cosc"),
                                   self.k("sinc"), [mk, table])
                    self.split(kcmp[0][:, g, :], kcmp[1][:, g, :], kc[:, g, :], [mk, mz])
            else:
                for g in range(2):
                    m2 = c.products(self.bank[7][0:N, g * HD:(g + 1) * HD],
                                    [(hidT[i][:, j, g * N:(g + 1) * N], w2[i][:, j, 0, :]) for j in range(2)], [m, small[i]])
                c.act(nc.scalar.copy, vcmp[:, :, :].rearrange("p g d -> p (g d)"), self.bank[7][0:N, 0:2 * HD], after=[m2])

    def conv_and_nsa(self, l):
        with ExitStack() as es:
            sb = self.allocator(es)
            kcmp = [sb(f"k_cmp_{n}", [P, 2, N_CMP + 1], F32R) for n in ("hi", "lo")]
            vcmp = sb("v_cmp", [N_CMP, 2, HD])
            table = self.load_tables("nsa", sb("nsa_tables", [P, self.group_width("nsa")]))
            self.conv(l, lambda buffers: self.compress(l, kcmp, vcmp, table, buffers))
            self.nsa(l, kcmp, vcmp)

    def nsa(self, l, kcmp, vcmp):
        nc, c, A = self.nc, self.c, self.A
        N = N_CMP
        H = 4
        with ExitStack() as es:
            sb = self.allocator(es)
            gl = sb("branch_gates", [P, NT, 24])
            glr = sb("branch_gate_rows", [24, T])
            q2 = [sb(f"q_twice{h}", [P, T]) for h in range(H)]
            k2 = [sb(f"k_twice{b}", [P, T]) for b in range(2)]
            qs = [sb(f"q_stacked{h}", [P, T], F32R) for h in range(H)]
            kh = [sb(f"k_hi{b}", [P, T], F32R) for b in range(2)]
            rt = [sb(f"rope_tmp{i}", [P, T]) for i in range(2)]
            vf, gf = sb("v_rows", [P, T]), [sb(f"gate_rows{i}", [P, T]) for i in range(2)]
            v = sb("v_tok", [P, NT, 2 * HD])
            gate, y = sb("gate", [P, NT, 2, P]), sb("y_tok", [P, NT, 2 * P])
            gtmp = sb("gate_tmp", [P, NT, P])
            kc = [sb(f"k_cmp_group{i}", [P, N + 1], F32R) for i in range(2)]
            vc, gg = sb("v_cmp_group", [N, HD]), sb("gates_group", [P, NT, 12])
            pc, pcT, y_cmp = sb("p_cmp", [P, H, NT * N]), sb("p_cmpT", [N, NT, P]), sb("y_cmp", [P, NT, 2 * P])
            cst = sb("cmp_stat", [P, 3, H, NT])
            coef = sb("coef", [P, H, NT])
            self.attention_buffers(es, 1)
            z = self.z1
            ld = c.dma((glr[:, :], z[C1["ngl"]:C1["ngl"] + 24, :]))
            m = self.to_tokens(gl[:, :, :], glr, self.bank[0], [ld], 24)
            self.sigmoid(gl[:, :, :], gl[:, :, :], [m])
            c.barrier()
            with nc.Fori(0, 2) as grp:
                lk = [c.dma(*self.twice(k2[i], z[bass.ds(grp * HD + C1[n], HD), :])) for i, n in enumerate(("nks", "nkw"))]
                lq = [c.dma(*self.twice(q2[h], z[bass.ds(grp * 256 + C1["nq"] + h * HD, HD), :])) for h in range(H)]
                lv = c.dma((vf[0:HD, :], z[bass.ds(grp * HD + C1["nvs"], HD), :]), (vf[HD:P, :], z[bass.ds(grp * HD + C1["nvw"], HD), :]))
                lg = [c.dma((gf[i][:, :], z[bass.ds(grp * 256 + C1["ng"] + i * P, P), :])) for i in range(2)]
                one = lambda x: x[:, bass.ds(grp, 1), :].rearrange("p a n -> p (a n)")
                mg1 = [c.dve(nc.vector.tensor_copy, kc[0][:, :], one(kcmp[0])),
                       c.dve(nc.vector.tensor_copy, kc[1][:, :], one(kcmp[1])),
                       c.dve(nc.vector.tensor_copy, vc[:, :], one(vcmp)),
                       c.dve(nc.vector.tensor_copy, gg[:, :, :], gl[:, :, bass.ds(grp * 12, 12)])]
                rot = (self.k("rot1"), self.k("cos1"), self.k("sin1"))
                ready, tmp_free = [], [None, None]
                n = 0
                for i in range(2):
                    m = self.rope(k2[i][:, :], rt[n % 2][:, :], self.bank[n % 2], *rot, [lk[i], tmp_free[n % 2]])
                    tmp_free[n % 2] = m
                    ready.append(self.split(kh[i][:, :], self.low(k2[i])[:, :], k2[i][:, :], [m]))
                    n += 1
                for h in range(H):
                    m = self.rope(q2[h][:, :], rt[n % 2][:, :], self.bank[n % 2], *rot, [lq[h], tmp_free[n % 2]])
                    tmp_free[n % 2] = m
                    ready.append(self.stack(q2[h], qs[h], HD ** -0.5, [m]))
                    n += 1
                mv = self.to_tokens(v[:, :, :], vf, self.bank[6], [lv])
                mg = None
                for i in range(2):
                    m = c.transposes([(self.bank[7][:, t * P:(t + 1) * P], gf[i][:, t * P:(t + 1) * P]) for t in range(NT)],
                                     self.k("ident"), [lg[i], mg])
                    mg = self.silu(gate[:, :, i, :], self.bank[7][:, :].rearrange("p (t n) -> p t n", n=P), gtmp[:, :, :], [m])
                def compressed():
                    bank, m = self.bank[7], None
                    for h in range(H):
                        for t in range(NT):
                            at = (h * NT + t) * (N + 1)
                            m = c.products(bank[:, at:at + N + 1], [(qs[h][:, t * P:(t + 1) * P], kc[0][:, :]),
                                                                    (qs[h][:, t * P:(t + 1) * P], kc[1][:, :])], [ready, mg1, mg])
                        yield
                    neg, one = self.k("cmpneg").rearrange("p (t n) -> p t n", n=N).unsqueeze(1), self.k("cmpone").unsqueeze(1)
                    m = c.dve(nc.vector.tensor_tensor, pc[:, :, :].rearrange("p h (t n) -> p h t n", n=N),
                              bank[:, :].rearrange("p (h t n) -> p h t n", h=H, t=NT)[:, :, :, 0:N],
                              neg.to_broadcast([P, H, NT, N]), ALU.add, after=[m])
                    yield
                    p4 = pc[:, :, :].rearrange("p h (t n) -> p (h t) n", n=N)
                    st = [cst[:, i, :, :].rearrange("p h t -> p (h t)") for i in range(3)]
                    m = c.dve(nc.vector.tensor_reduce, st[0], p4, AX.X, ALU.max, after=[m])
                    yield
                    m = c.dve(nc.vector.tensor_tensor, p4, p4, st[0].unsqueeze(2).to_broadcast([P, H * NT, N]), ALU.subtract, after=[m])
                    yield
                    m = c.act(nc.scalar.activation, p4, p4, ACT.Exp, after=[m])
                    yield
                    m = c.dve(nc.vector.tensor_reduce, st[1], p4, AX.X, ALU.add, after=[m])
                    yield
                    mp = c.dve(nc.vector.tensor_tensor, pc[:, :, :], pc[:, :, :], one.to_broadcast([P, H, NT * N]), ALU.mult, after=[m])
                    mi = c.dve(nc.vector.reciprocal, st[2], st[1], after=[m])
                    yield
                    mf = c.dve(nc.vector.tensor_tensor, coef[:, :, :], gg[:, :, :].rearrange("p t (h b) -> p h t b", b=3)[:, :, :, 0],
                               cst[:, 2, :, :], ALU.mult, after=[mi, mg1])
                    my = None
                    for h in range(H):
                        m = c.transposes([(bank[0:N, t * P:(t + 1) * P], pc[:, h, t * N:(t + 1) * N]) for t in range(NT)],
                                         self.k("ident"), after=[mp, my])
                        yield
                        m = c.act(nc.scalar.copy, pcT[:, :, :].rearrange("p t n -> p (t n)"), bank[0:N, :], after=[m])
                        yield
                        for t in range(NT):
                            m2 = c.products(bank[:, t * HD:(t + 1) * HD], [(pcT[:, t, :], vc[:, :])], [m, mg1])
                        yield
                        my = c.dve(nc.vector.tensor_tensor, y_cmp[:, :, h * HD:(h + 1) * HD],
                                   bank[:, 0:NT * HD].rearrange("p (t d) -> p t d", d=HD),
                                   coef[:, h, :].unsqueeze(2).to_broadcast([P, NT, HD]), ALU.mult, after=[m2, mf])
                        yield

                units = []
                n = 0
                for br in range(2):
                    for h in range(H):
                        for t in range(NT):
                            W = (t + 1) * P

                            def out(o, scale, marks, h=h, t=t, br=br):
                                w = y[:, t, h * HD:(h + 1) * HD]
                                if br == 0:
                                    return c.dve(nc.vector.tensor_scalar, w, o, scale, None, ALU.mult, after=marks)
                                return c.dve(nc.vector.scalar_tensor_tensor, w, o, scale, w, ALU.mult, ALU.add, after=marks)
                            units.append(dict(
                                maps=[(qs[h][:, t * P:(t + 1) * P], (kh[br][:, 0:W], self.low(k2[br])[:, 0:W]))], width=W,
                                extra=[(self.r("ident"), self.r("later"), t * P, P)], decay=None, sink=None,
                                coef=gg[:, t, 3 * h + 1 + br:3 * h + 2 + br], mix=None,
                                values=[v[:, i, br * HD:(br + 1) * HD] for i in range(t + 1)], out=out))
                self.attention(units, [ready, mv, mg], compressed())
                m = c.dve(nc.vector.tensor_tensor, y[:, :, :], y[:, :, :], y_cmp[:, :, :], ALU.add, after=[c.dve.mark()])
                m = c.dve(nc.vector.tensor_tensor, y[:, :, :], y[:, :, :], gate[:, :, :, :].rearrange("p t i n -> p t (i n)"),
                          ALU.mult, after=[m])
                self.store_T(y, 2, [self.bank[6], self.bank[7]], grp * 2 + 4, [m])
                c.barrier()

    def stream(self, sb, trips, slots, parts, kt, load, products, drain, tail=(), prepare=()):
        nc, c = self.nc, self.c
        w = [sb(f"w{s}", [P, kt, P]) for s in range(slots)]
        wh = [sb(f"w_hi{s}", [P, kt, P], F32R) for s in range(slots)]
        for s in range(slots):
            nc.tensor.sem_inc(c.mm[s], 1)
            nc.vector.sem_inc(c.ev[s], 1)

        def fetch(i, s, width=P):
            nc.sync.wait_ge(c.mm[s], i + 1)
            for out, in_ in load(i, s, w[s], width):
                nc.sync.dma_start(out, in_).then_inc(c.ld[s], 16)

        def split(i, s, width=P):
            nc.scalar.wait_ge(c.ld[s], i * (16 * parts) + 16 * parts)
            nc.scalar.copy(wh[s][:, :, 0:width], w[s][:, :, 0:width]).then_inc(c.hi[s], 1)
            nc.vector.wait_ge(c.hi[s], i + 1)
            nc.vector.tensor_tensor(self.low(w[s])[:, :, 0:width], w[s][:, :, 0:width],
                                    wh[s][:, :, 0:width].bitcast(F32), ALU.subtract).then_inc(c.lo[s], 1)

        def multiply(i, s, width=P):
            nc.tensor.wait_ge(c.lo[s], i + 1)
            nc.tensor.wait_ge(c.ev[s], i + 1)
            products(s, wh[s], self.low(w[s])[:, :, :], width).then_inc(c.mm[s], 1)

        tiles = [(trips - 1, s, P) for s in range(slots)] + [(trips + j // slots, j % slots, wd) for j, wd in enumerate(tail)]
        ahead = slots - 1
        for s in range(ahead):
            fetch(0, s)
        prepare = iter(prepare)
        made = [next(prepare, None)]
        split(0, 0)
        made += list(prepare)
        c.pe.wait(made)
        with nc.Fori(0, trips - 1) as i:
            for s in range(slots):
                fetch(i + (s + ahead) // slots, (s + ahead) % slots)
                split(i + (s + 1) // slots, (s + 1) % slots)
                multiply(i, s)
                drain(i, s, i * slots + s, P)
        for n, (i, s, wd) in enumerate(tiles):
            if n + ahead < len(tiles):
                fetch(*tiles[n + ahead])
            if n + 1 < len(tiles):
                split(*tiles[n + 1])
            multiply(i, s, wd)
            drain(i, s, i * slots + s, wd)

    def three_passes(self, bank, width, terms):
        nc = self.nc
        for n, (wh, wl, xh, xl) in enumerate(terms):
            nc.tensor.matmul(bank[0:width, :], wh, xh, start=n == 0, stop=False)
            nc.tensor.matmul(bank[0:width, :], wh, xl, start=False, stop=False)
            m = nc.tensor.matmul(bank[0:width, :], wl, xh, start=False, stop=n == len(terms) - 1)
        return m

    def in_projection(self, l, g_dram, w_in, n, z):
        nc, c = self.nc, self.c
        S = 4
        full = n // P
        trips = full // S
        tail = [P] * (full - trips * S) + [n % P]
        with ExitStack() as es:
            sb = self.allocator(es)
            zt = [sb(f"z_tile{s}", [P, T]) for s in range(S)]

            def products(s, wh, wl, width):
                return self.three_passes(self.bank[s], width, [
                    (wh[:, k, 0:width], wl[:, k, 0:width], self.hH[:, k, :], self.hL[:, k, :]) for k in range(KD)])

            def load(i, s, out, width):
                return [(out[:, :, 0:width], w_in[l, :, bass.ds(i * (S * P) + s * P, width)].rearrange("(k p) n -> p k n", p=P))]

            def drain(i, s, tile, width):
                nc.scalar.wait_ge(c.mm[s], i + 2)
                nc.scalar.wait_ge(c.st[s], i * 16 + 1)
                nc.scalar.copy(zt[s][0:width, :], self.bank[s][0:width, :]).then_inc(c.ev[s], 1)
                nc.scalar.wait_ge(c.ev[s], i + 2)
                nc.scalar.dma_start(z[bass.ds(tile * P, width), :], zt[s][0:width, :]).then_inc(c.st[s], 16)

            for s in range(S):
                nc.gpsimd.sem_inc(c.st[s], 1)
            self.stream(sb, trips, S, 1, KD, load, products, drain, tail, self.norm_pieces(sb, None, g_dram))
            for s in range(S):
                stored = trips + sum(1 for j in range(len(tail)) if j % S == s)
                nc.gpsimd.wait_ge(c.st[s], 16 * stored + 1)
            c.barrier()

    def stream_add(self, load_cols, xh, xl, kt, slots, prepare=()):
        nc, c = self.nc, self.c
        with ExitStack() as es:
            sb = self.allocator(es)

            def load(i, s, out, width):
                return [(out[:, :, :], load_cols(i * slots + s))]

            def products(s, wh, wl, width):
                return self.three_passes(self.bank[s], P, [(wh[:, k, :], wl[:, k, :], xh[:, k, :], xl[:, k, :]) for k in range(kt)])

            def drain(i, s, tile, width):
                nc.vector.wait_ge(c.mm[s], i + 2)
                x = self.xT[:, bass.ds(tile, 1), :].rearrange("p a t -> p (a t)")
                nc.vector.tensor_tensor(x, x, self.bank[s][:, :], ALU.add).then_inc(c.ev[s], 1)
            self.stream(sb, KD // slots, slots, 1, kt, load, products, drain, prepare=prepare)
            c.barrier()

    def load_x(self, x):
        nc, c = self.nc, self.c
        with ExitStack() as es:
            xt = self.allocator(es)("x_tok", [P, NT, D])
            lc = self.load_tables("all", self.resident)
            for name in ("ident", "nident", "later", "far"):
                c.dve(nc.vector.tensor_copy, self.r(name), self.k(name), after=[lc])
            lx = c.dma((xt[:, :, :], x.rearrange("(t p) d -> p t d", p=P)))
            for k in range(KD):
                m = c.transposes([(self.bank[k][:, t * P:(t + 1) * P], xt[:, t, k * P:(k + 1) * P]) for t in range(NT)],
                                 self.k("ident"), after=[lc, lx])
                c.dve(nc.vector.tensor_copy, self.xT[:, k, :], self.bank[k][:, :], after=[m])
            c.barrier()

    def store(self, out, src):
        nc, c = self.nc, self.c
        with ExitStack() as es:
            xt = self.allocator(es)("x_tok", [P, NT, D])
            for k in range(KD):
                m = c.transposes([(self.bank[k][:, t * P:(t + 1) * P], src[:, k, t * P:(t + 1) * P]) for t in range(NT)],
                                 self.k("ident"))
                for t in range(NT):
                    m2 = c.dve(nc.vector.tensor_copy, xt[:, t, k * P:(k + 1) * P], self.bank[k][:, t * P:(t + 1) * P], after=[m])
            c.dma((out.rearrange("(t p) d -> p t d", p=P), xt[:, :, :]), after=[m2])
            c.barrier()

    def first_block(self):
        A = self.A
        with self.nc.Fori(0, DEPTH) as l:
            self.in_projection(l, A["norm_g"][l], A["w_in"], C1_WIDTH, self.z1)
            self.fox(l)
            self.conv_and_nsa(l)
            with ExitStack() as es:
                yh, yl = self.allocator(es)("y_hi", [P, KD, T], F32R), self.low(self.yT)
                self.stream_add(lambda e: cols_of(A["w_out"], l, e * P, P), yh, yl, KD, 4,
                                self.split_pieces(yh, yl, self.yT, KD, 5))
        self.norm(self.xT, A["final_g"])

    def scan_rows(self, out, rows, keep, op, backward, after):
        nc, c = self.nc, self.c
        if backward:
            out, rows, keep = out[:, ::-1], rows[:, ::-1], keep[:, ::-1]
        return c.dve(nc.vector.tensor_tensor_scan, out, keep, rows, 0.0, ALU.mult, op, after=after)

    def to_cols(self, dst, rows, bank, after):
        n = rows.shape[0]
        m = self.c.transposes([(bank[:, t * n:(t + 1) * n], rows[:, t * P:(t + 1) * P]) for t in range(NT)],
                              self.k("ident"), after)
        return self.c.dve(self.nc.vector.tensor_copy, dst, bank[:, 0:NT * n].rearrange("p (t n) -> p t n", n=n), after=[m])

    def norm_blocks(self, y, n, gain, sq, ss, eps, after):
        nc, c = self.nc, self.c
        for i in range(n):
            m = c.act(nc.scalar.activation, sq[:, i, :], y[:, i, :], ACT.Square, accum_out=ss[:, i:i + 1], after=after)
        m = c.act(nc.scalar.activation, ss[:, 0:n], ss[:, 0:n], ACT.Ln, bias=eps, scale=1.0 / P, after=[m])
        m = c.act(nc.scalar.activation, ss[:, 0:n], ss[:, 0:n], ACT.Exp, scale=-0.5, after=[m])
        for i in range(n):
            m2 = c.dve(nc.vector.scalar_tensor_tensor, y[:, i, :], y[:, i, :], ss[:, i:i + 1], gain(i), ALU.mult, ALU.mult,
                       after=[m, *after])
        return m2

    def gdn(self, l, beside):
        nc, c, A = self.nc, self.c, self.A
        H = 4
        W4 = [P, NT, P]
        with ExitStack() as es:
            sb = self.allocator(es)
            par = [sb(f"gdn_params{d}", [H, 2]) for d in range(2)]
            q5 = sb("chunk_scalars", [P, 6, NT, 2, H])
            g = sb("log_decay", [P, NT, 8])
            tot = sb("chunk_total", [P, NT, 8])
            ar, br, tmp, gcr = [[sb(f"{n}_rows{d}", [H, T]) for d in range(2)] for n in ("a", "beta", "a_tmp", "gc")]
            table = self.load_tables("gdn", sb("gdn_tables", [P, self.group_width("gdn")]))
            gain = sb("gdn_gain", [P, P])
            eps = sb("gdn_eps", [P, 1])
            pad = sb("qkv_padded", [P, 3, T + 4])
            z = self.z2
            wide = sb("gc_wide", [P, 2, T])
            zf = sb("z_rows", [P, T])
            taps = sb("qkv_taps", [P, 3, 5])
            acc = sb("qkv", [P, 3, T])
            sqt = sb("qkv_tmp", [P, 3, T])
            zt = sb("z_gate", W4)
            ktok, vtok = sb("k_tok", W4), sb("v_tok", W4)
            osum = sb("o_sum", W4)
            ss = sb("sum_sq", [P, 8])
            hq = sb("head_scalars", [P, 6, NT, 2])
            buf = {n: [sb(f"{n}{d}", W4) for d in range(2)] for n in
                   ("A", "AT", "aT", "M", "MT", "LT", "X", "vb", "kbe", "kdec")}
            S = [sb(f"state{d}", [P, P]) for d in range(2)]
            vn = [sb(f"v_new{d}", [P, P]) for d in range(2)]
            q_now, z_now, z_tmp = sb("q_now", [P, T]), sb("z_gate_now", W4), sb("z_gate_tmp", W4)
            flat = lambda x: x[:, :, :].rearrange("p t n -> p (t n)")
            ch = [slice(t * P, (t + 1) * P) for t in range(NT)]
            wide3 = lambda name: self.k(name).unsqueeze(1).to_broadcast(W4)
            lev = lambda name, s: self.k(name)[:, s * P:(s + 1) * P].unsqueeze(1).to_broadcast(W4)

            def prepare(h, acc_free, wide_free, bank_free):
                lw = [c.dma((pad[:, i, 2:2 + T], z[bass.ds(h * P + C2["a_qkv"] + 512 * i, P), :])) for i in range(3)]
                lt = c.dma(*[(taps[:, i, :], A["gdn_conv_w_2"][l, :, bass.ds(h * P + 512 * i, P)].rearrange("w p -> p w"))
                             for i in range(3)], slow=True)
                lz = c.dma((zf[:, :], z[bass.ds(h * P + C2["a_z"], P), :]))
                if wide_free is not None:
                    c.dma(*[(wide[:, d, :], self.row(h + d * H)) for d in range(2)], after=wide_free)
                yield
                free, silus = list(bank_free), []
                for i in range(3):
                    m = c.dve(nc.vector.tensor_scalar, acc[:, i, :], pad[:, i, 0:T], taps[:, i, 0:1], None, ALU.mult,
                              after=[lw[i], lt, acc_free])
                    yield
                    for w in range(1, 5):
                        m = c.dve(nc.vector.scalar_tensor_tensor, acc[:, i, :], pad[:, i, w:w + T], taps[:, i, w:w + 1],
                                  acc[:, i, :], ALU.mult, ALU.add, after=[m])
                        yield
                    m = c.act(nc.scalar.activation, sqt[:, i, :], acc[:, i, :], ACT.Tanh, scale=0.5, after=[m])
                    yield
                    m = c.dve(nc.vector.scalar_tensor_tensor, acc[:, i, :], sqt[:, i, :], 1.0, acc[:, i, :], ALU.add, ALU.mult, after=[m])
                    yield
                    m = c.dve(nc.vector.tensor_scalar, acc[:, i, :], acc[:, i, :], 0.5, None, ALU.mult, after=[m])
                    yield
                    silus.append(m)
                m = c.transposes([(self.bank[0][:, ch[t]], zf[:, ch[t]]) for t in range(NT)], self.k("ident"), [lz, free])
                yield
                gate = self.silu(flat(zt), self.bank[0][:, :], flat(z_tmp), [m, acc_free])
                yield
                c.pool(nc.gpsimd.tensor_tensor, zt[:, :, :], zt[:, :, :], gain[:, :].unsqueeze(1).to_broadcast(W4),
                       ALU.mult, after=[gate])
                yield
                for i in range(2):
                    m = c.act(nc.scalar.activation, sqt[:, i, :], acc[:, i, :], ACT.Square, after=[silus[i]])
                    m = c.products(self.bank[i][:, :], [(self.k("ones"), sqt[:, i, :])], [m, free, gate])
                    yield
                    m = c.act(nc.scalar.activation, sqt[:, i, :], self.bank[i][:, :], ACT.Ln, bias=eps[:, 0:1], after=[m])
                    free = [*free, m]
                    m = c.act(nc.scalar.activation, sqt[:, i, :], sqt[:, i, :], ACT.Exp, scale=-0.5, after=[m])
                    yield
                    c.dve(nc.vector.scalar_tensor_tensor, acc[:, i, :], acc[:, i, :],
                          P ** -0.5 if i == 0 else 1.0, sqt[:, i, :], ALU.mult, ALU.mult, after=[m])
                    yield

            def head(h, ahead):
                side = None

                def turn(n=1):
                    for _ in range(n if side is not None else 0):
                        next(side, None)
                mh = c.dve(nc.vector.tensor_copy, hq[:, :, :, :].rearrange("p i t d -> p (i t d)"),
                           q5[:, :, :, :, bass.ds(h, 1)].rearrange("p i t d o -> p (i t d o)"))
                qn = c.dve(nc.vector.tensor_copy, q_now[:, :], acc[:, 0, :])
                mz = c.pool(nc.gpsimd.tensor_copy, z_now[:, :, :], zt[:, :, :])
                qT, kT, vT = q_now[:, :], acc[:, 1, :], acc[:, 2, :]
                tok = []
                for bb, dst, src in ((self.bank[6], ktok, kT), (self.bank[7], vtok, vT)):
                    m = c.transposes([(bb[:, ch[t]], src[:, ch[t]]) for t in range(NT)], self.k("ident"))
                    tok.append(c.act(nc.scalar.copy, flat(dst), bb[:, :], after=[m]))
                for t in range(NT):
                    mkk = c.products(self.bank[0][:, ch[t]], [(kT[:, ch[t]], kT[:, ch[t]])])
                for t in range(NT):
                    mkq = c.products(self.bank[1][:, ch[t]], [(kT[:, ch[t]], qT[:, ch[t]])], [qn])
                mAT, mM, mMT, maT, mA, used = [None] * 2, [None] * 2, [None] * 2, [None] * 2, [None] * 2, [None] * 2
                mvb = [None] * 2
                for d in range(2):
                    A_, AT, aT = buf["A"][d], buf["AT"][d], buf["aT"][d]
                    for t in range(NT):
                        gc = hq[:, 5, t, d:d + 1]
                        row = wide[:, d, ch[t]]
                        m1 = c.dve(nc.vector.tensor_scalar, A_[:, t, :], row, gc, 0.0, ALU.subtract, ALU.max, after=[mh])
                        m2 = c.dve(nc.vector.tensor_scalar, aT[:, t, :], row, gc, 0.0, ALU.subtract, ALU.min, after=[mh])
                    m1 = c.act(nc.scalar.activation, flat(A_), flat(A_), ACT.Exp, scale=-1.0, after=[m1])
                    m2 = c.act(nc.scalar.activation, flat(aT), flat(aT), ACT.Exp, after=[m2])
                    m1 = c.dve(nc.vector.tensor_tensor, A_[:, :, :], A_[:, :, :], wide3("sup" if d else "slow"), ALU.mult, after=[m1])
                    m2 = c.pool(nc.gpsimd.tensor_tensor, aT[:, :, :], aT[:, :, :], wide3("low" if d else "up"), ALU.mult, after=[m2])
                    maT[d] = c.dve(nc.vector.tensor_tensor, flat(aT), flat(aT), self.bank[1][:, :], ALU.mult, after=[m2, mkq])
                    for t in range(NT):
                        mA[d] = c.dve(nc.vector.scalar_tensor_tensor, A_[:, t, :], self.bank[0][:, ch[t]], hq[:, 0, t, d:d + 1],
                                      A_[:, t, :], ALU.mult, ALU.mult, after=[m1, mkk])
                    bb = self.bank[2 + d]
                    m = c.transposes([(bb[:, ch[t]], A_[:, t, :]) for t in range(NT)], self.k("ident"), [mA[d]])
                    mAT[d] = c.act(nc.scalar.copy, flat(AT), bb[:, :], after=[m])
                    for n, src, i in (("vb", vtok, 0), ("kbe", ktok, 1), ("kdec", ktok, 3)):
                        mvb[d] = c.pool(nc.gpsimd.tensor_tensor, buf[n][d][:, :, :], src[:, :, :],
                                        hq[:, i, :, d:d + 1].to_broadcast(W4), ALU.mult, after=[tok, mh])
                if ahead:
                    side = prepare(h + 1, [qn, mz, tok, mkk, mkq], [mA, maT], [mA, maT])
                for d in range(2):
                    A_, AT, M, MT = buf["A"][d], buf["AT"][d], buf["M"][d], buf["MT"][d]
                    lo, up = ("levup", "levlow") if d else ("levlow", "levup")
                    m1 = c.dve(nc.vector.tensor_tensor, M[:, :, :], A_[:, :, :], lev(lo, 0), ALU.mult, after=[mA[d]])
                    m2 = c.dve(nc.vector.tensor_tensor, MT[:, :, :], AT[:, :, :], lev(up, 0), ALU.mult, after=[mAT[d]])
                    mM[d] = c.dve(nc.vector.tensor_tensor, M[:, :, :], wide3("ident"), M[:, :, :], ALU.subtract, after=[m1])
                    mMT[d] = c.dve(nc.vector.tensor_tensor, MT[:, :, :], wide3("ident"), MT[:, :, :], ALU.subtract, after=[m2])
                for s in range(1, LEVELS):
                    for d in range(2):
                        A_, AT, M, MT = buf["A"][d], buf["AT"][d], buf["M"][d], buf["MT"][d]
                        LT, X = buf["LT"][d], buf["X"][d]
                        bx, by, bz = self.bank[2 + 3 * d], self.bank[3 + 3 * d], self.bank[4 + 3 * d]
                        up = "levlow" if d else "levup"
                        ml = c.pool(nc.gpsimd.tensor_tensor, LT[:, :, :], AT[:, :, :], lev(up, s), ALU.mult, after=[mAT[d], used[d]])
                        for t in range(NT):
                            m = c.products(bx[:, ch[t]], [(LT[:, t, :], M[:, t, :])], [ml, mM[d], mMT[d], mAT])
                        used[d] = m
                        mx = c.act(nc.scalar.copy, flat(X), bx[:, :], after=[m])
                        if s < LEVELS - 1:
                            for t in range(NT):
                                m = c.products(by[:, ch[t]], [(MT[:, t, :], X[:, t, :])], [mx])
                            my = m
                        for t in range(NT):
                            m = c.products(bz[:, ch[t]], [(X[:, t, :], MT[:, t, :])], [mx])
                        if s < LEVELS - 1:
                            mM[d] = c.dve(nc.vector.tensor_tensor, flat(M), flat(M), by[:, :], ALU.subtract, after=[my])
                        mMT[d] = c.dve(nc.vector.tensor_tensor, flat(MT), flat(MT), bz[:, :], ALU.subtract, after=[m])
                        turn(2)
                U, WT = buf["A"], buf["LT"]
                mu, mw = [None] * 2, [None] * 2
                for d in range(2):
                    bu, bw = self.bank[2 + 3 * d], self.bank[3 + 3 * d]
                    for t in range(NT):
                        m = c.products(bu[:, ch[t]], [(buf["MT"][d][:, t, :], buf["vb"][d][:, t, :])], [mMT[d], mvb[d]])
                    mu[d] = c.act(nc.scalar.copy, flat(U[d]), bu[:, :], after=[m])
                    for t in range(NT):
                        m = c.products(bw[:, ch[t]], [(buf["kbe"][d][:, t, :], buf["MT"][d][:, t, :])], [mMT[d], mvb[d]])
                    mw[d] = c.dve(nc.vector.tensor_copy, flat(WT[d]), bw[:, :], after=[m])
                    turn(2)
                mS, mo, last = [None] * 2, [None] * NT, [None] * 2
                for n in range(NT):
                    for d in range(2):
                        t = NT - 1 - n if d else n
                        o = osum[:, t, :]
                        b1, b2, b3 = [self.bank[3 * d + j] for j in (2, 3, 4)]
                        if n == 0:
                            V, mv = U[d][:, t, :], mu[d]
                        else:
                            m = c.products(b1[:, 0:P], [(WT[d][:, t, :], S[d][:, :])], [mw, mS[d], mu, last[d]])
                            mv = c.dve(nc.vector.tensor_tensor, vn[d][:, :], U[d][:, t, :], b1[:, 0:P], ALU.subtract, after=[m, mS[d]])
                            V = vn[d][:, :]
                            mq = c.products(b2[:, 0:P], [(qT[:, ch[t]], S[d][:, :])], [mS[d], last[d]])
                        mi = c.products(b3[:, 0:P], [(buf["aT"][d][:, t, :], V)], [mv, maT[d], mw, mu, last[d]])
                        if mo[t] is None:
                            mo[t] = c.dve(nc.vector.tensor_copy, o, b3[:, 0:P], after=[mi, mz])
                        else:
                            mo[t] = c.dve(nc.vector.tensor_tensor, o, o, b3[:, 0:P], ALU.add, after=[mi, mo[t]])
                        if n > 0:
                            mo[t] = c.dve(nc.vector.scalar_tensor_tensor, o, b2[:, 0:P], hq[:, 2, t, d:d + 1], o,
                                          ALU.mult, ALU.add, after=[mq, mo[t]])
                        last[d] = mo[t]
                        if n < NT - 1:
                            ms = c.products(b3[:, P:2 * P], [(buf["kdec"][d][:, t, :], V)], [mo[t]])
                            if n == 0:
                                mS[d] = c.dve(nc.vector.tensor_copy, S[d][:, :], b3[:, P:2 * P], after=[ms])
                            else:
                                mS[d] = c.dve(nc.vector.scalar_tensor_tensor, S[d][:, :], S[d][:, :], hq[:, 4, t, d:d + 1],
                                              b3[:, P:2 * P], ALU.mult, ALU.add, after=[ms])
                            last[d] = mS[d]
                        turn()
                turn(100)
                m = self.norm_blocks(osum, NT, lambda i: z_now[:, i, :], vtok, ss, eps[:, 0:1],
                                     [mo, mz, mvb])
                self.store_T(osum, 1, [self.bank[7]], h, [m])
                c.barrier()

            lg = c.dma((gain[:, :], A["gdn_norm_g_2"][l].partition_broadcast(P)))
            c.dve(nc.vector.memset, eps[:, :], EPS)
            c.dve(nc.vector.memset, pad[:, :, 0:2], 0.0)
            c.dve(nc.vector.memset, pad[:, :, T + 2:], 0.0)
            first = prepare(0, [lg, c.dve.mark()], None, [])
            side = beside([flat(buf[n][d]) for n in ("A", "AT", "M", "MT", "LT", "X", "vb") for d in range(2)])

            def turn():
                next(first, None)
                next(side, None)
            turn()
            mb, mc, mg, stored = [], [], [], []
            c.dve.wait(table)
            for d in range(2):
                hs = slice(d * H, (d + 1) * H)
                at = C2["a_ab"] + d * H
                ld = c.dma((ar[d][:, :], z[at:at + H, :]), (br[d][:, :], z[at + 8:at + 8 + H, :]),
                           (par[d][:, 0:1], A["gdn_a_log_2"][l, d].unsqueeze(1)), (par[d][:, 1:2], A["gdn_dt_bias_2"][l, d].unsqueeze(1)), slow=True)
                turn()
                m = self.sigmoid(br[d][:, :], br[d][:, :], [ld])
                turn()
                mb.append(self.to_cols(q5[:, 0, :, d, :], br[d][:, :], self.bank[5], [m, c.dve.mark()]))
                m = c.dve(nc.vector.tensor_scalar, ar[d][:, :], ar[d][:, :], par[d][:, 1:2], None, ALU.add, after=[ld])
                m = c.act(nc.scalar.activation, tmp[d][:, :], ar[d][:, :], ACT.Abs, after=[m])
                m = c.act(nc.scalar.activation, tmp[d][:, :], tmp[d][:, :], ACT.Exp, scale=-1.0, after=[m])
                m = c.act(nc.scalar.activation, tmp[d][:, :], tmp[d][:, :], ACT.Ln, bias=1.0, after=[m])
                turn()
                ma = c.act(nc.scalar.activation, par[d][:, 0:1], par[d][:, 0:1], ACT.Exp, after=[ld])
                m = c.dve(nc.vector.scalar_tensor_tensor, ar[d][:, :], ar[d][:, :], 0.0, tmp[d][:, :], ALU.max, ALU.add, after=[m])
                m = c.dve(nc.vector.tensor_scalar, ar[d][:, :], ar[d][:, :], par[d][:, 0:1], -1.0, ALU.mult, ALU.mult, after=[m, ma])
                mg.append(self.to_cols(g[:, :, hs], ar[d][:, :], self.bank[6], [m, c.dve.mark()]))
                turn()
                m = self.scan_rows(gcr[d][:, :], ar[d][:, :], self.k("carryb" if d else "carryf", H), ALU.add, d, [m])
                mc.append(self.to_cols(q5[:, 5, :, d, :], gcr[d][:, :], self.bank[7], [m, c.dve.mark()]))
                stored.append(c.dma((self.rows[hs, :], gcr[d][:, :]), after=[m]))
                turn()
            m = c.products(self.bank[2][:, 0:32], [(self.k("ones"), g[:, :, :].rearrange("p t n -> p (t n)"))], mg)
            mt = c.dve(nc.vector.tensor_copy, tot[:, :, :].rearrange("p t n -> p (t n)"), self.bank[2][:, 0:32], after=[m])
            q = [q5[:, i, :, :, :].rearrange("p t d h -> p t (d h)") for i in range(6)]
            c.act(nc.scalar.activation, q[4], tot[:, :, :], ACT.Exp, after=[mt])
            me = c.act(nc.scalar.activation, q[2], q[5], ACT.Exp, after=mc)
            m = c.dve(nc.vector.tensor_tensor, q[3], tot[:, :, :], q[5], ALU.subtract, after=[*mc, mt])
            c.act(nc.scalar.activation, q[3], q[3], ACT.Exp, after=[m])
            c.dve(nc.vector.tensor_tensor, q[1], q[2], q[0], ALU.mult, after=[me, *mb])
            c.dma(*[(wide[:, d, :], self.row(d * H)) for d in range(2)], after=stored)
            for _ in first:
                next(side, None)
            for _ in side:
                pass
            c.barrier()
            with nc.Fori(0, H - 1) as h:
                head(h, True)
            head(H - 1, False)

    def diff(self, l):
        nc, c, A = self.nc, self.c, self.A
        with ExitStack() as es:
            sb = self.allocator(es)
            table = self.load_tables("rope", sb("rope_tables", [P, self.group_width("rope")]))
            lp = sb("lambda_params", [P, 4, HD])
            lam = sb("lambda", [P, 4])
            gain = sb("diff_gain", [P, P])
            eps = sb("diff_eps", [P, 1])
            ld = c.dma((lp[:, :, :].rearrange("p a d -> p (a d)"), A["diff_lambda_2"][l].rearrange("a d -> (a d)").partition_broadcast(P)),
                       (gain[:, :], A["diff_norm_g_2"][l].partition_broadcast(P)), slow=True)
            c.dve(nc.vector.memset, eps[:, :], EPS)
            for i in range(2):
                m = c.dve(nc.vector.tensor_tensor, lp[:, 2 * i, :], lp[:, 2 * i, :], lp[:, 2 * i + 1, :], ALU.mult, after=[ld])
                m = c.dve(nc.vector.tensor_reduce, lam[:, i:i + 1], lp[:, 2 * i, :], AX.X, ALU.add, after=[m])
            m = c.act(nc.scalar.activation, lam[:, 0:2], lam[:, 0:2], ACT.Exp, after=[m])
            m = c.dve(nc.vector.tensor_tensor, lam[:, 2:3], lam[:, 0:1], lam[:, 1:2], ALU.subtract, after=[m])
            m = c.dve(nc.vector.tensor_tensor, lam[:, 2:3], lam[:, 2:3], self.k("lam")[:, bass.ds(l, 1)], ALU.add, after=[m, table])
            m = c.dve(nc.vector.tensor_copy, lam[:, 3:4], self.k("lam")[:, bass.ds(l + DEPTH, 1)])
            c.dve(nc.vector.tensor_scalar, gain[:, :], gain[:, :], lam[:, 3:4], None, ALU.mult, after=[m, ld])
            c.barrier()
            q2, k2 = [[sb(f"{n}_twice{i}", [P, T]) for i in range(4)] for n in "qk"]
            qs, kh = [[sb(f"{n}{i}", [P, T], F32R) for i in range(4)] for n in ("q_stacked", "k_hi")]
            vf, rt = [sb(f"v_rows{j}", [P, T]) for j in range(2)], [sb(f"rope_tmp{i}", [P, T]) for i in range(4)]
            v, y = [sb(f"v_tok{j}", [P, NT, P]) for j in range(2)], sb("y_tok", [P, NT * 2, P])
            sq = sb("y_squared", [P, NT * 2, P])
            ss = sb("sum_sq", [P, 8])
            self.attention_buffers(es, 2)
            with nc.Fori(0, 2) as pair:
                lk, lq = [[c.dma(*self.twice(x[i], self.z2[bass.ds(pair * 2 * P + C2[n] + i * HD, HD), :])) for i in range(4)]
                          for x, n in ((k2, "b_k"), (q2, "b_q"))]
                lv = [c.dma((vf[j][:, :], self.z2[bass.ds(pair * 2 * P + C2["b_v"] + j * P, P), :])) for j in range(2)]
                rot = (self.k("rot2"), self.k("cos2"), self.k("sin2"))
                ready, free = [], [None] * 4
                for i in range(4):
                    for n, x in enumerate((k2[i], q2[i])):
                        b = 2 * (i % 2) + n
                        free[b] = self.rope(x[:, :], rt[b][:, :], self.bank[b], *rot, [(lk, lq)[n][i], free[b]])
                        if n == 0:
                            ready.append(self.split(kh[i][:, :], self.low(x)[:, :], x[:, :], [free[b]]))
                        else:
                            ready.append(self.stack(x, qs[i], HD ** -0.5, [free[b]]))
                mv = [self.to_tokens(v[j][:, :, :], vf[j], self.bank[6 + j], [lv[j]]) for j in range(2)]

                def mix(p0, p1, rinv, marks):
                    m = c.dve(nc.vector.tensor_tensor, rinv[1], rinv[1], lam[:, 2:3], ALU.mult, after=marks)
                    m = c.dve(nc.vector.tensor_scalar, p1, p1, rinv[1], None, ALU.mult, after=[m])
                    return c.dve(nc.vector.scalar_tensor_tensor, p0, p0, rinv[0], p1, ALU.mult, ALU.subtract, after=[m])
                units = []
                for j in range(2):
                    for t in range(NT):
                        def out(o, rinv, marks, at=2 * t + j):
                            return c.dve(nc.vector.tensor_copy, y[:, at, :], o, after=marks)
                        units.append(dict(maps=[(qs[i][:, t * P:(t + 1) * P], (kh[i][:, :], self.low(k2[i])[:, :])) for i in (2 * j, 2 * j + 1)],
                                          width=T, extra=[], decay=None, sink=None, coef=None, mix=mix,
                                          values=[v[j][:, i, :] for i in range(NT)], out=out))
                self.attention(units, [ready, mv])
                m = self.norm_blocks(y, NT * 2, lambda i: gain[:, :], sq, ss, eps[:, 0:1], [c.dve.mark()])
                self.store_T(y[:, :, :].rearrange("p (t j) d -> p t (j d)", j=2), 2, [self.bank[6], self.bank[7]], pair * 2 + 4, [m])
                c.barrier()

    def swa(self, l):
        nc, c, A = self.nc, self.c, self.A
        with ExitStack() as es:
            sb = self.allocator(es)
            self.load_tables("rope", sb("rope_tables", [P, self.group_width("rope")]))
            sinks = sb("sinks", [P, 8])
            q2, qs = [sb(f"q_twice{h}", [P, T]) for h in range(4)], [sb(f"q_stacked{h}", [P, T], F32R) for h in range(4)]
            k2, kh = sb("k_twice", [P, T]), sb("k_hi", [P, T], F32R)
            vf, rt = sb("v_rows", [HD, T]), [sb(f"rope_tmp{i}", [P, T]) for i in range(2)]
            v, y = sb("v_tok", [P, NT, HD]), sb("y_tok", [P, NT, 2 * P])
            sk, nsk = sb("group_sinks", [P, 4]), sb("group_sinks_neg", [P, 4])
            self.attention_buffers(es, 1)
            c.dma((sinks[:, :], A["swa_sink_2"][l].partition_broadcast(P)), slow=True)
            c.barrier()
            with nc.Fori(0, 2) as grp:
                z = self.z2
                lk = c.dma(*self.twice(k2, z[bass.ds(grp * HD + C2["c_k"], HD), :]))
                lq = [c.dma(*self.twice(q2[h], z[bass.ds(grp * 256 + C2["c_q"] + h * HD, HD), :])) for h in range(4)]
                lv = c.dma((vf[:, :], z[bass.ds(grp * HD + C2["c_v"], HD), :]))
                m = c.dve(nc.vector.tensor_copy, sk[:, :], sinks[:, bass.ds(grp * 4, 4)])
                ms = c.dve(nc.vector.tensor_scalar, nsk[:, :], sk[:, :], -1.0, None, ALU.mult, after=[m])
                rot = (self.k("rot2"), self.k("cos2"), self.k("sin2"))
                tmp_free = [None, None]
                m = self.rope(k2[:, :], rt[0][:, :], self.bank[0], *rot, [lk])
                tmp_free[0] = m
                ready = [ms, self.split(kh[:, :], self.low(k2)[:, :], k2[:, :], [m])]
                for h in range(4):
                    n = (h + 1) % 2
                    m = self.rope(q2[h][:, :], rt[n][:, :], self.bank[n], *rot, [lq[h], tmp_free[n]])
                    tmp_free[n] = m
                    ready.append(self.stack(q2[h], qs[h], HD ** -0.5, [m]))
                mv = self.to_tokens(v[:, :, :], vf, self.bank[6], [lv], HD)
                units = []
                for h in range(4):
                    for t in range(NT):
                        lo, hi = max(t - 1, 0), min(t + 2, NT)
                        extra = [(self.r("ident"), self.r("far"), 0, P)] if t > 0 else []
                        extra += [(self.r("ident"), self.r("later"), (hi - lo - 1) * P, P)] if t < NT - 1 else []

                        def out(o, rinv, marks, h=h, t=t):
                            return c.dve(nc.vector.tensor_scalar, y[:, t, h * HD:(h + 1) * HD], o, rinv, None, ALU.mult, after=marks)
                        units.append(dict(maps=[(qs[h][:, t * P:(t + 1) * P], (kh[:, lo * P:hi * P], self.low(k2)[:, lo * P:hi * P]))], width=(hi - lo) * P,
                                          extra=extra, decay=None, sink=(sk[:, h:h + 1], nsk[:, h:h + 1]), coef=None, mix=None,
                                          values=[v[:, i, :] for i in range(lo, hi)], out=out))
                self.attention(units, [ready, mv])
                self.store_T(y, 2, [self.bank[6], self.bank[7]], grp * 2 + 8, [c.dve.mark()])
                c.barrier()

    def mlstm_gates(self, l, cols, scratch):
        nc, c, A = self.nc, self.c, self.A
        z = self.z2
        bias = [s[0:4, 0:2] for s in scratch[12:14]]
        ir, fr, tmp, Br, rr, Rr = [[scratch[2 * n + d][0:4, 0:T] for d in range(2)] for n in range(6)]
        ld = []
        for d in range(2):
            at = C2["d_if"] + 4 * d
            ld.append(c.dma((ir[d], z[at:at + 4, :]), (fr[d], z[at + 8:at + 12, :]),
                            (bias[d][:, 0:1], A["mlstm_gate_b_2"][l, 0, d].unsqueeze(1)),
                            (bias[d][:, 1:2], A["mlstm_gate_b_2"][l, 1, d].unsqueeze(1)), slow=True))
        yield
        m1, m2 = [None] * 2, [None] * 2
        for d in range(2):
            m1[d] = c.dve(nc.vector.tensor_scalar, ir[d], ir[d], bias[d][:, 0:1], None, ALU.add, after=[ld[d]])
            m2[d] = c.dve(nc.vector.tensor_scalar, fr[d], fr[d], bias[d][:, 1:2], None, ALU.add, after=[ld[d]])
            yield
            m2[d] = self.log_sigmoid(fr[d], tmp[d], [m2[d]])
            yield
        for d in range(2):
            m2[d] = self.scan_rows(Br[d], fr[d], self.k("onesrow", 4), ALU.add, d, [m2[d]])
            yield
            m1[d] = c.dve(nc.vector.tensor_tensor, rr[d], ir[d], Br[d], ALU.subtract, after=[m1[d], m2[d]])
            yield
        for d in range(2):
            hs = slice(4 * d, 4 * d + 4)
            mR = self.scan_rows(Rr[d], rr[d], self.k("onesrow", 4), ALU.max, d, [m1[d]])
            c.dma((self.rows_R[hs, :], Rr[d]), after=[mR])
            yield
            m2[d] = c.dve(nc.vector.tensor_tensor, Br[d], Br[d], Rr[d], ALU.add, after=[mR])
            self.to_cols(cols[:, 0, :, hs], rr[d], self.bank[3], [m1[d], c.dve.mark()])
            yield
            m2[d] = self.to_cols(cols[:, 1, :, hs], Br[d], self.bank[4], [m2[d], c.dve.mark()])
            yield
        c.act(nc.scalar.activation, cols[:, 1, :, :], cols[:, 1, :, :], ACT.Exp, scale=-1.0, after=m2)

    def mlstm(self, l, cols):
        nc, c, A = self.nc, self.c, self.A
        with ExitStack() as es:
            sb = self.allocator(es)
            gain = sb("mlstm_gain", [P, P])
            eps = sb("mlstm_eps", [P, 1])
            z = self.z2
            c.dma((gain[:, :], A["mlstm_norm_g_2"][l].partition_broadcast(P)))
            c.dve(nc.vector.memset, eps[:, :], EPS)
            c.barrier()
            q2, k2 = [[sb(f"{n}_twice{i}", [P, T]) for i in range(2)] for n in "qk"]
            qh, ks = [[sb(f"{n}{i}", [P, T], F32R) for i in range(2)] for n in ("q_hi", "k_stacked")]
            vf, of = [[sb(f"{n}_rows{i}", [P, T]) for i in range(2)] for n in ("v", "o")]
            V = P + 1
            va = sb("v_and_one", [P, NT, 2, V])
            og, y = sb("o_gate", [P, NT, 2, P]), sb("y_tok", [P, NT, 2, P])
            pc = sb("pair_cols", [P, 2, NT, 2, 2])
            pR = sb("pair_R", [P, 2, 2, T])
            WT = [[sb(f"weights{i}_{d}", [P, NT, T]) for d in range(2)] for i in range(2)]
            den = sb("den", [P, 2, 2, NT])
            ss = sb("sum_sq", [P, 8])
            with nc.Fori(0, 2) as pair:
                lq, lk = [[c.dma(*self.twice(x[h], z[bass.ds(pair * P + C2[n] + h * HD, HD), :])) for h in range(2)]
                          for x, n in ((q2, "d_q"), (k2, "d_k"))]
                lv, lo = [[c.dma((x[h][:, :], z[bass.ds(pair * 256 + C2[n] + h * P, P), :])) for h in range(2)]
                          for x, n in ((vf, "d_v"), (of, "d_o"))]
                mc = []
                for i in range(2):
                    for d in range(2):
                        mc.append(c.dve(nc.vector.tensor_copy, pc[:, i, :, d, :], cols[:, i, :, bass.ds(pair * 2 + 4 * d, 2)]))
                mc.append(c.dma(*[(pR[:, d, h, :], self.row(pair * 2 + 4 * d + h, self.rows_R)) for d in range(2) for h in range(2)]))
                m1 = c.dve(nc.vector.memset, va[:, :, :, P:V], 1.0)
                mv, mq = [m1], []
                for h in range(2):
                    mq.append(self.split(qh[h][:, :], self.low(q2[h])[:, :], q2[h][:, :], [lq[h]]))
                    mq.append(self.stack(k2[h], ks[h], HD ** -0.5, [lk[h]]))
                    mv.append(self.to_tokens(va[:, :, h, 0:P], vf[h], self.bank[2 + h], [lv[h]]))
                    m = self.sigmoid(of[h][:, :], of[h][:, :], [lo[h]])
                    mo = self.to_tokens(og[:, :, h, :], of[h], self.bank[4 + h], [m])
                upto = lambda j, d: slice(0, (j + 1) * P) if d else slice(j * P, T)
                made = {}
                todo = [(h, j, d) for h in range(2) for j in range(NT) for d in range(2)]
                for h, j, d in todo:
                    w = WT[h][d][:, j, upto(j, d)]
                    made[h, j, d] = c.dve(nc.vector.tensor_scalar, w, pR[:, d, h, upto(j, d)], pc[:, 0, j, d, h:h + 1], 0.0,
                                          ALU.subtract, ALU.max, after=[mc])
                for h, j, d in todo:
                    w, diag = WT[h][d][:, j, upto(j, d)], WT[h][d][:, j, j * P:(j + 1) * P]
                    a = c.act(nc.scalar.activation, w, w, ACT.Exp, scale=-1.0, after=[made[h, j, d]])
                    made[h, j, d] = c.pool(nc.gpsimd.tensor_tensor, diag, diag, self.k("low" if d else "up"), ALU.mult, after=[a])
                mo = c.pool(nc.gpsimd.tensor_tensor, og[:, :, :, :].rearrange("p t h n -> p (t h) n"),
                            og[:, :, :, :].rearrange("p t h n -> p (t h) n"),
                            gain[:, :].unsqueeze(1).to_broadcast([P, 2 * NT, P]), ALU.mult, after=[mo])
                my = None
                free = [[mv, mo]] * 4
                fs = [[], []]
                for h in range(2):
                    mw = [[None] * NT for _ in range(2)]
                    for j in range(NT):
                        bs = self.bank[j % 2]
                        kk = ks[h][:, j * P:(j + 1) * P]
                        m = c.products(bs[:, :], [(kk, qh[h][:, :]), (kk, self.low(q2[h])[:, :])], [mq, fs[j % 2]])
                        for d in range(2):
                            w = WT[h][d][:, j, upto(j, d)]
                            mw[d][j] = c.dve(nc.vector.tensor_tensor, w, w, bs[:, upto(j, d)], ALU.mult, after=[made[h, j, d], m])
                        fs[j % 2] = [mw[0][j], mw[1][j]]
                    for d in range(2):
                        mo2 = []
                        for t in range(NT):
                            bo = self.bank[2 + 2 * d + t // 2]
                            js = range(t, NT) if d else range(0, t + 1)
                            m = c.products(bo[:, (t % 2) * V:(t % 2) * V + V],
                                           [(WT[h][d][:, j, t * P:(t + 1) * P], va[:, j, h, :]) for j in js],
                                           [mw[d], mv, free[2 * d + t // 2], free[2 * d + t // 2]])
                            mo2.append(m)
                        dn = den[:, d, h, :]
                        for i in range(2):
                            bo = self.bank[2 + 2 * d + i]
                            mm = c.act(nc.scalar.activation, dn[:, 2 * i:2 * i + 2],
                                       bo[:, 0:2 * V].rearrange("p (t v) -> p t v", v=V)[:, :, P], ACT.Abs, after=[m])
                        mm = c.dve(nc.vector.tensor_tensor, dn, dn, pc[:, 1, :, d, h], ALU.max, after=[mm, mc])
                        mm = c.dve(nc.vector.reciprocal, dn, dn, after=[mm])
                        for t in range(NT):
                            bo = self.bank[2 + 2 * d + t // 2]
                            num = bo[:, (t % 2) * V:(t % 2) * V + P]
                            if d == 0:
                                my = c.dve(nc.vector.tensor_scalar, y[:, t, h, :], num, dn[:, t:t + 1], None, ALU.mult, after=[mm])
                            else:
                                my = c.dve(nc.vector.scalar_tensor_tensor, y[:, t, h, :], num, dn[:, t:t + 1], y[:, t, h, :],
                                           ALU.mult, ALU.add, after=[mm, my])
                            free[2 * d + t // 2] = my
                fold = lambda x: x[:, :, :, :].rearrange("p t h n -> p (t h) n")
                m = self.norm_blocks(fold(y), 2 * NT, lambda i: fold(og)[:, i, :], pR[:, :, :, :].rearrange("p d h (a n) -> p (d h a) n", n=P),
                                     ss, eps[:, 0:1], [my, mo])
                self.store_T(y[:, :, :, :].rearrange("p t h n -> p t (h n)"), 2, [self.bank[6], self.bank[7]], pair * 2 + 12, [m])
                c.barrier()

    def gate_branches(self, l, mT):
        nc, c, A = self.nc, self.c, self.A
        B = 4
        KB = 4
        with ExitStack() as es:
            sb = self.allocator(es)
            yh, yl = sb("y_hi", [P, 16, T], F32R), self.low(self.yT)
            sg = [sb(f"gate{s}", [P, T]) for s in range(B)]

            def load(e, s, out, width):
                return [(out[:, 0:KD, :], A["w_gate_2"][l, :, s, bass.ds(e * P, P)].rearrange("(k p) n -> p k n", p=P)),
                        (out[:, KD:, :], A["w_branch_2"][l, s, :, bass.ds(e * P, P)].rearrange("(k p) n -> p k n", p=P))]

            def products(s, wh, wl, width):
                self.three_passes(self.bank[s], P, [(wh[:, k, :], wl[:, k, :], self.hH[:, k, :], self.hL[:, k, :]) for k in range(KD)])
                return self.three_passes(self.bank[4 + s], P, [
                    (wh[:, KD + k, :], wl[:, KD + k, :], yh[:, KB * s + k, :], yl[:, KB * s + k, :]) for k in range(KB)])

            def drain(e, s, tile, width):
                nc.scalar.wait_ge(c.mm[s], e + 2)
                nc.scalar.wait_ge(c.ev[s], e + 1)
                nc.scalar.activation(sg[s][:, :], self.bank[s][:, :], ACT.Tanh, scale=0.5).then_inc(c.mid[s], 1)
                nc.vector.wait_ge(c.mid[s], e + 1)
                nc.vector.scalar_tensor_tensor(sg[s][:, :], sg[s][:, :], 1.0, self.bank[4 + s][:, :], ALU.add, ALU.mult)\
                    .then_inc(c.fin[s], 1)
                nc.vector.wait_ge(c.fin[s], e + 1)
                acc = mT[:, bass.ds(e, 1), :].rearrange("p a t -> p (a t)")
                if s == 0:
                    m = nc.vector.tensor_scalar(acc, sg[s][:, :], 0.5, None, ALU.mult)
                else:
                    nc.vector.wait_ge(c.ev[s - 1], e + 2)
                    m = nc.vector.scalar_tensor_tensor(acc, sg[s][:, :], 0.5, acc, ALU.mult, ALU.add)
                m.then_inc(c.ev[s], 1)

            self.stream(sb, KD, B, 2, KD + KB, load, products, drain,
                        prepare=self.split_pieces(yh, yl, self.yT, 16, 10))
            c.barrier()

    def mlp(self, l):
        nc, c, A = self.nc, self.c, self.A
        F = 4 * KD // 2
        S = 4
        with nc.Fori(0, 2) as half, ExitStack() as es:
            sb = self.allocator(es)
            uh, ul = sb("hidden_hi", [P, F, T], F32R), sb("hidden_lo", [P, F, T], F32R)
            with ExitStack() as ws:
                sw = self.allocator(ws)
                relu = [sw(f"relu{s}", [P, T]) for s in range(S)]

                def load(i, s, out, width):
                    return [(out[:, :, :], cols_of(A["w_mlp1_2"], l, half * (F * P) + i * (S * P) + s * P, P))]

                def products(s, wh, wl, width):
                    return self.three_passes(self.bank[s], P, [
                        (wh[:, k, :], wl[:, k, :], self.hH[:, k, :], self.hL[:, k, :]) for k in range(KD)])

                def drain(i, s, tile, width):
                    hi = uh[:, bass.ds(tile, 1), :].rearrange("p a t -> p (a t)")
                    lo = ul[:, bass.ds(tile, 1), :].rearrange("p a t -> p (a t)")
                    nc.vector.wait_ge(c.mm[s], i + 2)
                    nc.vector.wait_ge(c.fin[s], i + 1)
                    nc.vector.tensor_scalar(relu[s][:, :], self.bank[s][:, :], 0.0, None, ALU.max).then_inc(c.mid[s], 1)
                    nc.scalar.wait_ge(c.mid[s], i + 1)
                    nc.scalar.activation(relu[s][:, :], relu[s][:, :], ACT.Square).then_inc(c.ev[s], 1)
                    nc.scalar.wait_ge(c.ev[s], i + 2)
                    nc.scalar.copy(hi, relu[s][:, :]).then_inc(c.st[s], 1)
                    nc.gpsimd.wait_ge(c.st[s], i + 1)
                    nc.gpsimd.tensor_tensor(lo, relu[s][:, :], hi.bitcast(F32), ALU.subtract).then_inc(c.fin[s], 1)
                for s in range(S):
                    nc.gpsimd.sem_inc(c.fin[s], 1)
                self.stream(sw, F // S, S, 1, KD, load, products, drain)
                c.barrier()
            self.stream_add(lambda e: A["w_mlp2_2"][l, bass.ds(half * (F * P), F * P), bass.ds(e * P, P)].rearrange("(k p) n -> p k n", p=P),
                            uh, ul, F, 2)

    def second_block(self):
        nc, A = self.nc, self.A
        with nc.Fori(0, DEPTH) as l:
            self.in_projection(l, A["norm1_g_2"][l], A["w_in_2"], C2_WIDTH, self.z2)
            with ExitStack() as es:
                cols = self.allocator(es)("r_and_exp_m", [P, 2, NT, 8])
                self.gdn(l, lambda buffers: self.mlstm_gates(l, cols, buffers))
                self.diff(l)
                self.swa(l)
                self.mlstm(l, cols)
            with ExitStack() as es:
                sb = self.allocator(es)
                mT = sb("mixed", [P, KD, T])
                self.gate_branches(l, mT)
                mh, ml = sb("mixed_hi", [P, KD, T], F32R), self.low(mT)[:, :, :]
                self.stream_add(lambda e: cols_of(A["w_out_2"], l, e * P, P), mh, ml, KD, 4,
                                self.split_pieces(mh, ml, mT, KD, 5))
            self.norm(None, A["norm2_g_2"][l])
            self.mlp(l)
        self.norm(self.xT, A["final_norm_g_2"])


def build(nc, A, table, out):
    cols, _ = constants()
    p = Program(nc, A, out, table, cols)
    p.load_x(A["x"][0])
    p.first_block()
    p.second_block()
    p.store(out[0], p.xT)


NAMES = ["x", "norm_g", "w_in", "fox_b", "conv_w", "conv_b", "conv_ln_g", "conv_ln_b", "conv_pw", "cmp_pe_k",
         "cmp_pe_v", "cmp_k_w1", "cmp_k_w2", "cmp_v_w1", "cmp_v_w2", "w_out", "final_g", "norm1_g_2", "w_in_2",
         "gdn_conv_w_2", "gdn_a_log_2", "gdn_dt_bias_2", "gdn_norm_g_2", "diff_lambda_2", "diff_norm_g_2",
         "swa_sink_2", "mlstm_gate_b_2", "mlstm_norm_g_2", "w_branch_2", "w_gate_2", "w_out_2", "norm2_g_2",
         "w_mlp1_2", "w_mlp2_2", "final_norm_g_2"]


def kernel(**inputs):
    import concourse.bacc as bacc
    from concourse.bass_utils import run_bass_kernel_spmd

    nc = bacc.Bacc("TRN2", target_bir_lowering=False, num_devices=1)
    arrays, A = {}, {}
    for name in NAMES:
        arrays["in_" + name] = np.ascontiguousarray(inputs[name])
        A[name] = nc.dram_tensor("in_" + name, arrays["in_" + name].shape, F32, kind="ExternalInput").ap()
    arrays["table"] = constants()[1]
    table = nc.dram_tensor("table", arrays["table"].shape, F32, kind="ExternalInput").ap()
    out = nc.dram_tensor("out", (1, T, D), F32, kind="ExternalOutput").ap()
    build(nc, A, table, out)
    r = run_bass_kernel_spmd(nc, [arrays], core_ids=[0])
    return r.results[0]["out"]
```
